# Optimizing a Trainium2 kernel written in Bass

```python
import jax, jax.numpy as jnp
from jax import lax
import numpy as np

D_MODEL = 1024
BATCH = 1
SEQ = 512
DEPTH = 1
DEC_BATCH = 8
DEC_SEQ = 1
PAST_LEN = 4096
PAGE_SIZE = 128

HG_HEADS = 8
HG_DK = 128
HG_DV = D_MODEL // HG_HEADS
HG_KW = HG_HEADS * HG_DK
HG_VW = HG_HEADS * HG_DV
HG_CHUNK = 16
LRU_W = D_MODEL
LRU_BLOCKS = 8
LRU_BW = LRU_W // LRU_BLOCKS
CONV_W = 4
LRU_C = 8.0
D_FF = ((-(-8 * D_MODEL // 3) + 255) // 256) * 256
EPS = 1e-6
_SIZES = (HG_KW, HG_KW, HG_VW, HG_VW, LRU_W, LRU_W, D_MODEL, D_MODEL)
N_IN = sum(_SIZES)

kernel_name = "hgrn2_rglru_gated_parallel_decoder_step"

def _rmsnorm(x, g):
    xf = x.astype(jnp.float32)
    y = xf * lax.rsqrt(jnp.mean(xf * xf, axis=-1, keepdims=True) + EPS) * g.astype(jnp.float32)
    return y.astype(x.dtype)

def _gla_chunk_step(S, xs):
    qc, kc, vc, bc = xs
    C = qc.shape[1]
    causal = jnp.tril(jnp.ones((C, C), bool))[None, :, :, None, None]
    diff = bc[:, :, None] - bc[:, None, :]
    decay = jnp.exp(jnp.where(causal, diff, -jnp.inf))
    scores = jnp.einsum('bthk,bshk,btshk->btsh', qc, kc, decay)
    o = (jnp.einsum('bthk,bhkv->bthv', qc * jnp.exp(bc), S)
         + jnp.einsum('btsh,bshv->bthv', scores, vc))
    b_last = bc[:, -1]
    S_new = (jnp.exp(b_last)[..., None] * S
             + jnp.einsum('bshk,bshv->bhkv', kc * jnp.exp(b_last[:, None] - bc), vc))
    return S_new, o

def _hgrn2(q, k, v, logf, S0, chunk):
    B, T, H, K = q.shape
    V = v.shape[-1]
    n = T // chunk

    def blocks(a):
        return jnp.moveaxis(a.reshape(B, n, chunk, H, a.shape[-1]), 1, 0)

    bc = jnp.cumsum(blocks(logf), axis=2)
    S_last, o = lax.scan(_gla_chunk_step, S0, (blocks(q), blocks(k), blocks(v), bc))
    return jnp.moveaxis(o, 0, 1).reshape(B, T, H, V), S_last

def _causal_conv(x, buf, w, b):
    T = x.shape[1]
    xp = jnp.concatenate([buf.astype(x.dtype), x], axis=1)
    y = b
    for j in range(CONV_W):
        y = y + xp[:, j:j + T] * w[j]
    return y, xp[:, -(CONV_W - 1):]

def _lru_combine(l, r):
    return (l[0] * r[0], r[0] * l[1] + r[1])

def _rglru(xc, ra, ix, log_lambda, h0, fresh):
    log_a = -LRU_C * jax.nn.sigmoid(ra) * jax.nn.softplus(-log_lambda)
    a = jnp.exp(log_a)
    mult = jnp.sqrt(-jnp.expm1(2.0 * log_a))
    if fresh:
        mult = mult.at[:, 0].set(1.0)
    b = mult * (jax.nn.sigmoid(ix) * xc)
    b = b.at[:, 0].add(a[:, 0] * h0)
    _, h = lax.associative_scan(_lru_combine, (a, b), axis=1)
    return h, h[:, -1]

def _layer(x, S0, h0, cbuf, fresh, chunk, lb,
           n_mix_pre, n_mix_post, n_ffn_pre, n_ffn_post, w_in, hg_onorm,
           conv_w, conv_b, wa, ba, wx, bx, log_lambda, w_pa, w_pb, w_o, w_fi, w_fo):
    B, T, _ = x.shape
    f32 = jnp.float32
    xn = _rmsnorm(x, n_mix_pre)
    proj = xn @ w_in
    idx = [int(s) for s in np.cumsum(_SIZES)[:-1]]
    q, fp, iv, og, lx, ly, ga, gb = jnp.split(proj, idx, axis=-1)

    lbh = lb.reshape(HG_HEADS, HG_DK)
    f = lbh + (1.0 - lbh) * jax.nn.sigmoid(fp.astype(f32).reshape(B, T, HG_HEADS, HG_DK))
    logf = jnp.log(f)
    kk = 1.0 - f
    qh = jax.nn.silu(q.astype(f32)).reshape(B, T, HG_HEADS, HG_DK)
    vh = iv.astype(f32).reshape(B, T, HG_HEADS, HG_DV)
    o, S_new = _hgrn2(qh, kk, vh, logf, S0.astype(f32), chunk)
    o = o * lax.rsqrt(jnp.mean(o * o, axis=-1, keepdims=True) + EPS) * hg_onorm.astype(f32)
    o = o * jax.nn.silu(og.astype(f32).reshape(B, T, HG_HEADS, HG_DV))
    out_a = o.reshape(B, T, HG_VW).astype(x.dtype) @ w_pa

    xc, cbuf_new = _causal_conv(lx, cbuf, conv_w, conv_b)
    xb = xc.reshape(B, T, LRU_BLOCKS, LRU_BW)
    ra = (jnp.einsum('btnc,ncd->btnd', xb, wa) + ba).reshape(B, T, LRU_W).astype(f32)
    ix = (jnp.einsum('btnc,ncd->btnd', xb, wx) + bx).reshape(B, T, LRU_W).astype(f32)
    h, h_last = _rglru(xc.astype(f32), ra, ix, log_lambda.astype(f32), h0.astype(f32), fresh)
    out_b = (jax.nn.gelu(ly) * h.astype(x.dtype)) @ w_pb

    merged = jax.nn.sigmoid(ga) * out_a + jax.nn.sigmoid(gb) * out_b
    x = x + _rmsnorm(merged @ w_o, n_mix_post)

    hn = _rmsnorm(x, n_ffn_pre)
    gate, up = jnp.split(hn @ w_fi, 2, axis=-1)
    x = x + _rmsnorm((jax.nn.silu(gate) * up) @ w_fo, n_ffn_post)
    return x, S_new.astype(S0.dtype), h_last.astype(h0.dtype), cbuf_new.astype(cbuf.dtype)

def setup_inputs(seed: int = 0) -> dict:
    key = jax.random.key(seed)
    ks = jax.random.split(key, 32)
    f32 = jnp.float32

    def nrm(k, shape, scale):
        return jax.random.normal(k, shape, f32) * scale

    def gain(k, shape):
        return 1.0 + 0.05 * jax.random.normal(k, shape, f32)

    a_c = jax.random.uniform(ks[20], (DEPTH, LRU_W), f32, 0.9, 0.999)
    s = a_c ** (1.0 / LRU_C)
    log_lambda = jnp.log(s) - jnp.log1p(-s)
    return {
        "x_prompt": nrm(ks[0], (BATCH, SEQ, D_MODEL), 1.0),
        "x_sample": nrm(ks[1], (DEC_BATCH, DEC_SEQ, D_MODEL), 1.0),
        "state_hgrn": nrm(ks[2], (DEPTH, DEC_BATCH, HG_HEADS, HG_DK, HG_DV), 0.3),
        "state_lru": nrm(ks[3], (DEPTH, DEC_BATCH, LRU_W), 0.5),
        "state_conv": nrm(ks[4], (DEPTH, DEC_BATCH, CONV_W - 1, LRU_W), 1.0),
        "norm_mix_pre": gain(ks[5], (DEPTH, D_MODEL)),
        "norm_mix_post": gain(ks[6], (DEPTH, D_MODEL)),
        "norm_ffn_pre": gain(ks[7], (DEPTH, D_MODEL)),
        "norm_ffn_post": gain(ks[8], (DEPTH, D_MODEL)),
        "w_in": nrm(ks[9], (DEPTH, D_MODEL, N_IN), D_MODEL ** -0.5),
        "hg_lb_logits": nrm(ks[10], (DEPTH + 1, HG_KW), 0.5),
        "hg_out_norm": gain(ks[11], (DEPTH, HG_DV)),
        "lru_conv_w": nrm(ks[12], (DEPTH, CONV_W, LRU_W), CONV_W ** -0.5),
        "lru_conv_b": nrm(ks[13], (DEPTH, LRU_W), 0.02),
        "lru_w_a": nrm(ks[14], (DEPTH, LRU_BLOCKS, LRU_BW, LRU_BW), LRU_BW ** -0.5),
        "lru_b_a": nrm(ks[15], (DEPTH, LRU_BLOCKS, LRU_BW), 0.1),
        "lru_w_x": nrm(ks[16], (DEPTH, LRU_BLOCKS, LRU_BW, LRU_BW), LRU_BW ** -0.5),
        "lru_b_x": nrm(ks[17], (DEPTH, LRU_BLOCKS, LRU_BW), 0.1),
        "lru_log_lambda": log_lambda,
        "w_branch_a": nrm(ks[18], (DEPTH, HG_VW, D_MODEL), HG_VW ** -0.5),
        "w_branch_b": nrm(ks[19], (DEPTH, LRU_W, D_MODEL), LRU_W ** -0.5),
        "w_out": nrm(ks[21], (DEPTH, D_MODEL, D_MODEL), D_MODEL ** -0.5),
        "w_ffn_in": nrm(ks[22], (DEPTH, D_MODEL, 2 * D_FF), D_MODEL ** -0.5),
        "w_ffn_out": nrm(ks[23], (DEPTH, D_FF, D_MODEL), D_FF ** -0.5),
    }

def reference(x_prompt, x_sample, state_hgrn, state_lru, state_conv,
              norm_mix_pre, norm_mix_post, norm_ffn_pre, norm_ffn_post, w_in,
              hg_lb_logits, hg_out_norm, lru_conv_w, lru_conv_b, lru_w_a, lru_b_a,
              lru_w_x, lru_b_x, lru_log_lambda, w_branch_a, w_branch_b, w_out,
              w_ffn_in, w_ffn_out):
    lb_all = jnp.cumsum(jax.nn.softmax(hg_lb_logits.astype(jnp.float32), axis=0), axis=0)
    yp, ys = x_prompt, x_sample
    hg_p, lru_p, cv_p, hg_s, lru_s, cv_s = [], [], [], [], [], []
    for l in range(DEPTH):
        lp = (norm_mix_pre[l], norm_mix_post[l], norm_ffn_pre[l], norm_ffn_post[l], w_in[l],
              hg_out_norm[l], lru_conv_w[l], lru_conv_b[l], lru_w_a[l], lru_b_a[l],
              lru_w_x[l], lru_b_x[l], lru_log_lambda[l], w_branch_a[l], w_branch_b[l],
              w_out[l], w_ffn_in[l], w_ffn_out[l])
        S0p = jnp.zeros((BATCH, HG_HEADS, HG_DK, HG_DV), state_hgrn.dtype)
        h0p = jnp.zeros((BATCH, LRU_W), state_lru.dtype)
        c0p = jnp.zeros((BATCH, CONV_W - 1, LRU_W), state_conv.dtype)
        yp, a1, a2, a3 = _layer(yp, S0p, h0p, c0p, True, HG_CHUNK, lb_all[l], *lp)
        ys, b1, b2, b3 = _layer(ys, state_hgrn[l], state_lru[l], state_conv[l], False,
                                ys.shape[1], lb_all[l], *lp)
        hg_p.append(a1); lru_p.append(a2); cv_p.append(a3)
        hg_s.append(b1); lru_s.append(b2); cv_s.append(b3)
    return (yp, ys, jnp.stack(hg_p), jnp.stack(lru_p), jnp.stack(cv_p),
            jnp.stack(hg_s), jnp.stack(lru_s), jnp.stack(cv_s))


_drawn_inputs = setup_inputs


def setup_inputs(seed=0):
    import zlib

    import numpy as np

    out = dict(_drawn_inputs(seed))
    spreads = {}
    factors = {}
    for name, (base, spread) in spreads.items():
        noise = np.random.default_rng([zlib.crc32(name.encode()), seed]).standard_normal(out[name].shape)
        drawn = base * np.exp(spread * noise) if base else spread * noise
        out[name] = __import__('jax').numpy.asarray(drawn.astype(out[name].dtype))
    for name, factor in factors.items():
        out[name] = (out[name] * factor).astype(out[name].dtype)
    return out
```

```python
from contextlib import ExitStack

import concourse.bass as bass
from concourse import mybir

F32 = mybir.dt.float32
F32R = mybir.dt.float32r
U8 = mybir.dt.uint8
ALU = mybir.AluOpType
AF = mybir.ActivationFunctionType
MUL, ADD, SUB = ALU.mult, ALU.add, ALU.subtract

P = 128
D = 1024
KT = D // P
TP = 512
NB = 8
T = TP + NB
TH = T // 2
NH = 8
NCH = TP // P
NLEV = 8
DFF = 2816
FT = DFF // P
KSPLIT = (6, 6, 5, 5)
KOFF = (0, 6, 12, 17)
CW = 4
EPS = 1e-6

R_MPRE, R_MPOST, R_FPRE, R_FPOST = 0, 8, 16, 24
R_LB, R_CW, R_CB, R_BA, R_BX, R_LL, R_ON = 32, 48, 80, 88, 96, 104, 112
NROW = 113
MW = P + (NLEV - 1) * P // 2

Q_HG, Q_LRU, Q_MIX, Q_OUT, Q_FFI, Q_FFO = NH, NH // 2, KT, 2, FT // 2, KT
G_HG = 0
G_LRU = G_HG + Q_HG
G_MIX = G_LRU + Q_LRU
G_OUT = G_MIX + Q_MIX
G_FFI = G_OUT + Q_OUT
G_FFO = G_FFI + Q_FFI


class Chain:

    def __init__(self, eng, sem):
        self.eng, self.sem, self.base, self.k, self.i, self.per = eng, sem, 0, 0, None, 0

    def begin(self, i, per):
        self.base += self.k
        self.i, self.per, self.k = i, per, 0

    def end(self, n):
        assert self.k == self.per, (self.k, self.per)
        self.base += self.per * n
        self.i, self.k = None, 0

    def link(self, ins):
        ins.then_inc(self.sem, 1)
        self.k += 1

    def wait(self):
        v = self.base + self.k
        self.eng.wait_ge(self.sem, v if self.i is None else self.i * self.per + v)

    def then_wait(self, ins):
        self.link(ins)
        self.wait()


def hybrid_decoder(nc, x_prompt, x_sample, state_hgrn, state_lru, state_conv, norm_mix_pre, norm_mix_post,
                   norm_ffn_pre, norm_ffn_post, w_in, hg_lb_logits, hg_out_norm, lru_conv_w, lru_conv_b,
                   lru_w_a, lru_b_a, lru_w_x, lru_b_x, lru_log_lambda, w_branch_a, w_branch_b, w_out,
                   w_ffn_in, w_ffn_out, ident_in, masks_in, y_p, y_s, hg_p, lru_p, cv_p, hg_s, lru_s, cv_s):
    with ExitStack() as ctx:
        def sb(name, shape, dt=F32):
            return ctx.enter_context(nc.sbuf_tensor(name, shape, dt))

        sems = {}

        def E(name):
            if name not in sems:
                sems[name] = ctx.enter_context(nc.semaphore(name))
            return sems[name]

        raw = sb("raw", [P, 4, KT, P])
        wh = sb("wh", [P, 2, KT, P], F32R)
        wl = sb("wl", [P, 2, KT, P], F32R)
        acts = sb("acts", [P, 64, T], F32R)
        tmp = sb("tmp", [P, 16 * T])
        extra = sb("extra", [P, 3 * T])
        ident = sb("ident", [P, P])
        ones = sb("ones", [P, P])
        masks = sb("masks", [P, TP + (NLEV - 1) * TP // 2], U8)
        prm = sb("prm", [P, NROW])
        lb = sb("lb", [P, 2 * NH])
        c4 = sb("c4", [P, NH])
        sp = sb("sp", [P, 5 * NH])
        eps = sb("eps", [P, 1])
        cst = sb("cst", [P, NH, 3 * NB])
        hst = sb("hst", [P, NH, NB])
        hout = sb("hout", [P, 1 + NB, NH])
        cout = sb("cout", [P, 3 * (1 + NB), NH])

        pp = [ctx.enter_context(nc.psum_tensor(f"proj{i}", [P, 2, 512], F32)) for i in range(2)]
        pr = ctx.enter_context(nc.psum_tensor("pr", [P, 2, 512], F32))
        pi = ctx.enter_context(nc.psum_tensor("pi", [P, 2, 512], F32))
        SA, SB, PO, PM = pr[:, 0, :], pr[:, 1, :], pi[:, 0, :], pi[:, 1, :]
        xt_dram = nc.dram_tensor("xt_scratch", (P, KT * T), F32, kind="Internal").ap()

        XN, OA, GB, MG, HN, HD = (0, 8), (16, 24), (32, 40), (48, 56), (0, 8), (16, 16 + FT)

        def U(i, n=T, at=0):
            return tmp[:, i * T + at:i * T + at + n]

        def X(i, n=T, at=0):
            return extra[:, i * T + at:i * T + at + n]

        def halves(ap):
            return ap.rearrange("p (a t) -> p a t", a=2)

        def proj(par):
            return pp[par][:, :, 0:TH]

        def PRM(r):
            return prm[:, r:r + 1] if isinstance(r, int) else prm[:, bass.ds(r, 1)]

        def hi_of(reg, j):
            return acts[:, reg[0] + j, :] if isinstance(j, int) else acts[:, bass.ds(j + reg[0], 1), :].rearrange("p a t -> p (a t)")

        def lo_of(reg, j):
            return acts[:, reg[1] + j, :] if isinstance(j, int) else acts[:, bass.ds(j + reg[1], 1), :].rearrange("p a t -> p (a t)")

        def col(t3, n):
            return t3[:, :, bass.ds(n, 1)]

        VT, QP, KS, FF, SIG, SOG, AT = U(0), U(1), U(2), U(3), U(5), U(6), U(7, TP)
        TT = U(4, TP)
        VTOK, KTOK, SQ, RS, O1 = U(8, TP), U(9, TP), U(10), U(11), U(12)
        SCH = U(13, TP)
        SS = tmp[:, 14 * T:14 * T + NB * P].rearrange("p (b v) -> p b v", b=NB)
        VBD = extra[0:NB, 0:NB * P]
        STOK = extra[0:NB, 1024:1024 + 2 * P]
        QS = extra[:, 1280:1280 + NB]
        TOFF = {1: None}
        at = 0
        for b in (2, 4, 8, 16, 32, 64, 128):
            TOFF[b] = at
            at += TP // b

        def tot(b):
            return FF[:, 0:TP] if b == 1 else TT[:, TOFF[b]:TOFF[b] + TP // b]

        def mask(i):
            return masks[:, 0:TP] if i == 0 else masks[:, TP + (i - 1) * TP // 2:TP + i * TP // 2]

        XP = tmp[:, 0:T + 3]
        XC, SR, SI, SQT, WW, AA = U(2), U(3), U(4), U(5), U(6), U(7)
        LY, GSQ, HH = U(8), U(9), U(10)

        def wblock(i):
            return tmp[:, 11 * T + i * P:11 * T + (i + 1) * P]

        wi, wfi = w_in[0], w_ffn_in[0]
        wpa, wpb, wo, wfo = w_branch_a[0], w_branch_b[0], w_out[0], w_ffn_out[0]

        def at_col(i, off):
            return i * P + off if off else (i * 2) * (P // 2)

        def load_hg(i, s):
            return wi, at_col(i, (2 * D, 0, D, 3 * D)[s])

        def load_lru(i, s):
            return wi, i * 2 * P + (4 * D, 5 * D)[s % 2] + (s // 2) * P

        def load_mix(i, s):
            return (wi, wpa, wi, wpb)[s], at_col(i, (6 * D, 0, 7 * D, 0)[s])

        def load_out(i, s):
            return (wo, i * 4 * P + s * P) if s else (wo, (i * 4) * P)

        def load_ffi(i, s):
            off = (s // 2) * P + (s % 2) * DFF
            return (wfi, i * 2 * P + off) if off else (wfi, (i * 2) * P)

        def load_ffo(i, s):
            return wfo[KOFF[s] * P:(KOFF[s] + KSPLIT[s]) * P, :], i * P

        def load_block(eng, s, w, at):
            nk = w.shape[0] // P
            eng.dma_start(raw[:, s, 0:nk], w[:, bass.ds(at, P)].rearrange("(k p) n -> p k n", p=P))\
               .then_inc(E(f"raw_in{s}"), 16)

        block = ctx.enter_context(nc.Block())

        @block.sync
        def _(eng):
            x_t = x_prompt[0].rearrange("(c p) d -> p c d", p=P)
            for ch in range(NCH):
                eng.dma_start(tmp[:, ch * D:(ch + 1) * D], x_t[:, ch, :]).then_inc(E("x_in"), 16)
            eng.dma_start(extra[0:NB, 0:D], x_sample[:, 0, :]).then_inc(E("x_in"), 16)
            eng.dma_start(ident[:], ident_in).then_inc(E("x_in"), 16)
            pv = extra[:, D:D + P]
            rows = ((norm_mix_pre, R_MPRE, 8), (norm_mix_post, R_MPOST, 8), (norm_ffn_pre, R_FPRE, 8),
                    (norm_ffn_post, R_FPOST, 8), (lru_conv_b, R_CB, 8), (lru_log_lambda, R_LL, 8))
            for src, r, n in rows:
                eng.dma_start(pv[r:r + n, :], src[0].rearrange("(n p) -> n p", p=P)).then_inc(E("p_in"), 16)
            eng.dma_start(pv[R_LB:R_LB + 16, :], hg_lb_logits.rearrange("a (n p) -> (a n) p", p=P)).then_inc(E("p_in"), 16)
            eng.dma_start(pv[R_CW:R_CW + 32, :], lru_conv_w[0].rearrange("a (n p) -> (a n) p", p=P)).then_inc(E("p_in"), 16)
            eng.dma_start(pv[R_BA:R_BA + 8, :], lru_b_a[0]).then_inc(E("p_in"), 16)
            eng.dma_start(pv[R_BX:R_BX + 8, :], lru_b_x[0]).then_inc(E("p_in"), 16)
            eng.dma_start(pv[R_ON:R_ON + 1, :], hg_out_norm).then_inc(E("p_in"), 16)
            eng.dma_start(raw[0:3 * NB, 3], state_conv[0].rearrange("b j (n p) -> (b j) n p", p=P)).then_inc(E("s_in"), 16)
            eng.dma_start(raw[0:NB, 2], state_lru[0].rearrange("b (n p) -> b n p", p=P)).then_inc(E("s_in"), 16)
            eng.dma_start(raw[:, 1].rearrange("p k n -> p (k n)")[:, 0:MW], masks_in).then_inc(E("m_in"), 16)
            load_block(eng, 0, *load_hg(0, 0))
            eng.wait_ge(E("m_made"), NLEV)
            load_block(eng, 1, *load_hg(0, 1))
            eng.wait_ge(E("turned"), 2)
            for s in range(2, 4):
                load_block(eng, s, *load_hg(0, s))
            eng.wait_ge(E("xt_ready"), KT)
            eng.dma_start(xt_dram, tmp[:, 8 * T:16 * T]).then_inc(E("xt_out"), 16)

            def load_quad(src, i, g):
                for s in range(4):
                    w, at = src(i, s)
                    eng.wait_ge(E("lo_ready"), 4 * (g - 1) + s + 1)
                    load_block(eng, s, w, at)

            with eng.Fori(1, Q_HG) as i:
                load_quad(load_hg, i, i + G_HG)

            def load_gates(i):
                if isinstance(i, int):
                    eng.wait_ge(E("hg_done"), 1)
                for bb in range(2):
                    n = 2 * i + bb
                    if not isinstance(i, int):
                        eng.wait_ge(E("p_gates"), 2 * i + (bb - 1))
                    for a, w in enumerate((lru_w_a, lru_w_x)):
                        src = w[0, bass.ds(n, 1)].rearrange("n c d -> c (n d)")
                        eng.dma_start(wblock(2 * bb + a), src).then_inc(E(f"gates_in{bb}"), 16)

            load_quad(load_lru, 0, G_LRU)
            load_gates(0)
            with eng.Fori(1, Q_LRU) as i:
                load_quad(load_lru, i, i + G_LRU)
                load_gates(i)
            with eng.Fori(0, Q_MIX) as i:
                load_quad(load_mix, i, i + G_MIX)
            with eng.Fori(0, Q_OUT) as i:
                load_quad(load_out, i, i + G_OUT)
            eng.wait_ge(E("xt_out"), 16)
            eng.wait_ge(E("row_out"), 16 * 5)
            eng.dma_start(tmp[:, 8 * T:16 * T], xt_dram).then_inc(E("xt_back"), 16)
            with eng.Fori(0, Q_FFI) as i:
                load_quad(load_ffi, i, i + G_FFI)
            with eng.Fori(0, Q_FFO) as i:
                load_quad(load_ffo, i, i + G_FFO)
            for ch in range(NCH):
                eng.wait_ge(E("y_ready"), ch + 1)
                eng.dma_start(y_p[0, ch * P:(ch + 1) * P, :], raw[:, ch].rearrange("p k n -> p (k n)"))\
                   .then_inc(E("y_out"), 16)
            eng.wait_ge(E("y_ready"), NCH + 1)
            eng.dma_start(y_s[:, 0, :], extra[0:NB, 0:D]).then_inc(E("y_out"), 16)
            eng.wait_ge(E("y_out"), 16 * (NCH + 1))
            eng.wait_ge(E("xt_back"), 16)

        @block.gpsimd
        def _(eng):
            eng.wait_ge(E("rows_ready"), 1)
            rows = tmp[:, 13 * T:13 * T + 4 * P]
            hrow = rows[0:72, 0:P]
            eng.dma_start(lru_p[0, 0].rearrange("(n p) -> n p", p=P), hrow[0:8, :]).then_inc(E("row_out"), 16)
            eng.dma_start(lru_s[0].rearrange("b (n p) -> (b n) p", p=P), hrow[8:72, :]).then_inc(E("row_out"), 16)
            eng.dma_start(cv_p[0, 0].rearrange("j (n p) -> (j n) p", p=P), rows[0:24, P:2 * P]).then_inc(E("row_out"), 16)
            for k in range(2):
                eng.dma_start(cv_s[0, 4 * k:4 * k + 4].rearrange("b j (n p) -> (b j n) p", p=P),
                              rows[0:96, (2 + k) * P:(3 + k) * P]).then_inc(E("row_out"), 16)
            eng.wait_ge(E("row_out"), 16 * 5)

        @block.scalar
        def _(eng):
            ch = Chain(eng, E("act_order"))
            act = eng.activation

            def prep(u, s, nk=KT):
                g = (u - s) // 4 if isinstance(u, int) else None
                eng.wait_ge(E(f"raw_in{s}"), 16 * (g + 1) if g is not None else u * 4 + (16 - 4 * s))
                if not isinstance(u, int) or u >= 2:
                    eng.wait_ge(E("unit_done"), u - 1)
                act(wh[:, s % 2, 0:nk], raw[:, s, 0:nk], AF.Copy).then_inc(E("hi_ready"), 1)

            def posted(s):
                return E(f"proj_free{s % 2}")

            def stats(k, src):
                for j in range(KT):
                    if 8 * k + j >= 2:
                        eng.wait_ge(E("n_mm"), 8 * k + j - 1)
                    act(X(j % 2), src(j), AF.Square).then_inc(E("n_sq"), 1)
                eng.wait_ge(E("n_mm"), 8 * k + 8)
                act(halves(X(2)), pr[:, :, 0:TH], AF.Sqrt, bias=eps[:, 0:1], scale=1.0 / D).then_inc(E("n_std"), 1)

            eng.wait_ge(E("turned"), 1)
            act(prm[:], PM[:, 0:NROW], AF.Copy).then_inc(E("prm_ready"), 1)
            eng.wait_ge(E("turned"), 2)
            act(cst[:].rearrange("p n r -> p (n r)"), SA[:, 0:NH * 3 * NB], AF.Copy).then_inc(E("cst_ready"), 1)
            act(hst[:].rearrange("p n r -> p (n r)"), SB[:, 0:NH * NB], AF.Copy).then_inc(E("cst_ready"), 1)
            eng.wait_ge(E("lb_in"), 1)
            act(sp[:, 0:16], sp[:, 0:16], AF.Exp).then_inc(E("lb_exp"), 1)
            eng.wait_ge(E("lb_in"), 2)
            act(sp[:, 16:24], sp[:, 16:24], AF.Exp).then_inc(E("lb_exp"), 1)
            for j in range(KT):
                eng.wait_ge(E("x_turned"), j + 1)
                ch.link(act(U(8 + j, TP), pp[j % 2][:, 0, :], AF.Copy))
                act(U(8 + j, NB, TP), pp[j % 2][:, 1, 0:NB], AF.Copy).then_inc(E("xt_ready"), 1)
            ch.wait()
            eng.wait_ge(E("xt_ready"), KT)
            eng.wait_ge(E("eps_ready"), 2)
            stats(0, lambda j: U(8 + j))
            prep(0, 0)
            for j in range(KT):
                eng.wait_ge(E("d_norm"), j + 1)
                act(hi_of(XN, j), X(j % 2), AF.Copy).then_inc(E("a_nhi"), 1)

            eng.wait_ge(E("xn_done"), 1)
            eng.wait_ge(E("xt_out"), 16)

            def hg_steps(h, prev):
                prep(4 * h + 1, 1)
                if prev:
                    eng.wait_ge(E("unit_done"), 4 * h)
                    eng.wait_ge(E("d_f"), h)
                    act(halves(SIG), proj(1), AF.Sigmoid).then_inc(E("a_sg"), 1)
                prep(4 * h + 2, 2)
                eng.wait_ge(E("unit_done"), 4 * h + 1)
                if prev:
                    sample_rows(h - 1)
                act(halves(VT), proj(0), AF.Copy).then_inc(posted(0), 1)
                if prev:
                    turned_keys(h - 1)
                prep(4 * h + 3, 3)
                eng.wait_ge(E("unit_done"), 4 * h + 2)
                if prev:
                    eng.wait_ge(posted(1), 2 * h)
                act(halves(SIG), proj(1), AF.Sigmoid).then_inc(E("a_sq"), 1)
                if prev:
                    squares(h - 1)
                    state_out(h - 1)
                prep(4 * h + 4, 0)
                eng.wait_ge(E("unit_done"), 4 * h + 3)
                eng.wait_ge(posted(1), 2 * h + 1)
                act(halves(SIG), proj(0), AF.Sigmoid).then_inc(posted(2), 1)
                if prev:
                    roots(h - 1)
                eng.wait_ge(E("p_vt"), h + 1)
                act(VTOK, SA, AF.Copy).then_inc(E("a_vt"), 1)
                if prev:
                    out_high(h - 1)
                    state_in(h)

            def state_in(h):
                eng.wait_ge(E("st_out"), 32 * h)
                eng.dma_start(SS, state_hgrn[0, :, bass.ds(h, 1)].rearrange("b h k v -> k (b h) v"))\
                   .then_inc(E("st_in"), 16)

            def state_out(h):
                eng.wait_ge(E("d_kv"), h + 1)
                eng.dma_start(hg_p[0, 0, bass.ds(h, 1)].rearrange("h k v -> k (h v)"), SCH[:, 3 * P:4 * P])\
                   .then_inc(E("st_out"), 16)
                eng.wait_ge(E("d_half"), 2 * h + 2)
                eng.dma_start(hg_s[0, :, bass.ds(h, 1)].rearrange("b h k v -> k (b h) v"), SS)\
                   .then_inc(E("st_out"), 16)

            def sample_rows(h):
                eng.wait_ge(E("p_st"), h + 1)
                act(STOK, PM[0:NB, 0:2 * P], AF.Copy).then_inc(E("a_st"), 1)

            def turned_keys(h):
                eng.wait_ge(E("p_kst"), h + 1)
                act(KTOK, SB, AF.Copy).then_inc(E("a_kst"), 1)

            def squares(h):
                eng.wait_ge(E("p_os"), h + 1)
                eng.wait_ge(E("p_so"), h + 1)
                ch.link(act(SQ[:, 0:TP], PO, AF.Square))
                act(SQ[:, TP:T], PM[:, 0:NB], AF.Square).then_inc(E("a_square"), 1)

            def roots(h):
                eng.wait_ge(E("p_ones"), h + 1)
                ch.link(act(RS[:, 0:TP], SB, AF.Sqrt, bias=eps[:, 0:1], scale=1.0 / P))
                act(RS[:, TP:T], PM[:, NB:2 * NB], AF.Sqrt, bias=eps[:, 0:1], scale=1.0 / P).then_inc(E("a_sqrt"), 1)

            def out_high(h):
                eng.wait_ge(E("d_o"), h + 1)
                act(hi_of(OA, h), O1, AF.Copy).then_inc(E("a_ohi"), 1)

            ch.begin(0, 0)
            hg_steps(0, False)
            ch.end(1)
            eng.dma_start(SS, state_hgrn[0, :, 0].rearrange("b k v -> k b v")).then_inc(E("st_in"), 16)
            with eng.Fori(1, NH) as h:
                ch.begin(h - 1, 2)
                hg_steps(h, True)
                ch.end(NH - 1)
            h = NH - 1
            eng.wait_ge(E("unit_done"), 4 * NH)
            eng.wait_ge(E("d_f"), NH)
            act(halves(SIG), proj(1), AF.Sigmoid).then_inc(E("a_sg"), 1)
            sample_rows(h)
            turned_keys(h)
            squares(h)
            state_out(h)
            roots(h)
            out_high(h)

            eng.wait_ge(E("hg_done"), 1)

            def lru_pair(i):
                u0 = i * 4 + 4 * G_LRU
                for bb in range(2):
                    n = i * 2 + bb
                    prep(u0 + 2 * bb + 1, 2 * bb + 1)
                    if bb == 1:
                        gates(n - 1, 1)
                    elif not isinstance(i, int):
                        gates(n - 1, 1)
                    prep(u0 + 2 * bb + 2, (2 * bb + 2) % 4)
                    eng.wait_ge(E("unit_done"), u0 + 2 * bb + 1)
                    eng.wait_ge(E("d_xc"), n)
                    eng.wait_ge(E("d_m1"), n)
                    act(halves(XP[:, 3:3 + T]), proj(0), AF.Copy).then_inc(posted(0), 1)
                    eng.wait_ge(posted(0), i * 2 + 2 * G_LRU + bb + 1)
                    act(XC[:, 0:TP], XP[:, 0:TP], AF.Identity, bias=PRM(n + R_CB), scale=PRM(n + R_CW))\
                        .then_inc(E("a_tap"), 1)

            def gates(n, par):
                eng.wait_ge(E("unit_done"), n * 2 + 4 * G_LRU + 2)
                eng.wait_ge(E("d_hl"), n)
                ch.link(act(halves(LY), proj(1), AF.Copy))
                act(halves(GSQ), proj(1), AF.Square, scale=0.044715 ** 0.5).then_inc(posted(1), 1)
                eng.wait_ge(E("p_gates"), n + 1)
                eng.wait_ge(E("d_w"), n)
                ch.then_wait(act(halves(SR), pr[:, :, 0:TH], AF.Sigmoid, bias=PRM(n + R_BA)))
                act(SR, SR, AF.Tanh, scale=c4[:, n:n + 1] if isinstance(n, int) else c4[:, bass.ds(n, 1)]).then_inc(E("a_t"), 1)
                act(halves(SI), pi[:, :, 0:TH], AF.Sigmoid, bias=PRM(n + R_BX)).then_inc(E("a_si"), 1)
                eng.wait_ge(E("d_u"), n + 1)
                act(GSQ, GSQ, AF.Tanh, scale=0.7978845608028654).then_inc(E("a_th"), 1)
                eng.wait_ge(E("a_t"), n + 1)
                act(SQT, SR, AF.Sqrt).then_inc(E("a_sqt"), 1)
                eng.wait_ge(E("d_gh"), n + 1)
                act(hi_of(GB, n), LY, AF.Copy).then_inc(E("a_ghi"), 1)

            ch.begin(0, 2)
            lru_pair(0)
            ch.end(1)
            with eng.Fori(1, Q_LRU) as i:
                ch.begin(i - 1, 4)
                lru_pair(i)
                ch.end(Q_LRU - 1)
            prep(4 * G_MIX + 1, 1)
            gates(NH - 1, 1)

            eng.wait_ge(E("d_hl"), NH)
            with eng.Fori(0, Q_MIX) as j:
                g = j + G_MIX
                u0 = j * 4 + 4 * G_MIX
                prep(u0 + 2, 2)
                eng.wait_ge(E("unit_done"), u0 + 1)
                eng.wait_ge(posted(1), j * 2 + (2 * G_MIX - 1))
                act(halves(U(0)), proj(0), AF.Sigmoid).then_inc(posted(0), 1)
                prep(u0 + 3, 3)
                prep(u0 + 4, 0)
                eng.wait_ge(E("unit_done"), u0 + 3)
                eng.wait_ge(posted(1), j * 2 + 2 * G_MIX)
                act(halves(U(2)), proj(0), AF.Sigmoid).then_inc(posted(0), 1)
                prep(u0 + 5, 1)
                eng.wait_ge(E("d_mb"), j + 1)
                act(hi_of(MG, j), U(3), AF.Copy).then_inc(E("a_mhi"), 1)

            eng.wait_ge(E("d_mlo"), KT)
            with eng.Fori(0, Q_OUT) as i:
                for s in range(4):
                    u = i * 4 + 4 * G_OUT + s
                    eng.wait_ge(E("unit_done"), u + 1)
                    act(halves(tmp[:, bass.ds(i * 4 * T + s * T, T)]), proj(s % 2), AF.Copy).then_inc(posted(s), 1)
                    prep(u + 2, (s + 2) % 4)
            eng.wait_ge(posted(0), 2 * G_FFI)
            eng.wait_ge(posted(1), 2 * G_FFI)
            stats(1, lambda j: U(j))
            eng.wait_ge(E("d_x1"), KT)
            stats(2, lambda j: U(j))
            for j in range(KT):
                eng.wait_ge(E("d_norm"), KT + j + 1)
                act(hi_of(HN, j), X(j % 2), AF.Copy).then_inc(E("a_nhi"), 1)

            def ffi(i, last):
                u0 = i * 4 + 4 * G_FFI
                for jj in range(2):
                    j = i * 2 + jj
                    eng.wait_ge(E("unit_done"), u0 + 2 * jj + 1)
                    eng.wait_ge(posted(0), j + 2 * G_FFI)
                    act(halves(U(8)), proj(0), AF.Sigmoid).then_inc(E("a_sgate"), 1)
                    prep(u0 + 2 * jj + 2, (2 * jj + 2) % 4)
                    prep(u0 + 2 * jj + 3, (2 * jj + 3) % 4)
                    eng.wait_ge(posted(1), j + 2 * G_FFI + 1)
                    act(hi_of(HD, j), U(10), AF.Copy).then_inc(E("a_hhi"), 1)

            with eng.Fori(0, Q_FFI) as i:
                ffi(i, False)

            def ffo(i, last):
                for jj in range(2):
                    j = i * 2 + jj
                    for s in range(4):
                        u = i * 8 + 4 * G_FFO + 4 * jj + s
                        if not (last and jj == 1 and s >= 2):
                            eng.wait_ge(E("unit_done"), u + 1)
                            prep(u + 2, (s + 2) % 4, KSPLIT[(s + 2) % 4])
                    eng.wait_ge(E("unit_done"), u + 1)
                    act(halves(tmp[:, bass.ds(j * T + 8 * T, T)]), proj(jj), AF.Copy).then_inc(posted(jj), 1)

            eng.wait_ge(E("d_hlo"), FT)
            with eng.Fori(0, KT // 2 - 1) as i:
                ffo(i, False)
            ffo(KT // 2 - 1, True)
            eng.wait_ge(posted(0), 2 * G_FFO + KT // 2)
            eng.wait_ge(posted(1), 2 * G_FFO + KT // 2)
            stats(3, lambda j: U(8 + j))
            for cch in range(NCH):
                eng.wait_ge(E("y_turned"), cch + 1)
                act(raw[:, cch].rearrange("p (a k) n -> p a (k n)", a=2), pp[cch % 2][:, :, :], AF.Copy)\
                    .then_inc(E("y_ready"), 1)
            eng.wait_ge(E("y_turned"), NCH + 1)
            act(extra[0:NB, 0:D].rearrange("p (a k) -> p a k", a=2), pp[0][0:NB, :, :], AF.Copy).then_inc(E("y_ready"), 1)

        @block.vector
        def _(eng):
            ch = Chain(eng, E("dve_order"))
            tt, ts, stt, cp = eng.tensor_tensor, eng.tensor_scalar, eng.scalar_tensor_tensor, eng.tensor_copy

            def posted(s):
                return E(f"proj_free{s % 2}")

            def prep(u, s, nk=KT):
                eng.wait_ge(E("hi_ready"), u + 1)
                tt(wl[:, s % 2, 0:nk], raw[:, s, 0:nk], wh[:, s % 2, 0:nk].bitcast(F32), SUB).then_inc(E("lo_ready"), 1)

            def inverse_rms(k):
                eng.wait_ge(E("n_std"), k + 1)
                eng.reciprocal(X(2), X(2)).then_inc(E("n_rs"), 1)
                eng.wait_ge(E("n_rs"), k + 1)

            def normed(k, src, gain, reg):
                for j in range(KT):
                    n = KT * k + j
                    if j >= 2:
                        eng.wait_ge(E("a_nhi"), n - 1)
                        eng.wait_ge(E("d_nlo"), n - 1)
                    stt(X(j % 2), src(j), PRM(gain + j), X(2), MUL, MUL).then_inc(E("d_norm"), 1)
                    eng.wait_ge(E("a_nhi"), n + 1)
                    tt(lo_of(reg, j), X(j % 2), hi_of(reg, j).bitcast(F32), SUB).then_inc(E("d_nlo"), 1)

            eng.memset(ones[:], 1.0).then_inc(E("eps_ready"), 1)
            eng.memset(eps[:], EPS).then_inc(E("eps_ready"), 1)
            eng.wait_ge(E("m_in"), 16)
            for i in range(NLEV):
                n = P if i == 0 else P // 2
                at = 0 if i == 0 else P + (i - 1) * n
                src = raw[:, 1].rearrange("p k n -> p (k n)")[:, at:at + n].unsqueeze(1).to_broadcast([P, NCH, n])
                cp(mask(i).rearrange("p (c n) -> p c n", c=NCH), src).then_inc(E("m_made"), 1)
            eng.wait_ge(E("prm_ready"), 1)
            L0, L1 = prm[:, R_LB:R_LB + 8], prm[:, R_LB + 8:R_LB + 16]
            ll = prm[:, R_LL:R_LL + 8]
            mx = sp[:, 24:32]
            ch.then_wait(tt(mx, L0, L1, ALU.max))
            ch.link(tt(sp[:, 0:8], L0, mx, SUB))
            tt(sp[:, 8:16], L1, mx, SUB).then_inc(E("lb_in"), 1)
            ch.wait()
            ch.then_wait(ts(sp[:, 16:24], ll, -1.0, None, MUL))
            tt(sp[:, 16:24], sp[:, 16:24], ll, ALU.min).then_inc(E("lb_in"), 1)
            eng.wait_ge(E("lb_exp"), 1)
            ch.then_wait(tt(mx, sp[:, 0:8], sp[:, 8:16], ADD))
            ch.then_wait(eng.reciprocal(mx, mx))
            ch.link(tt(lb[:, 0:8], sp[:, 0:8], mx, MUL))
            ch.wait()
            ch.then_wait(ts(lb[:, 8:16], lb[:, 0:8], -1.0, 1.0, MUL, ADD))
            eng.wait_ge(E("lb_exp"), 2)
            ee, z, z2, acc = sp[:, 16:24], sp[:, 0:8], sp[:, 8:16], sp[:, 24:32]
            ch.then_wait(ts(z, ee, 2.0, None, ADD))
            ch.then_wait(eng.reciprocal(z, z))
            ch.then_wait(tt(z, z, ee, MUL))
            ch.then_wait(tt(z2, z, z, MUL))
            ch.then_wait(ts(acc, z2, 1.0 / 19, 1.0 / 17, MUL, ADD))
            for k in (15, 13, 11, 9, 7, 5, 3, 1):
                ch.then_wait(tt(acc, acc, z2, MUL))
                ch.then_wait(ts(acc, acc, 1.0 / k, None, ADD))
            ch.then_wait(tt(acc, acc, z, MUL))
            ch.then_wait(ts(z, ll, -4.0, 0.0, MUL, ALU.max))
            ch.then_wait(stt(c4[:], acc, 8.0, z, MUL, ADD))

            inverse_rms(0)
            normed(0, lambda j: U(8 + j), R_MPRE, XN)
            prep(0, 0)
            eng.wait_ge(E("xt_out"), 16)
            eng.memset(AT, 0.0).then_inc(E("xn_done"), 1)
            eng.wait_ge(E("xn_done"), 1)
            eng.wait_ge(E("m_made"), NLEV)

            def cols_of(ap, b):
                return ap.rearrange("p (n two b) -> p n two b", two=2, b=b)

            def level(h, i):
                eng.wait_ge(E("p_L"), h * 8 + i)
                if i == 1:
                    tt(QP[:, 0:TP], QP[:, 0:TP], FF[:, 0:TP], MUL).then_inc(E("d_L"), 1)
                else:
                    b = 1 << (i - 2)
                    n = TP // (2 * b)
                    tb = tot(b).rearrange("p (n two) -> p n two", two=2)
                    q2, k1 = cols_of(QP[:, 0:TP], b)[:, :, 1, :], cols_of(KS[:, 0:TP], b)[:, :, 0, :]
                    if i > 2:
                        ch.wait()
                    eng.wait_ge(E("d_L"), h * 8 + i - 1)
                    eng.wait_ge(E("d_take"), h * 8 + i - 1)
                    ch.link(tt(q2, q2, tb[:, :, 0:1].to_broadcast([P, n, b]), MUL))
                    ch.link(tt(tot(2 * b), tb[:, :, 0], tb[:, :, 1], MUL))
                    tt(k1, k1, tb[:, :, 1:2].to_broadcast([P, n, b]), MUL).then_inc(E("d_L"), 1)
                take(i - 1)

            def take(i):
                bank = SB if i % 2 == 0 else SA
                if i == 0:
                    eng.copy_predicated(AT, mask(0), bank).then_inc(E("d_take"), 1)
                else:
                    hs = 1 << (i - 1)
                    v = "p (n b) -> p n b"
                    eng.copy_predicated(cols_of(AT, hs)[:, :, 1, :], mask(i).rearrange(v, b=hs),
                                        bank[:, 0:TP // 2].rearrange(v, b=hs)).then_inc(E("d_take"), 1)

            def chunk_states(h):
                eng.wait_ge(E("p_kv"), h + 1)
                eng.wait_ge(E("st_out"), h * 32)
                t128 = tot(P)
                ch.wait()
                ch.then_wait(cp(SCH[:, 0:P], SA[:, 0:P]))
                for k in range(1, NCH):
                    o = stt(SCH[:, k * P:(k + 1) * P], SCH[:, (k - 1) * P:k * P], t128[:, k:k + 1],
                            SA[:, k * P:(k + 1) * P], MUL, ADD)
                    if k < NCH - 1:
                        ch.then_wait(o)
                o.then_inc(E("d_kv"), 1)

            def sample_values(h):
                eng.wait_ge(E("a_st"), h + 1)
                vs = STOK[:, P:2 * P].unsqueeze(1).to_broadcast([NB, NB, P])
                dd = ident[0:NB, 0:NB].unsqueeze(2).to_broadcast([NB, NB, P])
                tt(VBD.rearrange("p (b v) -> p b v", b=NB), vs, dd, MUL).then_inc(E("d_vbd"), 1)

            def sample_states(h):
                eng.wait_ge(E("st_in"), h * 16 + 16)
                for k, bank in enumerate((PM, SB)):
                    eng.wait_ge(E("p_outer"), h * 2 + k + 1)
                    for b in range(4):
                        o = stt(SS[:, 4 * k + b, :], SS[:, 4 * k + b, :], FF[:, TP + 4 * k + b:TP + 4 * k + b + 1],
                                bank[:, b * P:(b + 1) * P], MUL, ADD)
                        if b < 3:
                            ch.link(o)
                    o.then_inc(E("d_half"), 1)

            def finish(h):
                eng.wait_ge(E("a_sqrt"), h + 1)
                eng.wait_ge(E("a_ohi"), h)
                eng.wait_ge(E("d_olo"), h)
                ch.link(eng.reciprocal(RS, RS))
                ch.link(stt(O1[:, 0:TP], PO, PRM(R_ON), SOG[:, 0:TP], MUL, MUL))
                stt(O1[:, TP:T], PM[:, 0:NB], PRM(R_ON), SOG[:, TP:T], MUL, MUL).then_inc(E("d_o1"), 1)
                ch.wait()
                eng.wait_ge(E("d_o1"), h + 1)
                tt(O1, O1, RS, MUL).then_inc(E("d_o"), 1)

            def finish_low(h):
                eng.wait_ge(E("a_ohi"), h + 1)
                tt(lo_of(OA, h), O1, hi_of(OA, h).bitcast(F32), SUB).then_inc(E("d_olo"), 1)

            def out_gate(h):
                eng.wait_ge(E("a_sg"), h + 1)
                tt(halves(SOG), proj(1), halves(SIG), MUL).then_inc(posted(1), 1)

            def hg_steps(h, prev):
                prep(4 * h + 1, 1)
                if prev:
                    level(h - 1, 4)
                    out_gate(h - 1)
                    level(h - 1, 5)
                    level(h - 1, 6)
                    level(h - 1, 7)
                prep(4 * h + 2, 2)
                if prev:
                    level(h - 1, 8)
                    sample_values(h - 1)
                    chunk_states(h - 1)
                prep(4 * h + 3, 3)
                if prev:
                    sample_states(h - 1)
                    eng.wait_ge(E("p_os"), h)
                eng.wait_ge(E("a_sq"), h + 1)
                tt(halves(QP), proj(1), halves(SIG), MUL).then_inc(posted(1), 1)
                prep(4 * h + 4, 0)
                eng.wait_ge(posted(0), 2 * h + 2)
                eng.wait_ge(posted(1), 2 * h + 1)
                if prev:
                    eng.wait_ge(E("p_so"), h)
                ch.link(cp(QS, QP[:, TP:T]))
                lbs = lambda a: lb[:, a:a + 1] if isinstance(a, int) else lb[:, bass.ds(a, 1)]
                ch.then_wait(ts(FF, SIG, lbs(h + NH), lbs(h), MUL, ADD))
                ts(KS, FF, -1.0, 1.0, MUL, ADD).then_inc(E("d_f"), 1)
                eng.wait_ge(E("d_f"), h + 1)
                if prev:
                    finish(h - 1)
                level(h, 1)
                if prev:
                    finish_low(h - 1)
                level(h, 2)
                level(h, 3)

            ch.begin(0, PER0)
            hg_steps(0, False)
            ch.end(1)
            with eng.Fori(1, NH) as h:
                ch.begin(h - 1, PER1)
                hg_steps(h, True)
                ch.end(NH - 1)
            h = NH - 1
            for i in (4, 5, 6, 7):
                level(h, i)
                if i == 4:
                    out_gate(h)
            level(h, 8)
            sample_values(h)
            chunk_states(h)
            sample_states(h)
            finish(h)
            finish_low(h)
            eng.wait_ge(E("d_olo"), NH)
            eng.wait_ge(E("p_so"), NH)
            eng.wait_ge(E("p_os"), NH)
            eng.wait_ge(E("st_out"), 32 * NH)
            eng.memset(XP[:, 0:3], 0.0).then_inc(E("hg_done"), 1)

            def conv(n):
                eng.wait_ge(E("a_tap"), n + 1)
                w = lambda j: PRM(n + (R_CW + 8 * j))
                cs = (cst[:, n, :] if isinstance(n, int) else cst[:, bass.ds(n, 1), :].rearrange("p a r -> p (a r)"))\
                    .rearrange("p (b j) -> p b j", j=3)
                xs = XC[:, TP:T]
                ch.link(ts(xs, cs[:, :, 0], w(0), PRM(n + R_CB), MUL, ADD))
                ch.link(stt(XC[:, 0:TP], XP[:, 1:1 + TP], w(1), XC[:, 0:TP], MUL, ADD))
                ch.wait()
                ch.link(stt(xs, cs[:, :, 1], w(1), xs, MUL, ADD))
                ch.link(stt(XC[:, 0:TP], XP[:, 2:2 + TP], w(2), XC[:, 0:TP], MUL, ADD))
                ch.wait()
                ch.link(stt(xs, cs[:, :, 2], w(2), xs, MUL, ADD))
                ch.link(stt(XC[:, 0:TP], XP[:, 3:3 + TP], w(3), XC[:, 0:TP], MUL, ADD))
                ch.link(cp(cout[:, 0:3, bass.ds(n, 1)], XP[:, TP:TP + 3].unsqueeze(2)))
                co = cout[:, 3:27, bass.ds(n, 1)].rearrange("p (b j) n -> p b (j n)", j=3)
                ch.link(cp(co[:, :, 0:2], cs[:, :, 1:3]))
                ch.link(cp(co[:, :, 2:3], XP[:, 3 + TP:3 + T].unsqueeze(2)))
                ch.wait()
                stt(xs, XP[:, 3 + TP:3 + T], w(3), xs, MUL, ADD).then_inc(E("d_xc"), 1)

            def recurrence(n):
                eng.wait_ge(posted(1), n + 2 * G_LRU + 1)
                stt(GSQ, GSQ, 1.0, LY, ADD, MUL).then_inc(E("d_u"), 1)
                eng.wait_ge(E("a_t"), n + 1)
                ch.then_wait(ts(WW, SR, 1.0, None, ADD))
                ch.link(eng.reciprocal(WW, WW))
                eng.wait_ge(E("a_si"), n + 1)
                eng.wait_ge(E("d_xc"), n + 1)
                tt(SI, SI, XC, MUL).then_inc(E("d_m1"), 1)
                ch.wait()
                ch.link(ts(AA, WW, 2.0, -1.0, MUL, ADD))
                eng.wait_ge(E("a_sqt"), n + 1)
                stt(SQT, SQT, 2.0, WW, MUL, MUL).then_inc(E("d_w"), 1)
                eng.wait_ge(E("d_w"), n + 1)
                eng.wait_ge(E("d_m1"), n + 1)
                ch.link(tt(SQT[:, 1:T], SQT[:, 1:T], SI[:, 1:T], MUL))
                ch.link(cp(SQT[:, 0:1], SI[:, 0:1]))
                hs = hst[:, n, :] if isinstance(n, int) else hst[:, bass.ds(n, 1), :].rearrange("p a r -> p (a r)")
                ch.wait()
                ch.link(tt(HH[:, TP:T], AA[:, TP:T], hs, MUL))
                ch.link(eng.tensor_tensor_scan(HH[:, 0:TP], AA[:, 0:TP], SQT[:, 0:TP], 0.0, MUL, ADD))
                eng.wait_ge(E("a_th"), n + 1)
                ch.link(stt(LY, GSQ, 1.0, LY, ADD, MUL))
                ch.wait()
                ch.then_wait(tt(HH[:, TP:T], HH[:, TP:T], SQT[:, TP:T], ADD))
                stt(LY, LY, 0.5, HH, MUL, MUL).then_inc(E("d_gh"), 1)
                ch.link(cp(hout[:, :, bass.ds(n, 1)], HH[:, TP - 1:T].unsqueeze(2)))
                eng.wait_ge(E("a_ghi"), n + 1)
                tt(lo_of(GB, n), LY, hi_of(GB, n).bitcast(F32), SUB).then_inc(E("d_hl"), 1)

            def lru_pair(i):
                u0 = i * 4 + 4 * G_LRU
                for bb in range(2):
                    n = i * 2 + bb
                    prep(u0 + 2 * bb + 1, 2 * bb + 1)
                    if bb == 1 or not isinstance(i, int):
                        recurrence(n - 1)
                    prep(u0 + 2 * bb + 2, (2 * bb + 2) % 4)
                    conv(n)

            ch.begin(0, PER2)
            lru_pair(0)
            ch.end(1)
            with eng.Fori(1, Q_LRU) as i:
                ch.begin(i - 1, PER3)
                lru_pair(i)
                ch.end(Q_LRU - 1)
            prep(4 * G_MIX + 1, 1)
            recurrence(NH - 1)

            eng.wait_ge(E("a_ghi"), NH)
            eng.wait_ge(E("d_hl"), NH)
            with eng.Fori(0, Q_MIX) as j:
                u0 = j * 4 + 4 * G_MIX
                prep(u0 + 2, 2)
                eng.wait_ge(posted(0), j * 2 + 2 * G_MIX + 1)
                eng.wait_ge(E("unit_done"), u0 + 2)
                tt(halves(U(1)), proj(1), halves(U(0)), MUL).then_inc(posted(1), 1)
                prep(u0 + 3, 3)
                prep(u0 + 4, 0)
                eng.wait_ge(posted(0), j * 2 + 2 * G_MIX + 2)
                eng.wait_ge(E("unit_done"), u0 + 4)
                eng.wait_ge(E("d_mlo"), j)
                eng.wait_ge(E("a_mhi"), j)
                tt(halves(U(3)), proj(1), halves(U(2)), MUL).then_inc(posted(1), 1)
                prep(u0 + 5, 1)
                eng.wait_ge(posted(1), j * 2 + 2 * G_MIX + 2)
                tt(U(3), U(3), U(1), ADD).then_inc(E("d_mb"), 1)
                eng.wait_ge(E("a_mhi"), j + 1)
                tt(lo_of(MG, j), U(3), hi_of(MG, j).bitcast(F32), SUB).then_inc(E("d_mlo"), 1)
            rows = tmp[:, 13 * T:13 * T + 4 * P]
            eng.wait_ge(E("p_rows"), 1)
            ch.link(cp(rows[0:72, 0:P], SA[0:72, 0:P]))
            ch.link(cp(rows[0:24, P:2 * P], SA[0:24, P:2 * P]))
            cp(rows[0:96, 2 * P:4 * P], SA[0:96, 2 * P:4 * P]).then_inc(E("rows_ready"), 1)

            with eng.Fori(0, Q_OUT) as i:
                for s in range(4):
                    prep(i * 4 + 4 * G_OUT + s + 2, (s + 2) % 4)
            inverse_rms(1)
            eng.wait_ge(E("xt_back"), 16)
            for j in range(KT):
                ch.then_wait(stt(U(j), U(j), PRM(R_MPOST + j), X(2), MUL, MUL))
                tt(U(j), U(j), U(8 + j), ADD).then_inc(E("d_x1"), 1)
            inverse_rms(2)
            normed(1, lambda j: U(j), R_FPRE, HN)

            def ffi(i, last):
                u0 = i * 4 + 4 * G_FFI
                for jj in range(2):
                    j = i * 2 + jj
                    eng.wait_ge(E("a_sgate"), j + 1)
                    tt(halves(U(9)), proj(0), halves(U(8)), MUL).then_inc(posted(0), 1)
                    prep(u0 + 2 * jj + 2, (2 * jj + 2) % 4)
                    prep(u0 + 2 * jj + 3, (2 * jj + 3) % 4)
                    eng.wait_ge(E("unit_done"), u0 + 2 * jj + 2)
                    eng.wait_ge(E("a_hhi"), j)
                    eng.wait_ge(E("d_hlo"), j)
                    eng.wait_ge(posted(0), j + 2 * G_FFI + 1)
                    tt(halves(U(10)), proj(1), halves(U(9)), MUL).then_inc(posted(1), 1)
                    eng.wait_ge(posted(1), j + 2 * G_FFI + 1)
                    eng.wait_ge(E("a_hhi"), j + 1)
                    tt(lo_of(HD, j), U(10), hi_of(HD, j).bitcast(F32), SUB).then_inc(E("d_hlo"), 1)

            with eng.Fori(0, Q_FFI) as i:
                ffi(i, False)

            def ffo(i, last):
                for jj in range(2):
                    for s in range(4):
                        if not (last and jj == 1 and s >= 2):
                            prep(i * 8 + 4 * G_FFO + 4 * jj + s + 2, (s + 2) % 4, KSPLIT[(s + 2) % 4])

            with eng.Fori(0, KT // 2 - 1) as i:
                ffo(i, False)
            ffo(KT // 2 - 1, True)
            inverse_rms(3)
            for j in range(KT):
                ch.then_wait(stt(U(8 + j), U(8 + j), PRM(R_FPOST + j), X(2), MUL, MUL))
                tt(U(8 + j), U(8 + j), U(j), ADD).then_inc(E("d_y"), 1)

        @block.tensor
        def _(eng):
            mm = eng.matmul

            def unit(u, s, reg, fill=None, koff=0, nk=KT, par=None, free=None, first=True, last=True):
                par = s % 2 if par is None else par
                eng.wait_ge(E("lo_ready"), u + 1)
                if free is not None:
                    eng.wait_ge(E(f"proj_free{par}"), free)
                for k in range(nk):
                    xh, xl = acts[:, reg[0] + koff + k], acts[:, reg[1] + koff + k]
                    a, b = wh[:, s % 2, k, :], wl[:, s % 2, k, :]
                    for w, x in ((a, xh), (a, xl), (b, xh)):
                        for hf in range(2):
                            st = first and k == 0 and w is a and x is xh
                            o = mm(pp[par][:, hf, 0:TH], w, x[:, hf * TH:(hf + 1) * TH], start=st,
                                   stop=last and k == nk - 1 and w is b)
                    if k == nk - 1:
                        o.then_inc(E("unit_done"), 1)
                    if fill and k % 2 == 1 and k // 2 in fill:
                        for f in fill[k // 2]:
                            f()

            def stats(k):
                for j in range(KT):
                    eng.wait_ge(E("n_sq"), 8 * k + j + 1)
                    for hf in range(2):
                        o = mm(pr[:, hf, 0:TH], ones[:], X(j % 2, TH, hf * TH), start=j == 0, stop=j == KT - 1)
                    o.then_inc(E("n_mm"), 1)

            eng.wait_ge(E("x_in"), 16 * (NCH + 2))
            eng.wait_ge(E("p_in"), 16 * 11)
            eng.transpose(PM[:, 0:NROW], extra[0:NROW, D:D + P], ident[0:NROW, 0:NROW]).then_inc(E("turned"), 1)
            eng.wait_ge(E("s_in"), 32)
            for n in range(NH):
                eng.transpose(SA[:, n * 24:(n + 1) * 24], raw[0:24, 3, n, :], ident[0:24, 0:24])
                o = eng.transpose(SB[:, n * NB:(n + 1) * NB], raw[0:NB, 2, n, :], ident[0:NB, 0:NB])
            o.then_inc(E("turned"), 1)
            for j in range(KT):
                if j >= 2:
                    eng.wait_ge(E("xt_ready"), j - 1)
                for cch in range(NCH):
                    eng.transpose(pp[j % 2][:, 0, cch * P:(cch + 1) * P],
                                  tmp[:, cch * D + j * P:cch * D + (j + 1) * P], ident[:])
                o = eng.transpose(pp[j % 2][:, 1, 0:NB], extra[0:NB, j * P:(j + 1) * P], ident[0:NB, 0:NB])
                o.then_inc(E("x_turned"), 1)
            eng.wait_ge(E("turned"), 2)
            eng.wait_ge(E("cst_ready"), 2)
            eng.wait_ge(E("eps_ready"), 2)
            stats(0)
            eng.wait_ge(E("d_nlo"), KT)

            def turn_values(h, prev):
                if prev:
                    eng.wait_ge(E("d_kv"), h)
                eng.wait_ge(E("proj_free0"), 2 * h + 1)
                for k in range(NCH):
                    o = eng.transpose(SA[:, k * P:(k + 1) * P], VT[:, k * P:(k + 1) * P], ident[:])
                o.then_inc(E("p_vt"), 1)

            def score(h, i, prev=True):
                if i == 0:
                    eng.wait_ge(E("d_f"), h + 1)
                    if prev:
                        eng.wait_ge(E("a_sqrt"), h)
                else:
                    eng.wait_ge(E("d_L"), h * 8 + i)
                    if i == 1:
                        eng.wait_ge(E("a_vt"), h + 1)
                    else:
                        eng.wait_ge(E("d_take"), h * 8 + i - 1)
                bank = SB if i % 2 == 0 else SA
                n = P if i == 0 else P // 2
                for k in range(NCH):
                    rhs = QP[:, k * P:(k + 1) * P]
                    if i:
                        rhs = rhs.rearrange("p (n two b) -> p n two b", two=2, b=1 << (i - 1))[:, :, 1, :]
                    o = mm(bank[:, k * n:(k + 1) * n], KS[:, k * P:(k + 1) * P], rhs, start=True, stop=True)
                o.then_inc(E("p_L"), 1)

            def turn_sample(h):
                if not isinstance(h, int) or h > 0:
                    eng.wait_ge(E("d_o1"), h)
                    eng.wait_ge(E("a_sqrt"), h)
                eng.transpose(PM[0:NB, 0:P], KS[:, TP:T], ident[:])
                eng.transpose(PM[0:NB, P:2 * P], VT[:, TP:T], ident[:]).then_inc(E("p_st"), 1)

            def turn_keys(h):
                eng.wait_ge(E("d_L"), h * 8 + 8)
                eng.wait_ge(E("d_take"), h * 8 + 7)
                for k in range(NCH):
                    o = eng.transpose(SB[:, k * P:(k + 1) * P], KS[:, k * P:(k + 1) * P], ident[:])
                o.then_inc(E("p_kst"), 1)

            def key_values(h):
                eng.wait_ge(E("a_kst"), h + 1)
                eng.wait_ge(E("d_take"), h * 8 + 8)
                for k in range(NCH):
                    o = mm(SA[:, k * P:(k + 1) * P], KTOK[:, k * P:(k + 1) * P], VTOK[:, k * P:(k + 1) * P],
                           start=True, stop=True)
                o.then_inc(E("p_kv"), 1)

            def out_scores(h):
                if not isinstance(h, int) or h > 0:
                    eng.wait_ge(E("d_o1"), h)
                for k in range(NCH):
                    mm(PO[:, k * P:(k + 1) * P], VTOK[:, k * P:(k + 1) * P], AT[:, k * P:(k + 1) * P],
                       start=k == 0, stop=False, skip_group_check=True)

            def out_states(h):
                eng.wait_ge(E("d_kv"), h + 1)
                for k in range(1, NCH):
                    o = mm(PO[:, k * P:(k + 1) * P], SCH[:, (k - 1) * P:k * P], QP[:, k * P:(k + 1) * P],
                           start=False, stop=k == NCH - 1, skip_group_check=True)
                o.then_inc(E("p_os"), 1)

            def outer(h, k):
                eng.wait_ge(E("d_vbd"), h + 1)
                mm((PM, SB)[k], STOK[:, 0:P], VBD[:, k * 512:(k + 1) * 512], start=True, stop=True)\
                    .then_inc(E("p_outer"), 1)

            def sample_out(h):
                eng.wait_ge(E("d_half"), h * 2 + 2)
                for b in range(NB):
                    o = mm(PM[:, b:b + 1], SS[:, b, :], QS[:, b:b + 1], start=True, stop=True)
                o.then_inc(E("p_so"), 1)

            def head_sums(h):
                eng.wait_ge(E("a_square"), h + 1)
                mm(SB, ones[:], SQ[:, 0:TP], start=True, stop=True)
                mm(PM[:, NB:2 * NB], ones[:], SQ[:, TP:T], start=True, stop=True).then_inc(E("p_ones"), 1)

            def hg_steps(h, prev):
                free = (lambda k: 2 * h + k) if prev else (lambda k: None)
                p = h - 1
                unit(4 * h, 0, XN, {k: [lambda k=k: score(p, k + 3)] for k in range(4)} if prev else None, free=free(0))
                unit(4 * h + 1, 1, XN, {0: [lambda: score(p, 7), lambda: turn_sample(p)], 1: [lambda: turn_keys(p)],
                                        2: [lambda: key_values(p)], 3: [lambda: out_scores(p)]} if prev else None, free=free(0))
                unit(4 * h + 2, 2, XN, {0: [lambda: out_states(p), lambda: outer(p, 0)], 1: [lambda: outer(p, 1)],
                                        2: [lambda: sample_out(p)], 3: [lambda: head_sums(p)]} if prev else None, free=2 * h + 1)
                unit(4 * h + 3, 3, XN, {0: [lambda: turn_values(h, prev)], 1: [lambda: score(h, 0, prev)],
                                        2: [lambda: score(h, 1)], 3: [lambda: score(h, 2)]}, free=2 * h + 1)

            hg_steps(0, False)
            with eng.Fori(1, NH) as h:
                hg_steps(h, True)
            h = NH - 1
            for i in range(3, 8):
                score(h, i)
            turn_sample(h)
            turn_keys(h)
            key_values(h)
            out_scores(h)
            out_states(h)
            outer(h, 0)
            outer(h, 1)
            sample_out(h)
            head_sums(h)

            def gate_sums(n, bb, i):
                eng.wait_ge(E("d_xc"), n + 1)
                if not isinstance(n, int) or n > 0:
                    eng.wait_ge(E("a_si"), n)
                else:
                    eng.wait_ge(E("hg_done"), 1)
                eng.wait_ge(E(f"gates_in{bb}"), i * 32 + 32)
                for a, bank in enumerate((pr, pi)):
                    for hf in range(2):
                        o = mm(bank[:, hf, 0:TH], wblock(2 * bb + a), XC[:, hf * TH:(hf + 1) * TH], start=True, stop=True)
                o.then_inc(E("p_gates"), 1)

            def lru_pair(i):
                for bb in range(2):
                    n = i * 2 + bb
                    v = i * 2 + 2 * G_LRU + bb
                    u = i * 4 + 4 * G_LRU + 2 * bb
                    unit(u, 2 * bb, XN, free=v)
                    unit(u + 1, 2 * bb + 1, XN, {3: [lambda: gate_sums(n, bb, i)]}, free=v)

            lru_pair(0)
            with eng.Fori(1, Q_LRU) as i:
                lru_pair(i)

            with eng.Fori(0, Q_MIX) as j:
                for s, reg in enumerate((XN, OA, XN, GB)):
                    if s % 2:
                        eng.wait_ge(E("d_hl" if s == 3 else "d_olo"), NH)
                    unit(j * 4 + 4 * G_MIX + s, s, reg, free=j * 2 + 2 * G_MIX + s // 2)
            eng.wait_ge(E("d_hl"), NH)
            hv, cv = hout[:].rearrange("p a n -> p (a n)"), cout[:].rearrange("p a n -> p (a n)")
            eng.transpose(SA[0:72, 0:P], hv, ident[:])
            eng.transpose(SA[0:24, P:2 * P], cv[:, 0:24], ident[:])
            for k in range(2):
                o = eng.transpose(SA[0:96, (2 + k) * P:(3 + k) * P], cv[:, 24 + 96 * k:120 + 96 * k], ident[:])
            o.then_inc(E("p_rows"), 1)
            eng.wait_ge(E("d_mlo"), KT)
            with eng.Fori(0, Q_OUT) as i:
                for s in range(4):
                    unit(i * 4 + 4 * G_OUT + s, s, MG, free=i * 2 + 2 * G_OUT + s // 2)
            stats(1)
            stats(2)
            eng.wait_ge(E("d_nlo"), 2 * KT)
            with eng.Fori(0, Q_FFI) as i:
                for s in range(4):
                    unit(i * 4 + 4 * G_FFI + s, s, HN, free=i * 2 + 2 * G_FFI + s // 2)
            eng.wait_ge(E("d_hlo"), FT)
            with eng.Fori(0, KT // 2) as i:
                for jj in range(2):
                    for s in range(4):
                        unit(i * 8 + 4 * G_FFO + 4 * jj + s, s, HD, koff=KOFF[s], nk=KSPLIT[s], par=jj,
                             free=i + 2 * G_FFO if s == 0 else None, first=s == 0, last=s == 3)
            stats(3)
            for cch in range(NCH + 1):
                eng.wait_ge(E("d_y"), KT)
                if cch >= 2:
                    eng.wait_ge(E("y_ready"), cch - 1)
                m = P if cch < NCH else NB
                for j in range(KT):
                    o = eng.transpose(pp[cch % 2][0:m, j // 4, (j % 4) * P:(j % 4 + 1) * P],
                                      U(8 + j, m, cch * P), ident[:])
                o.then_inc(E("y_turned"), 1)


PER0, PER1, PER2, PER3 = 6, 27, 28, 38

_INS = ["x_prompt", "x_sample", "state_hgrn", "state_lru", "state_conv", "norm_mix_pre", "norm_mix_post",
        "norm_ffn_pre", "norm_ffn_post", "w_in", "hg_lb_logits", "hg_out_norm", "lru_conv_w", "lru_conv_b",
        "lru_w_a", "lru_b_a", "lru_w_x", "lru_b_x", "lru_log_lambda", "w_branch_a", "w_branch_b", "w_out",
        "w_ffn_in", "w_ffn_out"]
_OUTS = [(1, TP, D), (NB, 1, D), (1, 1, NH, P, P), (1, 1, D), (1, 1, CW - 1, D),
         (1, NB, NH, P, P), (1, NB, D), (1, NB, CW - 1, D)]


def _level_masks(np):
    s = np.arange(P)[:, None]
    out = [np.eye(P, dtype=np.float32)]
    for i in range(1, NLEV):
        hs = 1 << (i - 1)
        tc = np.arange(P // 2)[None, :]
        t = tc // hs * 2 * hs + hs + tc % hs
        m = (s // (2 * hs) == t // (2 * hs)) & (s % (2 * hs) < hs)
        out.append(m.astype(np.float32))
    return np.ascontiguousarray(np.concatenate(out, axis=1))


def kernel(**inputs):
    import numpy as np
    import concourse.bacc as bacc
    from concourse import mybir as mb
    from concourse.bass_utils import run_bass_kernel_spmd as run

    nc = bacc.Bacc("TRN2", target_bir_lowering=False, num_devices=1)
    arrays, args = {}, []
    for name in _INS:
        a = np.ascontiguousarray(inputs[name])
        arrays[f"in_{name}"] = a
        args.append(nc.dram_tensor(f"in_{name}", a.shape, mb.dt.from_np(a.dtype), kind="ExternalInput").ap())
    for name, a in (("ident", np.eye(P, dtype=np.float32)), ("masks", _level_masks(np))):
        arrays[f"in_{name}"] = a
        args.append(nc.dram_tensor(f"in_{name}", a.shape, mb.dt.from_np(a.dtype), kind="ExternalInput").ap())
    for i, shape in enumerate(_OUTS):
        args.append(nc.dram_tensor(f"out_{i}", shape, mb.dt.float32, kind="ExternalOutput").ap())
    hybrid_decoder(nc, *args)
    r = run(nc, [arrays], core_ids=[0])
    return tuple(r.results[0][f"out_{i}"] for i in range(len(_OUTS)))
```

```python
from contextlib import ExitStack

import concourse.bass as bass
from concourse import mybir

F32 = mybir.dt.float32
F32R = mybir.dt.float32r
U8 = mybir.dt.uint8
ALU = mybir.AluOpType
AF = mybir.ActivationFunctionType
MUL, ADD, SUB = ALU.mult, ALU.add, ALU.subtract

P = 128
D = 1024
KT = D // P
TP = 512
NB = 8
T = TP + NB
TH = T // 2
NH = 8
NCH = TP // P
NLEV = 8
DFF = 2816
FT = DFF // P
KSPLIT = (6, 6, 5, 5)
KOFF = (0, 6, 12, 17)
CW = 4
EPS = 1e-6

R_MPRE, R_MPOST, R_FPRE, R_FPOST = 0, 8, 16, 24
R_LB, R_CW, R_CB, R_BA, R_BX, R_LL, R_ON = 32, 48, 80, 88, 96, 104, 112
NROW = 113
MW = P + (NLEV - 1) * P // 2

Q_HG, Q_LRU, Q_MIX, Q_OUT, Q_FFI, Q_FFO = NH, NH // 2, KT, 2, FT // 2, KT
G_HG = 0
G_LRU = G_HG + Q_HG
G_MIX = G_LRU + Q_LRU
G_OUT = G_MIX + Q_MIX
G_FFI = G_OUT + Q_OUT
G_FFO = G_FFI + Q_FFI


class Chain:

    def __init__(self, eng, sem):
        self.eng, self.sem, self.base, self.k, self.i, self.per = eng, sem, 0, 0, None, 0

    def begin(self, i, per):
        self.base += self.k
        self.i, self.per, self.k = i, per, 0

    def end(self, n):
        assert self.k == self.per, (self.k, self.per)
        self.base += self.per * n
        self.i, self.k = None, 0

    def link(self, ins):
        ins.then_inc(self.sem, 1)
        self.k += 1

    def wait(self):
        v = self.base + self.k
        self.eng.wait_ge(self.sem, v if self.i is None else self.i * self.per + v)

    def then_wait(self, ins):
        self.link(ins)
        self.wait()


def hybrid_decoder(nc, x_prompt, x_sample, state_hgrn, state_lru, state_conv, norm_mix_pre, norm_mix_post,
                   norm_ffn_pre, norm_ffn_post, w_in, hg_lb_logits, hg_out_norm, lru_conv_w, lru_conv_b,
                   lru_w_a, lru_b_a, lru_w_x, lru_b_x, lru_log_lambda, w_branch_a, w_branch_b, w_out,
                   w_ffn_in, w_ffn_out, ident_in, masks_in, y_p, y_s, hg_p, lru_p, cv_p, hg_s, lru_s, cv_s):
    with ExitStack() as ctx:
        def sb(name, shape, dt=F32):
            return ctx.enter_context(nc.sbuf_tensor(name, shape, dt))

        sems = {}

        def E(name):
            if name not in sems:
                sems[name] = ctx.enter_context(nc.semaphore(name))
            return sems[name]

        raw = sb("raw", [P, 4, KT, P])
        wh = sb("wh", [P, 2, KT, P], F32R)
        wl = sb("wl", [P, 2, KT, P], F32R)
        acts = sb("acts", [P, 64, T], F32R)
        tmp = sb("tmp", [P, 16 * T])
        extra = sb("extra", [P, 3 * T])
        ident = sb("ident", [P, P])
        ones = sb("ones", [P, P])
        masks = sb("masks", [P, TP + (NLEV - 1) * TP // 2], U8)
        prm = sb("prm", [P, NROW])
        lb = sb("lb", [P, 2 * NH])
        c4 = sb("c4", [P, 2 * NH])
        sp = sb("sp", [P, 5 * NH])
        eps = sb("eps", [P, 1])
        cst = sb("cst", [P, NH, 3 * NB])
        hst = sb("hst", [P, NH, NB])
        hout = sb("hout", [P, 1 + NB, NH])
        cout = sb("cout", [P, 3 * (1 + NB), NH])

        pp = [ctx.enter_context(nc.psum_tensor(f"proj{i}", [P, 2, 512], F32)) for i in range(2)]
        pr = ctx.enter_context(nc.psum_tensor("pr", [P, 2, 512], F32))
        pi = ctx.enter_context(nc.psum_tensor("pi", [P, 2, 512], F32))
        SA, SB, PO, PM = pr[:, 0, :], pr[:, 1, :], pi[:, 0, :], pi[:, 1, :]
        xt_dram = nc.dram_tensor("xt_scratch", (P, KT * T), F32, kind="Internal").ap()

        XN, OA, GB, MG, HN, HD = (0, 8), (16, 24), (32, 40), (48, 56), (0, 8), (16, 16 + FT)

        def U(i, n=T, at=0):
            return tmp[:, i * T + at:i * T + at + n]

        def X(i, n=T, at=0):
            return extra[:, i * T + at:i * T + at + n]

        def halves(ap):
            return ap.rearrange("p (a t) -> p a t", a=2)

        def proj(par):
            return pp[par][:, :, 0:TH]

        def PRM(r):
            return prm[:, r:r + 1] if isinstance(r, int) else prm[:, bass.ds(r, 1)]

        def hi_of(reg, j):
            return acts[:, reg[0] + j, :] if isinstance(j, int) else acts[:, bass.ds(j + reg[0], 1), :].rearrange("p a t -> p (a t)")

        def lo_of(reg, j):
            return acts[:, reg[1] + j, :] if isinstance(j, int) else acts[:, bass.ds(j + reg[1], 1), :].rearrange("p a t -> p (a t)")

        def col(t3, n):
            return t3[:, :, bass.ds(n, 1)]

        FF, QP, KS, VT, SIG, SOG, AT = U(0), U(1), U(2), U(3), U(5), U(6), U(7, TP)
        TT = U(11, TP)
        VTOK, KTOK, SQ, O1 = U(8, TP), U(9, TP), U(10), U(12)
        SCH = U(13, TP)
        SS = tmp[:, 14 * T:14 * T + NB * P].rearrange("p (b v) -> p b v", b=NB)
        VBD = extra[0:NB, 0:NB * P]
        STOK = extra[0:NB, 1024:1024 + 2 * P]
        QS = extra[:, 1280:1280 + NB]
        TOFF = {1: None}
        at = 0
        for b in (2, 4, 8, 16, 32, 64, 128):
            TOFF[b] = at
            at += TP // b

        def tot(b):
            return FF[:, 0:TP] if b == 1 else TT[:, TOFF[b]:TOFF[b] + TP // b]

        def mask(i):
            return masks[:, 0:TP] if i == 0 else masks[:, TP + (i - 1) * TP // 2:TP + i * TP // 2]

        NX = CW - 1 + T + CW * NB
        XP = tmp[:, 6 * T - NX:6 * T]
        XS = XP[:, CW - 1 + T:NX].rearrange("p (b j) -> p b j", j=CW)
        XF = tmp[:, 3 * T:3 * T + NX - (CW - 1)]
        SR, SI, AA, XC, TA, SQT = U(0), U(1), U(2), U(3), U(6), U(7)
        GSQ, GG, HH, A2 = U(8), U(9), U(10), U(12)

        def wblock(i):
            return tmp[:, 4 * T + (i * P + P // 2):4 * T + (i * P + 3 * P // 2)] if i < 3 else extra[:, 1288:1288 + P]

        wi, wfi = w_in[0], w_ffn_in[0]
        wpa, wpb, wo, wfo = w_branch_a[0], w_branch_b[0], w_out[0], w_ffn_out[0]

        def at_col(i, off):
            return i * P + off if off else (i * 2) * (P // 2)

        def load_hg(i, s):
            return wi, at_col(i, (2 * D, 0, D, 3 * D)[s])

        def load_lru(i, s):
            return wi, i * 2 * P + (4 * D, 5 * D)[s % 2] + (s // 2) * P

        def load_mix(i, s):
            return (wi, wpa, wi, wpb)[s], at_col(i, (6 * D, 0, 7 * D, 0)[s])

        def load_out(i, s):
            return (wo, i * 4 * P + s * P) if s else (wo, (i * 4) * P)

        def load_ffi(i, s):
            off = (s // 2) * P + (s % 2) * DFF
            return (wfi, i * 2 * P + off) if off else (wfi, (i * 2) * P)

        def load_ffo(i, s):
            return wfo[KOFF[s] * P:(KOFF[s] + KSPLIT[s]) * P, :], i * P

        def load_block(eng, s, w, at):
            nk = w.shape[0] // P
            eng.dma_start(raw[:, s, 0:nk], w[:, bass.ds(at, P)].rearrange("(k p) n -> p k n", p=P))\
               .then_inc(E(f"raw_in{s}"), 16)

        block = ctx.enter_context(nc.Block())

        @block.sync
        def _(eng):
            x_t = x_prompt[0].rearrange("(c p) d -> p c d", p=P)
            for ch in range(NCH):
                eng.dma_start(tmp[:, ch * D:(ch + 1) * D], x_t[:, ch, :]).then_inc(E("x_in"), 16)
            eng.dma_start(extra[0:NB, 0:D], x_sample[:, 0, :]).then_inc(E("x_in"), 16)
            eng.dma_start(ident[:], ident_in).then_inc(E("x_in"), 16)
            pv = extra[:, D:D + P]
            rows = ((norm_mix_pre, R_MPRE, 8), (norm_mix_post, R_MPOST, 8), (norm_ffn_pre, R_FPRE, 8),
                    (norm_ffn_post, R_FPOST, 8), (lru_conv_b, R_CB, 8), (lru_log_lambda, R_LL, 8))
            for src, r, n in rows:
                eng.dma_start(pv[r:r + n, :], src[0].rearrange("(n p) -> n p", p=P)).then_inc(E("p_in"), 16)
            eng.dma_start(pv[R_LB:R_LB + 16, :], hg_lb_logits.rearrange("a (n p) -> (a n) p", p=P)).then_inc(E("p_in"), 16)
            eng.dma_start(pv[R_CW:R_CW + 32, :], lru_conv_w[0].rearrange("a (n p) -> (a n) p", p=P)).then_inc(E("p_in"), 16)
            eng.dma_start(pv[R_BA:R_BA + 8, :], lru_b_a[0]).then_inc(E("p_in"), 16)
            eng.dma_start(pv[R_BX:R_BX + 8, :], lru_b_x[0]).then_inc(E("p_in"), 16)
            eng.dma_start(pv[R_ON:R_ON + 1, :], hg_out_norm).then_inc(E("p_in"), 16)
            eng.dma_start(raw[0:3 * NB, 3], state_conv[0].rearrange("b j (n p) -> (b j) n p", p=P)).then_inc(E("s_in"), 16)
            eng.dma_start(raw[0:NB, 2], state_lru[0].rearrange("b (n p) -> b n p", p=P)).then_inc(E("s_in"), 16)
            eng.dma_start(raw[:, 1].rearrange("p k n -> p (k n)")[:, 0:MW], masks_in).then_inc(E("m_in"), 16)
            load_block(eng, 0, *load_hg(0, 0))
            eng.wait_ge(E("m_made"), NLEV)
            load_block(eng, 1, *load_hg(0, 1))
            eng.wait_ge(E("turned"), 2)
            for s in range(2, 4):
                load_block(eng, s, *load_hg(0, s))
            eng.wait_ge(E("xt_ready"), KT)
            eng.dma_start(xt_dram, tmp[:, 8 * T:16 * T]).then_inc(E("xt_out"), 16)

            def load_quad(src, i, g):
                for s in range(4):
                    w, at = src(i, s)
                    eng.wait_ge(E("lo_ready"), 4 * (g - 1) + s + 1)
                    load_block(eng, s, w, at)

            with eng.Fori(1, Q_HG) as i:
                load_quad(load_hg, i, i + G_HG)

            def load_gates(i):
                if isinstance(i, int):
                    eng.wait_ge(E("xt_out"), 16)
                for bb in range(2):
                    n = 2 * i + bb
                    if not isinstance(i, int):
                        eng.wait_ge(E("p_gates"), 2 * i + (bb - 1))
                    for a, w in enumerate((lru_w_a, lru_w_x)):
                        src = w[0, bass.ds(n, 1)].rearrange("n c d -> c (n d)")
                        eng.dma_start(wblock(2 * bb + a), src).then_inc(E(f"gates_in{bb}"), 16)

            load_quad(load_lru, 0, G_LRU)
            load_gates(0)
            with eng.Fori(1, Q_LRU) as i:
                load_quad(load_lru, i, i + G_LRU)
                load_gates(i)
            with eng.Fori(0, Q_MIX) as i:
                load_quad(load_mix, i, i + G_MIX)
            with eng.Fori(0, Q_OUT) as i:
                load_quad(load_out, i, i + G_OUT)
            eng.wait_ge(E("xt_out"), 16)
            eng.wait_ge(E("row_out"), 16 * 5)
            eng.dma_start(tmp[:, 8 * T:16 * T], xt_dram).then_inc(E("xt_back"), 16)
            with eng.Fori(0, Q_FFI) as i:
                load_quad(load_ffi, i, i + G_FFI)
            with eng.Fori(0, Q_FFO) as i:
                load_quad(load_ffo, i, i + G_FFO)
            for ch in range(NCH):
                eng.wait_ge(E("y_ready"), ch + 1)
                eng.dma_start(y_p[0, ch * P:(ch + 1) * P, :], raw[:, ch].rearrange("p k n -> p (k n)"))\
                   .then_inc(E("y_out"), 16)
            eng.wait_ge(E("y_ready"), NCH + 1)
            eng.dma_start(y_s[:, 0, :], extra[0:NB, 0:D]).then_inc(E("y_out"), 16)
            eng.wait_ge(E("y_out"), 16 * (NCH + 1))
            eng.wait_ge(E("xt_back"), 16)

        @block.gpsimd
        def _(eng):
            eng.wait_ge(E("rows_ready"), 1)
            rows = tmp[:, 13 * T:13 * T + 4 * P]
            hrow = rows[0:72, 0:P]
            eng.dma_start(lru_p[0, 0].rearrange("(n p) -> n p", p=P), hrow[0:8, :]).then_inc(E("row_out"), 16)
            eng.dma_start(lru_s[0].rearrange("b (n p) -> (b n) p", p=P), hrow[8:72, :]).then_inc(E("row_out"), 16)
            eng.dma_start(cv_p[0, 0].rearrange("j (n p) -> (j n) p", p=P), rows[0:24, P:2 * P]).then_inc(E("row_out"), 16)
            for k in range(2):
                eng.dma_start(cv_s[0, 4 * k:4 * k + 4].rearrange("b j (n p) -> (b j n) p", p=P),
                              rows[0:96, (2 + k) * P:(3 + k) * P]).then_inc(E("row_out"), 16)
            eng.wait_ge(E("row_out"), 16 * 5)

        @block.scalar
        def _(eng):
            ch = Chain(eng, E("act_order"))
            act = eng.activation

            def prep(u, s, nk=KT):
                g = (u - s) // 4 if isinstance(u, int) else None
                eng.wait_ge(E(f"raw_in{s}"), 16 * (g + 1) if g is not None else u * 4 + (16 - 4 * s))
                if not isinstance(u, int) or u >= 2:
                    eng.wait_ge(E("unit_done"), u - 1)
                act(wh[:, s % 2, 0:nk], raw[:, s, 0:nk], AF.Copy).then_inc(E("hi_ready"), 1)

            def posted(s):
                return E(f"proj_free{s % 2}")

            def inverse_rms(k, x):
                eng.wait_ge(E("n_mm"), k + 1)
                ch.then_wait(act(halves(X(x)), pr[:, :, 0:TH], AF.Ln, bias=eps[:, 0:1], scale=1.0 / D))
                act(X(x), X(x), AF.Exp, scale=-0.5).then_inc(E("n_rs"), 1)

            def stats(src):
                for j in range(KT):
                    if j >= 2:
                        eng.wait_ge(E("n_used"), j - 1)
                    act(X(j % 2), src(j), AF.Square).then_inc(E("n_sq"), 1)
                inverse_rms(0, 2)

            eng.wait_ge(E("turned"), 1)
            act(prm[:], PM[:, 0:NROW], AF.Copy).then_inc(E("prm_ready"), 1)
            eng.wait_ge(E("turned"), 2)
            act(cst[:].rearrange("p n r -> p (n r)"), SA[:, 0:NH * 3 * NB], AF.Copy).then_inc(E("cst_ready"), 1)
            act(hst[:].rearrange("p n r -> p (n r)"), SB[:, 0:NH * NB], AF.Copy).then_inc(E("cst_ready"), 1)
            eng.wait_ge(E("lb_in"), 1)
            act(sp[:, 0:16], sp[:, 0:16], AF.Exp).then_inc(E("lb_exp"), 1)
            eng.wait_ge(E("lb_in"), 2)
            act(sp[:, 16:24], sp[:, 16:24], AF.Exp).then_inc(E("lb_exp"), 1)
            for j in range(KT):
                eng.wait_ge(E("x_turned"), j + 1)
                ch.link(act(U(8 + j, TP), pp[j % 2][:, 0, :], AF.Copy))
                act(U(8 + j, NB, TP), pp[j % 2][:, 1, 0:NB], AF.Copy).then_inc(E("xt_ready"), 1)
            ch.wait()
            eng.wait_ge(E("xt_ready"), KT)
            eng.wait_ge(E("eps_ready"), 2)
            stats(lambda j: U(8 + j))
            prep(0, 0)
            for j in range(KT):
                eng.wait_ge(E("d_norm"), j + 1)
                act(hi_of(XN, j), X(j % 2), AF.Copy).then_inc(E("a_nhi"), 1)

            eng.wait_ge(E("xt_out"), 16)

            def hg_steps(h, prev):
                prep(4 * h + 1, 1)
                if prev:
                    eng.wait_ge(E("unit_done"), 4 * h)
                    eng.wait_ge(E("d_f"), h)
                    act(halves(SIG), proj(1), AF.Sigmoid).then_inc(E("a_sg"), 1)
                prep(4 * h + 2, 2)
                eng.wait_ge(E("unit_done"), 4 * h + 1)
                if prev:
                    sample_rows(h - 1)
                act(halves(VT), proj(0), AF.Copy).then_inc(posted(0), 1)
                if prev:
                    turned_keys(h - 1)
                prep(4 * h + 3, 3)
                eng.wait_ge(E("unit_done"), 4 * h + 2)
                if prev:
                    eng.wait_ge(posted(1), 2 * h)
                act(halves(SIG), proj(1), AF.Sigmoid).then_inc(E("a_sq"), 1)
                if prev:
                    squares(h - 1)
                    state_out(h - 1)
                prep(4 * h + 4, 0)
                eng.wait_ge(E("unit_done"), 4 * h + 3)
                eng.wait_ge(posted(1), 2 * h + 1)
                act(halves(SIG), proj(0), AF.Sigmoid).then_inc(posted(2), 1)
                if prev:
                    roots(h - 1)
                eng.wait_ge(E("p_vt"), h + 1)
                act(VTOK, SA, AF.Copy).then_inc(E("a_vt"), 1)
                if prev:
                    out_high(h - 1)
                    state_in(h)

            def state_in(h):
                eng.wait_ge(E("st_out"), 32 * h)
                eng.dma_start(SS, state_hgrn[0, :, bass.ds(h, 1)].rearrange("b h k v -> k (b h) v"))\
                   .then_inc(E("st_in"), 16)

            def state_out(h):
                eng.wait_ge(E("d_kv"), h + 1)
                eng.dma_start(hg_p[0, 0, bass.ds(h, 1)].rearrange("h k v -> k (h v)"), SCH[:, 3 * P:4 * P])\
                   .then_inc(E("st_out"), 16)
                eng.wait_ge(E("d_half"), 2 * h + 2)
                eng.dma_start(hg_s[0, :, bass.ds(h, 1)].rearrange("b h k v -> k (b h) v"), SS)\
                   .then_inc(E("st_out"), 16)

            def sample_rows(h):
                eng.wait_ge(E("p_st"), h + 1)
                act(STOK, PM[0:NB, 0:2 * P], AF.Copy).then_inc(E("a_st"), 1)

            def turned_keys(h):
                eng.wait_ge(E("p_kst"), h + 1)
                act(KTOK, SB, AF.Copy).then_inc(E("a_kst"), 1)

            def squares(h):
                eng.wait_ge(E("p_os"), h + 1)
                eng.wait_ge(E("p_so"), h + 1)
                ch.link(act(SQ[:, 0:TP], PO, AF.Square))
                act(SQ[:, TP:T], PM[:, 0:NB], AF.Square).then_inc(E("a_square"), 1)

            def roots(h):
                eng.wait_ge(E("p_ones"), h + 1)
                ch.link(act(SQ[:, 0:TP], SB, AF.Ln, bias=eps[:, 0:1], scale=1.0 / P))
                act(SQ[:, TP:T], PM[:, NB:2 * NB], AF.Ln, bias=eps[:, 0:1], scale=1.0 / P).then_inc(E("a_ln"), 1)
                ch.wait()
                eng.wait_ge(E("a_ln"), h + 1)
                act(SQ, SQ, AF.Exp, scale=-0.5).then_inc(E("a_rs"), 1)

            def out_high(h):
                eng.wait_ge(E("d_o"), h + 1)
                act(hi_of(OA, h), O1, AF.Copy).then_inc(E("a_ohi"), 1)

            hg_steps(0, False)
            eng.dma_start(SS, state_hgrn[0, :, 0].rearrange("b k v -> k b v")).then_inc(E("st_in"), 16)
            with eng.Fori(1, NH) as h:
                ch.begin(h - 1, 2)
                hg_steps(h, True)
                ch.end(NH - 1)

            def squares_of_ly(n):
                eng.wait_ge(E("unit_done"), n * 2 + 4 * G_LRU + 2)
                eng.wait_ge(posted(1), n + 2 * G_LRU)
                act(halves(GSQ), proj(1), AF.Square, scale=0.044715 ** 0.5).then_inc(E("a_gsq"), 1)

            def branch_high(n):
                eng.wait_ge(E("d_gh"), n + 1)
                act(hi_of(GB, n), GG, AF.Copy).then_inc(E("a_ghi"), 1)

            def cn(a, n):
                return c4[:, a + n:a + n + 1] if isinstance(n, int) else c4[:, bass.ds(n + a, 1)]

            def gelu_tanh(n):
                eng.wait_ge(E("d_u"), n + 1)
                act(GSQ, GSQ, AF.Tanh, scale=0.7978845608028654).then_inc(E("a_th"), 1)

            def gates(n):
                eng.wait_ge(E("p_gates"), n + 1)
                ch.link(act(halves(SR), pr[:, :, 0:TH], AF.Tanh, bias=PRM(n + R_BA), scale=0.5))
                act(halves(SI), pi[:, :, 0:TH], AF.Tanh, bias=PRM(n + R_BX), scale=0.5).then_inc(E("a_si"), 1)
                ch.wait()
                act(AA, SR, AF.Exp, bias=cn(NH, n), scale=cn(NH, n)).then_inc(E("a_a"), 1)
                act(TA, SR, AF.Tanh, bias=cn(0, n), scale=cn(0, n)).then_inc(E("a_t"), 1)

            def multiplier(n):
                eng.wait_ge(E("d_v"), n + 1)
                act(SQT, TA, AF.Sqrt, scale=0.25).then_inc(E("a_sqt"), 1)

            def pre_conv(n, u):
                eng.wait_ge(E("unit_done"), u + 1)
                eng.wait_ge(E("d_xc"), n)
                cs = cst[:, n, :] if isinstance(n, int) else cst[:, bass.ds(n, 1), :].rearrange("p a r -> p (a r)")
                act(XS[:, :, 0:CW - 1], cs.rearrange("p (b j) -> p b j", j=CW - 1), AF.Copy)
                act(halves(XP[:, CW - 1:CW - 1 + T]), proj(0), AF.Copy)
                act(XS[:, :, CW - 1], pp[0][:, 1, TH - NB:TH], AF.Copy).then_inc(posted(0), 1)

            def first_tap(n):
                eng.wait_ge(E("d_m1"), n)
                eng.wait_ge(posted(0), n + 2 * G_LRU + 1)
                act(XF, XP[:, 0:NX - (CW - 1)], AF.Identity, bias=PRM(n + R_CB), scale=PRM(n + R_CW))\
                    .then_inc(E("a_tap"), 1)

            h, u0 = NH - 1, 4 * G_LRU
            prep(u0 + 1, 1)
            eng.wait_ge(E("unit_done"), 4 * NH)
            eng.wait_ge(E("d_f"), NH)
            act(halves(SIG), proj(1), AF.Sigmoid).then_inc(E("a_sg"), 1)
            eng.wait_ge(posted(1), 2 * G_LRU)
            pre_conv(0, u0)
            prep(u0 + 2, 2)
            sample_rows(h)
            turned_keys(h)
            first_tap(0)
            eng.wait_ge(E("p_os"), NH)
            squares_of_ly(0)
            prep(u0 + 3, 3)
            squares(h)
            state_out(h)
            gelu_tanh(0)
            roots(h)
            out_high(h)
            pre_conv(1, u0 + 2)
            prep(u0 + 4, 0)
            gates(0)
            first_tap(1)
            multiplier(0)
            with eng.Fori(1, Q_LRU) as i:
                ch.begin(i - 1, 2)
                u0 = i * 4 + 4 * G_LRU
                for bb in range(2):
                    n = i * 2 + bb
                    squares_of_ly(n - 1)
                    prep(u0 + 2 * bb + 1, 2 * bb + 1)
                    gelu_tanh(n - 1)
                    branch_high(n - 2)
                    gates(n - 1)
                    prep(u0 + 2 * bb + 2, (2 * bb + 2) % 4)
                    pre_conv(n, u0 + 2 * bb)
                    first_tap(n)
                    multiplier(n - 1)
                ch.end(Q_LRU - 1)
            squares_of_ly(NH - 1)
            prep(4 * G_MIX + 1, 1)
            gelu_tanh(NH - 1)
            branch_high(NH - 2)
            gates(NH - 1)
            prep(4 * G_MIX + 2, 2)
            multiplier(NH - 1)
            def branch_gate(j, part):
                eng.wait_ge(E("unit_done"), j * 4 + 4 * G_MIX + 2 * part + 1)
                eng.wait_ge(posted(1), j * 2 + 2 * G_MIX - 1 + part)
                act(halves(U(2 * part)), proj(0), AF.Sigmoid).then_inc(posted(0), 1)

            def mix(j):
                u0 = j * 4 + 4 * G_MIX
                if not isinstance(j, int):
                    prep(u0 + 2, 2)
                    branch_gate(j, 0)
                prep(u0 + 3, 3)
                prep(u0 + 4, 0)
                branch_gate(j, 1)
                prep(u0 + 5, 1)
                eng.wait_ge(E("d_mb"), j + 1)
                act(hi_of(MG, j), U(3), AF.Copy).then_inc(E("a_mhi"), 1)

            eng.wait_ge(E("a_t"), NH)
            eng.wait_ge(E("a_a"), NH)
            branch_gate(0, 0)
            branch_high(NH - 1)
            eng.wait_ge(E("d_hl"), NH)
            mix(0)
            with eng.Fori(1, Q_MIX) as j:
                mix(j)

            eng.wait_ge(E("d_mlo"), KT)
            for i in range(Q_OUT):
                for s in range(4):
                    u = i * 4 + 4 * G_OUT + s
                    eng.wait_ge(E("unit_done"), u + 1)
                    eng.wait_ge(E("d_acc"), i * 4 + s - 1 if s else i * 4)
                    act(halves(X(s % 2)), proj(s % 2), AF.Square).then_inc(E("a_osq"), 1)
                    act(halves(U(4 * i + s)), proj(s % 2), AF.Copy,
                        scale=PRM(i * 4 + (R_MPOST + s))).then_inc(posted(s), 1)
                    prep(u + 2, (s + 2) % 4)
            inverse_rms(1, 0)
            for j in range(KT):
                eng.wait_ge(E("d_x1"), j + 1)
                act(hi_of(HN, j), U(j), AF.Copy, scale=PRM(R_FPRE + j)).then_inc(E("a_nhi"), 1)
                act(U(8 + j), U(j), AF.Square).then_inc(E("n_sq"), 1)
            inverse_rms(2, 0)

            def ffi(i):
                u0 = i * 4 + 4 * G_FFI
                for jj in range(2):
                    j = i * 2 + jj
                    prep(u0 + 2 * jj + 2, (2 * jj + 2) % 4)
                    eng.wait_ge(E("d_slr"), j)
                    eng.wait_ge(posted(0), j + 2 * G_FFI + 1)
                    act(U(9), U(8), AF.Sigmoid).then_inc(E("a_sgate"), 1)
                    prep(u0 + 2 * jj + 3, (2 * jj + 3) % 4)
                    eng.wait_ge(posted(1), j + 2 * G_FFI + 1)
                    act(hi_of(HD, j), U(11), AF.Copy).then_inc(E("a_hhi"), 1)

            ffi(0)
            with eng.Fori(1, Q_FFI) as i:
                ffi(i)

            def ffo(i, last):
                for jj in range(2):
                    j = i * 2 + jj
                    for s in range(4):
                        u = i * 8 + 4 * G_FFO + 4 * jj + s
                        if not (last and jj == 1 and s >= 2):
                            eng.wait_ge(E("unit_done"), u + 1)
                            prep(u + 2, (s + 2) % 4, KSPLIT[(s + 2) % 4])
                    eng.wait_ge(E("unit_done"), u + 1)
                    if isinstance(i, int) and j == 0:
                        eng.wait_ge(E("d_hlo"), FT)
                    eng.wait_ge(E("d_acc"), j + (KT - 1))
                    act(halves(X(1 + jj)), proj(jj), AF.Square).then_inc(E("a_osq"), 1)
                    act(halves(U(8 + j) if isinstance(i, int) else tmp[:, bass.ds(j * T + 8 * T, T)]), proj(jj), AF.Copy,
                        scale=PRM(j + R_FPOST)).then_inc(posted(jj), 1)

            ffo(0, False)
            with eng.Fori(1, KT // 2 - 1) as i:
                ffo(i, False)
            ffo(KT // 2 - 1, True)
            inverse_rms(3, 1)
            for cch in range(NCH):
                eng.wait_ge(E("y_turned"), cch + 1)
                act(raw[:, cch].rearrange("p (a k) n -> p a (k n)", a=2), pp[cch % 2][:, :, :], AF.Copy)\
                    .then_inc(E("y_ready"), 1)
            eng.wait_ge(E("y_turned"), NCH + 1)
            act(extra[0:NB, 0:D].rearrange("p (a k) -> p a k", a=2), pp[0][0:NB, :, :], AF.Copy).then_inc(E("y_ready"), 1)

        @block.vector
        def _(eng):
            ch = Chain(eng, E("dve_order"))
            tt, ts, stt, cp = eng.tensor_tensor, eng.tensor_scalar, eng.scalar_tensor_tensor, eng.tensor_copy

            def posted(s):
                return E(f"proj_free{s % 2}")

            def prep(u, s, nk=KT):
                eng.wait_ge(E("hi_ready"), u + 1)
                tt(wl[:, s % 2, 0:nk], raw[:, s, 0:nk], wh[:, s % 2, 0:nk].bitcast(F32), SUB).then_inc(E("lo_ready"), 1)

            def add_square(n, x, acc, j):
                eng.wait_ge(E("a_osq"), n + 1)
                if isinstance(j, int) and j == 0:
                    cp(X(acc), X(x)).then_inc(E("d_acc"), 1)
                else:
                    eng.wait_ge(E("d_acc"), n)
                    tt(X(acc), X(acc), X(x), ADD).then_inc(E("d_acc"), 1)

            def normed(src, gain, reg):
                for j in range(KT):
                    n = j
                    if j >= 2:
                        eng.wait_ge(E("a_nhi"), n - 1)
                        eng.wait_ge(E("d_nlo"), n - 1)
                    stt(X(j % 2), src(j), PRM(gain + j), X(2), MUL, MUL).then_inc(E("d_norm"), 1)
                    eng.wait_ge(E("a_nhi"), n + 1)
                    tt(lo_of(reg, j), X(j % 2), hi_of(reg, j).bitcast(F32), SUB).then_inc(E("d_nlo"), 1)

            eng.memset(ones[:], 1.0).then_inc(E("eps_ready"), 1)
            eng.memset(eps[:], EPS).then_inc(E("eps_ready"), 1)
            eng.wait_ge(E("m_in"), 16)
            for i in range(NLEV):
                n = P if i == 0 else P // 2
                at = 0 if i == 0 else P + (i - 1) * n
                src = raw[:, 1].rearrange("p k n -> p (k n)")[:, at:at + n].unsqueeze(1).to_broadcast([P, NCH, n])
                cp(mask(i).rearrange("p (c n) -> p c n", c=NCH), src).then_inc(E("m_made"), 1)
            eng.wait_ge(E("prm_ready"), 1)
            L0, L1 = prm[:, R_LB:R_LB + 8], prm[:, R_LB + 8:R_LB + 16]
            ll = prm[:, R_LL:R_LL + 8]
            mx = sp[:, 24:32]
            ch.then_wait(tt(mx, L0, L1, ALU.max))
            ch.link(tt(sp[:, 0:8], L0, mx, SUB))
            tt(sp[:, 8:16], L1, mx, SUB).then_inc(E("lb_in"), 1)
            ch.wait()
            ch.then_wait(ts(sp[:, 16:24], ll, -1.0, None, MUL))
            tt(sp[:, 16:24], sp[:, 16:24], ll, ALU.min).then_inc(E("lb_in"), 1)
            eng.wait_ge(E("lb_exp"), 1)
            ch.then_wait(tt(mx, sp[:, 0:8], sp[:, 8:16], ADD))
            ch.then_wait(eng.reciprocal(mx, mx))
            ch.link(tt(lb[:, 0:8], sp[:, 0:8], mx, MUL))
            ch.wait()
            ch.then_wait(ts(lb[:, 8:16], lb[:, 0:8], -1.0, 1.0, MUL, ADD))
            eng.wait_ge(E("lb_exp"), 2)
            ee, z, z2, acc = sp[:, 16:24], sp[:, 0:8], sp[:, 8:16], sp[:, 24:32]
            ch.then_wait(ts(z, ee, 2.0, None, ADD))
            ch.then_wait(eng.reciprocal(z, z))
            ch.then_wait(tt(z, z, ee, MUL))
            ch.then_wait(tt(z2, z, z, MUL))
            ch.then_wait(ts(acc, z2, 1.0 / 19, 1.0 / 17, MUL, ADD))
            for k in (15, 13, 11, 9, 7, 5, 3, 1):
                ch.then_wait(tt(acc, acc, z2, MUL))
                ch.then_wait(ts(acc, acc, 1.0 / k, None, ADD))
            ch.then_wait(tt(acc, acc, z, MUL))
            ch.then_wait(ts(z, ll, -4.0, 0.0, MUL, ALU.max))
            ch.then_wait(stt(c4[:, 0:NH], acc, 8.0, z, MUL, ADD))
            ch.link(ts(c4[:, NH:2 * NH], c4[:, 0:NH], -1.0, None, MUL))
            ch.link(ts(prm[:, R_BA:R_BX + 8], prm[:, R_BA:R_BX + 8], 0.5, None, MUL))

            eng.wait_ge(E("n_rs"), 1)
            normed(lambda j: U(8 + j), R_MPRE, XN)
            prep(0, 0)
            eng.wait_ge(E("xt_out"), 16)
            ch.link(eng.memset(AT, 0.0))
            ch.link(eng.memset(XP[:, 0:3], 0.0))
            ch.wait()
            eng.wait_ge(E("m_made"), NLEV)

            def cols_of(ap, b):
                return ap.rearrange("p (n two b) -> p n two b", two=2, b=b)

            def level(h, i):
                eng.wait_ge(E("p_L"), h * 8 + i)
                if i == 1:
                    tt(QP[:, 0:TP], QP[:, 0:TP], FF[:, 0:TP], MUL).then_inc(E("d_L"), 1)
                else:
                    b = 1 << (i - 2)
                    n = TP // (2 * b)
                    tb = tot(b).rearrange("p (n two) -> p n two", two=2)
                    q2, k1 = cols_of(QP[:, 0:TP], b)[:, :, 1, :], cols_of(KS[:, 0:TP], b)[:, :, 0, :]
                    if i > 2:
                        ch.wait()
                    eng.wait_ge(E("d_L"), h * 8 + i - 1)
                    eng.wait_ge(E("d_take"), h * 8 + i - 1)
                    ch.link(tt(q2, q2, tb[:, :, 0:1].to_broadcast([P, n, b]), MUL))
                    ch.link(tt(tot(2 * b), tb[:, :, 0], tb[:, :, 1], MUL))
                    tt(k1, k1, tb[:, :, 1:2].to_broadcast([P, n, b]), MUL).then_inc(E("d_L"), 1)
                take(i - 1)

            def take(i):
                bank = SB if i % 2 == 0 else SA
                if i == 0:
                    eng.copy_predicated(AT, mask(0), bank).then_inc(E("d_take"), 1)
                else:
                    hs = 1 << (i - 1)
                    v = "p (n b) -> p n b"
                    eng.copy_predicated(cols_of(AT, hs)[:, :, 1, :], mask(i).rearrange(v, b=hs),
                                        bank[:, 0:TP // 2].rearrange(v, b=hs)).then_inc(E("d_take"), 1)

            def chunk_states(h):
                eng.wait_ge(E("p_kv"), h + 1)
                eng.wait_ge(E("st_out"), h * 32)
                t128 = tot(P)
                ch.wait()
                ch.then_wait(cp(SCH[:, 0:P], SA[:, 0:P]))
                for k in range(1, NCH):
                    o = stt(SCH[:, k * P:(k + 1) * P], SCH[:, (k - 1) * P:k * P], t128[:, k:k + 1],
                            SA[:, k * P:(k + 1) * P], MUL, ADD)
                    if k < NCH - 1:
                        ch.then_wait(o)
                o.then_inc(E("d_kv"), 1)

            def sample_values(h):
                eng.wait_ge(E("a_st"), h + 1)
                vs = STOK[:, P:2 * P].unsqueeze(1).to_broadcast([NB, NB, P])
                dd = ident[0:NB, 0:NB].unsqueeze(2).to_broadcast([NB, NB, P])
                tt(VBD.rearrange("p (b v) -> p b v", b=NB), vs, dd, MUL).then_inc(E("d_vbd"), 1)

            def sample_states(h):
                eng.wait_ge(E("st_in"), h * 16 + 16)
                for k, bank in enumerate((PM, SB)):
                    eng.wait_ge(E("p_outer"), h * 2 + k + 1)
                    for b in range(4):
                        o = stt(SS[:, 4 * k + b, :], SS[:, 4 * k + b, :], FF[:, TP + 4 * k + b:TP + 4 * k + b + 1],
                                bank[:, b * P:(b + 1) * P], MUL, ADD)
                        if b < 3:
                            ch.link(o)
                    o.then_inc(E("d_half"), 1)

            def finish(h):
                eng.wait_ge(E("a_ln"), h + 1)
                eng.wait_ge(E("a_ohi"), h)
                eng.wait_ge(E("d_olo"), h)
                ch.link(stt(O1[:, 0:TP], PO, PRM(R_ON), SOG[:, 0:TP], MUL, MUL))
                stt(O1[:, TP:T], PM[:, 0:NB], PRM(R_ON), SOG[:, TP:T], MUL, MUL).then_inc(E("d_o1"), 1)
                ch.wait()
                eng.wait_ge(E("d_o1"), h + 1)
                eng.wait_ge(E("a_rs"), h + 1)
                tt(O1, O1, SQ, MUL).then_inc(E("d_o"), 1)

            def finish_low(h):
                eng.wait_ge(E("a_ohi"), h + 1)
                tt(lo_of(OA, h), O1, hi_of(OA, h).bitcast(F32), SUB).then_inc(E("d_olo"), 1)

            def out_gate(h):
                eng.wait_ge(E("a_sg"), h + 1)
                tt(halves(SOG), proj(1), halves(SIG), MUL).then_inc(posted(1), 1)

            def hg_steps(h, prev):
                prep(4 * h + 1, 1)
                if prev:
                    level(h - 1, 4)
                    out_gate(h - 1)
                    level(h - 1, 5)
                    level(h - 1, 6)
                    level(h - 1, 7)
                prep(4 * h + 2, 2)
                if prev:
                    level(h - 1, 8)
                    sample_values(h - 1)
                    chunk_states(h - 1)
                prep(4 * h + 3, 3)
                if prev:
                    sample_states(h - 1)
                    eng.wait_ge(E("p_os"), h)
                eng.wait_ge(E("a_sq"), h + 1)
                tt(halves(QP), proj(1), halves(SIG), MUL).then_inc(posted(1), 1)
                prep(4 * h + 4, 0)
                eng.wait_ge(posted(0), 2 * h + 2)
                eng.wait_ge(posted(1), 2 * h + 1)
                if prev:
                    eng.wait_ge(E("p_so"), h)
                ch.link(cp(QS, QP[:, TP:T]))
                lbs = lambda a: lb[:, a:a + 1] if isinstance(a, int) else lb[:, bass.ds(a, 1)]
                ch.then_wait(ts(FF, SIG, lbs(h + NH), lbs(h), MUL, ADD))
                ts(KS, FF, -1.0, 1.0, MUL, ADD).then_inc(E("d_f"), 1)
                eng.wait_ge(E("d_f"), h + 1)
                if prev:
                    finish(h - 1)
                level(h, 1)
                if prev:
                    finish_low(h - 1)
                level(h, 2)
                level(h, 3)

            hg_steps(0, False)
            with eng.Fori(1, NH) as h:
                ch.begin(h - 1, LINKS_HG)
                hg_steps(h, True)
                ch.end(NH - 1)
            def conv(n):
                eng.wait_ge(E("a_tap"), n + 1)
                w = lambda j: PRM(n + (R_CW + 8 * j))
                co = cout[:, 3:27, bass.ds(n, 1)].rearrange("p (b j) n -> p b (j n)", j=CW - 1)
                keep = ((cout[:, 0:3, bass.ds(n, 1)], XP[:, TP:TP + 3].unsqueeze(2)), (co, XS[:, :, 1:CW]))
                for j in range(1, CW):
                    ch.link(stt(XF, XP[:, j:j + NX - (CW - 1)], w(j), XF, MUL, ADD))
                    if j < CW - 1:
                        cp(*keep[j - 1])
                    ch.wait()
                cp(XC[:, TP:T], XF[:, T:T + CW * NB].rearrange("p (b j) -> p b j", j=CW)[:, :, CW - 1])\
                    .then_inc(E("d_xc"), 1)

            def gelu_inner(n):
                eng.wait_ge(E("a_gsq"), n + 1)
                tt_in = halves(GSQ)
                stt(tt_in, tt_in, 1.0, proj(1), ADD, MUL).then_inc(E("d_u"), 1)

            def branch_low(n):
                eng.wait_ge(E("a_ghi"), n + 1)
                tt(lo_of(GB, n), GG, hi_of(GB, n).bitcast(F32), SUB).then_inc(E("d_hl"), 1)

            def gelu(n):
                eng.wait_ge(E("a_th"), n + 1)
                eng.wait_ge(E("d_hl"), n)
                stt(halves(GG), halves(GSQ), 1.0, proj(1), ADD, MUL).then_inc(posted(1), 1)

            def gated(n):
                eng.wait_ge(E("a_si"), n + 1)
                eng.wait_ge(E("d_xc"), n + 1)
                stt(SI, SI, 1.0, XC, ADD, MUL).then_inc(E("d_m1"), 1)
                eng.wait_ge(E("a_a"), n + 1)
                ch.then_wait(tt(A2, AA, AA, MUL))
                eng.wait_ge(E("a_t"), n + 1)
                stt(TA, A2, 1.0, TA, ADD, MUL).then_inc(E("d_v"), 1)

            def recurrence(n):
                eng.wait_ge(E("a_sqt"), n + 1)
                eng.wait_ge(E("d_m1"), n + 1)
                ch.link(tt(SQT[:, 1:T], SQT[:, 1:T], SI[:, 1:T], MUL))
                ch.link(ts(SQT[:, 0:1], SI[:, 0:1], 0.5, None, MUL))
                hs = hst[:, n, :] if isinstance(n, int) else hst[:, bass.ds(n, 1), :].rearrange("p a r -> p (a r)")
                ch.link(tt(HH[:, TP:T], AA[:, TP:T], hs, MUL))
                ch.wait()
                ch.link(eng.tensor_tensor_scan(HH[:, 0:TP], AA[:, 0:TP], SQT[:, 0:TP], 0.0, MUL, ADD))
                ch.then_wait(tt(HH[:, TP:T], HH[:, TP:T], SQT[:, TP:T], ADD))
                stt(GG, GG, 0.5, HH, MUL, MUL).then_inc(E("d_gh"), 1)
                ch.link(cp(hout[:, :, bass.ds(n, 1)], HH[:, TP - 1:T].unsqueeze(2)))

            h, u0 = NH - 1, 4 * G_LRU
            prep(u0 + 1, 1)
            level(h, 4)
            out_gate(h)
            for i in (5, 6, 7):
                level(h, i)
            prep(u0 + 2, 2)
            level(h, 8)
            sample_values(h)
            chunk_states(h)
            conv(0)
            prep(u0 + 3, 3)
            sample_states(h)
            gelu_inner(0)
            gelu(0)
            finish(h)
            finish_low(h)
            prep(u0 + 4, 0)
            eng.wait_ge(E("d_olo"), NH)
            gated(0)
            conv(1)
            with eng.Fori(1, Q_LRU) as i:
                ch.begin(i - 1, LINKS_LRU)
                u0 = i * 4 + 4 * G_LRU
                for bb in range(2):
                    n = i * 2 + bb
                    gelu_inner(n - 1)
                    recurrence(n - 2)
                    prep(u0 + 2 * bb + 1, 2 * bb + 1)
                    branch_low(n - 2)
                    gelu(n - 1)
                    gated(n - 1)
                    prep(u0 + 2 * bb + 2, (2 * bb + 2) % 4)
                    conv(n)
                ch.end(Q_LRU - 1)
            gelu_inner(NH - 1)
            prep(4 * G_MIX + 1, 1)
            recurrence(NH - 2)
            branch_low(NH - 2)
            gelu(NH - 1)
            gated(NH - 1)
            prep(4 * G_MIX + 2, 2)
            recurrence(NH - 1)
            branch_low(NH - 1)
            eng.wait_ge(E("st_out"), 32 * NH)

            eng.wait_ge(E("a_ghi"), NH)
            eng.wait_ge(E("d_hl"), NH)
            def mix(j):
                u0 = j * 4 + 4 * G_MIX
                if not isinstance(j, int):
                    prep(u0 + 2, 2)
                eng.wait_ge(posted(0), j * 2 + 2 * G_MIX + 1)
                eng.wait_ge(E("unit_done"), u0 + 2)
                tt(halves(U(1)), proj(1), halves(U(0)), MUL).then_inc(posted(1), 1)
                prep(u0 + 3, 3)
                prep(u0 + 4, 0)
                eng.wait_ge(posted(0), j * 2 + 2 * G_MIX + 2)
                eng.wait_ge(E("unit_done"), u0 + 4)
                eng.wait_ge(E("d_mlo"), j)
                eng.wait_ge(E("a_mhi"), j)
                tt(halves(U(3)), proj(1), halves(U(2)), MUL).then_inc(posted(1), 1)
                prep(u0 + 5, 1)
                eng.wait_ge(posted(1), j * 2 + 2 * G_MIX + 2)
                tt(U(3), U(3), U(1), ADD).then_inc(E("d_mb"), 1)
                eng.wait_ge(E("a_mhi"), j + 1)
                tt(lo_of(MG, j), U(3), hi_of(MG, j).bitcast(F32), SUB).then_inc(E("d_mlo"), 1)

            mix(0)
            with eng.Fori(1, Q_MIX) as j:
                mix(j)
            rows = tmp[:, 13 * T:13 * T + 4 * P]
            eng.wait_ge(E("p_rows"), 1)
            ch.link(cp(rows[0:72, 0:P], SA[0:72, 0:P]))
            ch.link(cp(rows[0:24, P:2 * P], SA[0:24, P:2 * P]))
            cp(rows[0:96, 2 * P:4 * P], SA[0:96, 2 * P:4 * P]).then_inc(E("rows_ready"), 1)

            for i in range(Q_OUT):
                for s in range(4):
                    add_square(4 * i + s, s % 2, 2, 4 * i + s)
                    prep(i * 4 + 4 * G_OUT + s + 2, (s + 2) % 4)
            eng.wait_ge(E("n_rs"), 2)
            eng.wait_ge(E("xt_back"), 16)
            eng.wait_ge(posted(0), 2 * G_FFI)
            eng.wait_ge(posted(1), 2 * G_FFI)
            def ffn_low(j):
                eng.wait_ge(E("a_nhi"), KT + j + 1)
                stt(lo_of(HN, j), U(j), PRM(R_FPRE + j), hi_of(HN, j).bitcast(F32), MUL, SUB).then_inc(E("d_nlo"), 1)

            for j in range(KT):
                ch.then_wait(tt(U(j), U(j), X(0), MUL))
                tt(U(j), U(j), U(8 + j), ADD).then_inc(E("d_x1"), 1)
                if j:
                    ffn_low(j - 1)
            ffn_low(KT - 1)
            eng.wait_ge(E("n_rs"), 3)

            def ffi(i):
                u0 = i * 4 + 4 * G_FFI
                for jj in range(2):
                    j = i * 2 + jj
                    prep(u0 + 2 * jj + 2, (2 * jj + 2) % 4)
                    eng.wait_ge(E("unit_done"), u0 + 2 * jj + 1)
                    tt(halves(U(8)), proj(0), halves(X(0)), MUL).then_inc(posted(0), 1)
                    eng.wait_ge(E("a_sgate"), j + 1)
                    ch.then_wait(tt(U(10), U(8), U(9), MUL))
                    tt(U(10), U(10), X(0), MUL).then_inc(E("d_slr"), 1)
                    prep(u0 + 2 * jj + 3, (2 * jj + 3) % 4)
                    eng.wait_ge(E("unit_done"), u0 + 2 * jj + 2)
                    eng.wait_ge(E("a_hhi"), j)
                    eng.wait_ge(E("d_hlo"), j)
                    eng.wait_ge(E("d_slr"), j + 1)
                    tt(halves(U(11)), proj(1), halves(U(10)), MUL).then_inc(posted(1), 1)
                    eng.wait_ge(posted(1), j + 2 * G_FFI + 1)
                    eng.wait_ge(E("a_hhi"), j + 1)
                    tt(lo_of(HD, j), U(11), hi_of(HD, j).bitcast(F32), SUB).then_inc(E("d_hlo"), 1)

            ffi(0)
            with eng.Fori(1, Q_FFI) as i:
                ch.begin(i - 1, 2)
                ffi(i)
                ch.end(Q_FFI - 1)

            def ffo(i, last, first=False):
                for jj in range(2):
                    if jj == 0 and not first:
                        add_square(i * 2 + (KT - 1), 2, 0, i * 2 - 1)
                    if jj == 1:
                        add_square(i * 2 + KT, 1, 0, i * 2)
                    for s in range(4):
                        if not (last and jj == 1 and s >= 2):
                            prep(i * 8 + 4 * G_FFO + 4 * jj + s + 2, (s + 2) % 4, KSPLIT[(s + 2) % 4])

            ffo(0, False, first=True)
            with eng.Fori(1, KT // 2 - 1) as i:
                ffo(i, False)
            ffo(KT // 2 - 1, True)
            add_square(2 * KT - 1, 2, 0, KT - 1)
            eng.wait_ge(E("n_rs"), 4)
            eng.wait_ge(posted(0), 2 * G_FFO + KT // 2)
            eng.wait_ge(posted(1), 2 * G_FFO + KT // 2)
            for j in range(KT):
                ch.then_wait(tt(U(8 + j), U(8 + j), X(1), MUL))
                tt(U(8 + j), U(8 + j), U(j), ADD).then_inc(E("d_y"), 1)

        @block.tensor
        def _(eng):
            mm = eng.matmul

            def ktile(s, par, reg, k, start, stop, koff=0):
                xh, xl = acts[:, reg[0] + koff + k], acts[:, reg[1] + koff + k]
                a, b = wh[:, s % 2, k, :], wl[:, s % 2, k, :]
                for n, (w, x) in enumerate(((a, xh), (a, xl), (b, xh))):
                    for hf in range(2):
                        o = mm(pp[par][:, hf, 0:TH], w, x[:, hf * TH:(hf + 1) * TH],
                               start=start and n == 0, stop=stop and n == 2)
                return o

            def unit(u, s, reg, fill=None, koff=0, nk=KT, par=None, free=None, first=True, last=True, ready=None):
                par = s % 2 if par is None else par
                eng.wait_ge(E("lo_ready"), u + 1)
                if free is not None:
                    eng.wait_ge(E(f"proj_free{par}"), free)
                for k in range(nk):
                    if ready:
                        ready(k)
                    o = ktile(s, par, reg, k, first and k == 0, last and k == nk - 1, koff)
                    if k == nk - 1:
                        o.then_inc(E("unit_done"), 1)
                    if fill and k % 2 == 1 and k // 2 in fill:
                        for f in fill[k // 2]:
                            f()

            def sum_up(src, start=True, stop=True):
                for hf in range(2):
                    o = mm(pr[:, hf, 0:TH], ones[:], src[:, hf * TH:(hf + 1) * TH], start=start, stop=stop)
                return o

            def stats(k, src):
                for j in range(KT):
                    eng.wait_ge(E("n_sq"), 8 * k + j + 1)
                    o = sum_up(src(j), start=j == 0, stop=j == KT - 1)
                    if j < KT - 1:
                        o.then_inc(E("n_used"), 1)
                o.then_inc(E("n_mm"), 1)

            eng.wait_ge(E("x_in"), 16 * (NCH + 2))
            eng.wait_ge(E("p_in"), 16 * 11)
            eng.transpose(PM[:, 0:NROW], extra[0:NROW, D:D + P], ident[0:NROW, 0:NROW]).then_inc(E("turned"), 1)
            eng.wait_ge(E("s_in"), 32)
            for n in range(NH):
                eng.transpose(SA[:, n * 24:(n + 1) * 24], raw[0:24, 3, n, :], ident[0:24, 0:24])
                o = eng.transpose(SB[:, n * NB:(n + 1) * NB], raw[0:NB, 2, n, :], ident[0:NB, 0:NB])
            o.then_inc(E("turned"), 1)
            for j in range(KT):
                if j >= 2:
                    eng.wait_ge(E("xt_ready"), j - 1)
                for cch in range(NCH):
                    eng.transpose(pp[j % 2][:, 0, cch * P:(cch + 1) * P],
                                  tmp[:, cch * D + j * P:cch * D + (j + 1) * P], ident[:])
                o = eng.transpose(pp[j % 2][:, 1, 0:NB], extra[0:NB, j * P:(j + 1) * P], ident[0:NB, 0:NB])
                o.then_inc(E("x_turned"), 1)
            eng.wait_ge(E("turned"), 2)
            eng.wait_ge(E("cst_ready"), 2)
            eng.wait_ge(E("eps_ready"), 2)
            stats(0, lambda j: X(j % 2))
            eng.wait_ge(E("d_nlo"), KT)

            def turn_values(h, prev):
                if prev:
                    eng.wait_ge(E("d_kv"), h)
                eng.wait_ge(E("proj_free0"), 2 * h + 1)
                for k in range(NCH):
                    o = eng.transpose(SA[:, k * P:(k + 1) * P], VT[:, k * P:(k + 1) * P], ident[:])
                o.then_inc(E("p_vt"), 1)

            def score(h, i, prev=True):
                if i == 0:
                    eng.wait_ge(E("d_f"), h + 1)
                    if prev:
                        eng.wait_ge(E("a_ln"), h)
                else:
                    eng.wait_ge(E("d_L"), h * 8 + i)
                    if i == 1:
                        eng.wait_ge(E("a_vt"), h + 1)
                    else:
                        eng.wait_ge(E("d_take"), h * 8 + i - 1)
                bank = SB if i % 2 == 0 else SA
                n = P if i == 0 else P // 2
                for k in range(NCH):
                    rhs = QP[:, k * P:(k + 1) * P]
                    if i:
                        rhs = rhs.rearrange("p (n two b) -> p n two b", two=2, b=1 << (i - 1))[:, :, 1, :]
                    o = mm(bank[:, k * n:(k + 1) * n], KS[:, k * P:(k + 1) * P], rhs, start=True, stop=True)
                o.then_inc(E("p_L"), 1)

            def turn_sample(h):
                if not isinstance(h, int) or h > 0:
                    eng.wait_ge(E("d_o1"), h)
                    eng.wait_ge(E("a_ln"), h)
                eng.transpose(PM[0:NB, 0:P], KS[:, TP:T], ident[:])
                eng.transpose(PM[0:NB, P:2 * P], VT[:, TP:T], ident[:]).then_inc(E("p_st"), 1)

            def turn_keys(h):
                eng.wait_ge(E("d_L"), h * 8 + 8)
                eng.wait_ge(E("d_take"), h * 8 + 7)
                for k in range(NCH):
                    o = eng.transpose(SB[:, k * P:(k + 1) * P], KS[:, k * P:(k + 1) * P], ident[:])
                o.then_inc(E("p_kst"), 1)

            def key_values(h):
                eng.wait_ge(E("a_kst"), h + 1)
                eng.wait_ge(E("d_take"), h * 8 + 8)
                for k in range(NCH):
                    o = mm(SA[:, k * P:(k + 1) * P], KTOK[:, k * P:(k + 1) * P], VTOK[:, k * P:(k + 1) * P],
                           start=True, stop=True)
                o.then_inc(E("p_kv"), 1)

            def out_scores(h):
                if not isinstance(h, int) or h > 0:
                    eng.wait_ge(E("d_o1"), h)
                for k in range(NCH):
                    mm(PO[:, k * P:(k + 1) * P], VTOK[:, k * P:(k + 1) * P], AT[:, k * P:(k + 1) * P],
                       start=k == 0, stop=False, skip_group_check=True)

            def out_states(h):
                eng.wait_ge(E("d_kv"), h + 1)
                for k in range(1, NCH):
                    o = mm(PO[:, k * P:(k + 1) * P], SCH[:, (k - 1) * P:k * P], QP[:, k * P:(k + 1) * P],
                           start=False, stop=k == NCH - 1, skip_group_check=True)
                o.then_inc(E("p_os"), 1)

            def outer(h, k):
                eng.wait_ge(E("d_vbd"), h + 1)
                mm((PM, SB)[k], STOK[:, 0:P], VBD[:, k * 512:(k + 1) * 512], start=True, stop=True)\
                    .then_inc(E("p_outer"), 1)

            def sample_out(h):
                eng.wait_ge(E("d_half"), h * 2 + 2)
                for b in range(NB):
                    o = mm(PM[:, b:b + 1], SS[:, b, :], QS[:, b:b + 1], start=True, stop=True)
                o.then_inc(E("p_so"), 1)

            def head_sums(h):
                eng.wait_ge(E("a_square"), h + 1)
                mm(SB, ones[:], SQ[:, 0:TP], start=True, stop=True)
                mm(PM[:, NB:2 * NB], ones[:], SQ[:, TP:T], start=True, stop=True).then_inc(E("p_ones"), 1)

            def hg_steps(h, prev):
                free = (lambda k: 2 * h + k) if prev else (lambda k: None)
                p = h - 1
                unit(4 * h, 0, XN, {k: [lambda k=k: score(p, k + 3)] for k in range(4)} if prev else None, free=free(0))
                unit(4 * h + 1, 1, XN, {0: [lambda: score(p, 7), lambda: turn_sample(p)], 1: [lambda: turn_keys(p)],
                                        2: [lambda: key_values(p)], 3: [lambda: out_scores(p)]} if prev else None, free=free(0))
                unit(4 * h + 2, 2, XN, {0: [lambda: out_states(p), lambda: outer(p, 0)], 1: [lambda: outer(p, 1)],
                                        2: [lambda: sample_out(p)], 3: [lambda: head_sums(p)]} if prev else None, free=2 * h + 1)
                unit(4 * h + 3, 3, XN, {0: [lambda: turn_values(h, prev)], 1: [lambda: score(h, 0, prev)],
                                        2: [lambda: score(h, 1)], 3: [lambda: score(h, 2)]}, free=2 * h + 1)

            hg_steps(0, False)
            with eng.Fori(1, NH) as h:
                hg_steps(h, True)
            def gate_sums(n):
                i, bb = n if isinstance(n, tuple) else divmod(n, 2)
                n = i * 2 + bb
                eng.wait_ge(E("d_xc"), n + 1)
                if isinstance(n, int) and n == 0:
                    eng.wait_ge(E("a_ln"), NH)
                    eng.wait_ge(E("d_o1"), NH)
                else:
                    eng.wait_ge(E("a_si"), n)
                eng.wait_ge(E(f"gates_in{bb}"), i * 32 + 32)
                for a, bank in enumerate((pr, pi)):
                    for hf in range(2):
                        o = mm(bank[:, hf, 0:TH], wblock(2 * bb + a), XC[:, hf * TH:(hf + 1) * TH], start=True, stop=True)
                o.then_inc(E("p_gates"), 1)

            h, u0, v = NH - 1, 4 * G_LRU, 2 * G_LRU
            unit(u0, 0, XN, {k: [lambda k=k: score(h, k + 3)] for k in range(4)}, free=v)
            unit(u0 + 1, 1, XN, {0: [lambda: score(h, 7), lambda: turn_sample(h)], 1: [lambda: turn_keys(h)],
                                 2: [lambda: key_values(h)], 3: [lambda: out_scores(h)]}, free=v)
            unit(u0 + 2, 2, XN, {0: [lambda: out_states(h), lambda: outer(h, 0)], 1: [lambda: outer(h, 1)],
                                 2: [lambda: sample_out(h)], 3: [lambda: head_sums(h)]}, free=v + 1)
            unit(u0 + 3, 3, XN, {2: [lambda: gate_sums(0)]}, free=v + 1)
            with eng.Fori(1, Q_LRU) as i:
                u0, v = i * 4 + 4 * G_LRU, i * 2 + 2 * G_LRU
                unit(u0, 0, XN, {1: [lambda: gate_sums((i - 1, 1))]}, free=v)
                unit(u0 + 1, 1, XN, free=v)
                unit(u0 + 2, 2, XN, {1: [lambda: gate_sums((i, 0))]}, free=v + 1)
                unit(u0 + 3, 3, XN, free=v + 1)
            gate_sums(NH - 1)

            with eng.Fori(0, Q_MIX) as j:
                for s, reg in enumerate((XN, OA, XN, GB)):
                    if s % 2:
                        eng.wait_ge(E("d_hl" if s == 3 else "d_olo"), NH)
                    unit(j * 4 + 4 * G_MIX + s, s, reg, free=j * 2 + 2 * G_MIX + s // 2)
            eng.wait_ge(E("d_hl"), NH)
            hv, cv = hout[:].rearrange("p a n -> p (a n)"), cout[:].rearrange("p a n -> p (a n)")
            eng.transpose(SA[0:72, 0:P], hv, ident[:])
            eng.transpose(SA[0:24, P:2 * P], cv[:, 0:24], ident[:])
            for k in range(2):
                o = eng.transpose(SA[0:96, (2 + k) * P:(3 + k) * P], cv[:, 24 + 96 * k:120 + 96 * k], ident[:])
            o.then_inc(E("p_rows"), 1)
            for i in range(Q_OUT):
                for s in range(4):
                    unit(i * 4 + 4 * G_OUT + s, s, MG, free=i * 2 + 2 * G_OUT + s // 2,
                         ready=(lambda k: eng.wait_ge(E("d_mlo"), k + 1)) if i == s == 0 else None)
            eng.wait_ge(E("d_acc"), KT)
            sum_up(X(2)).then_inc(E("n_mm"), 1)

            def first_pair(reg, u, ready, after):
                for k in range(KT):
                    ready(k)
                    for s in range(2):
                        if k == 0:
                            eng.wait_ge(E("lo_ready"), u + s + 1)
                            eng.wait_ge(E(f"proj_free{s}"), u // 2)
                        o = ktile(s, s, reg, k, k == 0, k == KT - 1)
                        if k == KT - 1:
                            o.then_inc(E("unit_done"), 1)
                    after(k)

            def ffn_ready(k):
                eng.wait_ge(E("d_nlo"), KT + k + 1)

            def ffn_square(k):
                eng.wait_ge(E("n_sq"), KT + k + 1)
                if k == 0:
                    eng.wait_ge(E("n_rs"), 2)
                o = sum_up(U(8 + k), start=k == 0, stop=k == KT - 1)
                if k == KT - 1:
                    o.then_inc(E("n_mm"), 1)

            first_pair(HN, 4 * G_FFI, ffn_ready, ffn_square)
            for s in range(2, 4):
                unit(4 * G_FFI + s, s, HN, free=2 * G_FFI + s // 2)
            with eng.Fori(1, Q_FFI) as i:
                for s in range(4):
                    unit(i * 4 + 4 * G_FFI + s, s, HN, free=i * 2 + 2 * G_FFI + s // 2)

            def ffo(i):
                for jj in range(2):
                    for s in range(4):
                        if isinstance(i, int) and jj == 0:
                            eng.wait_ge(E("d_hlo"), KOFF[s] + KSPLIT[s])
                        unit(i * 8 + 4 * G_FFO + 4 * jj + s, s, HD, koff=KOFF[s], nk=KSPLIT[s], par=jj,
                             free=i + 2 * G_FFO if s == 0 else None, first=s == 0, last=s == 3)

            ffo(0)
            with eng.Fori(1, KT // 2) as i:
                ffo(i)
            eng.wait_ge(E("d_acc"), 2 * KT)
            sum_up(X(0)).then_inc(E("n_mm"), 1)
            for cch in range(NCH + 1):
                eng.wait_ge(E("d_y"), KT)
                if cch >= 2:
                    eng.wait_ge(E("y_ready"), cch - 1)
                m = P if cch < NCH else NB
                for j in range(KT):
                    o = eng.transpose(pp[cch % 2][0:m, j // 4, (j % 4) * P:(j % 4 + 1) * P],
                                      U(8 + j, m, cch * P), ident[:])
                o.then_inc(E("y_turned"), 1)


LINKS_HG, LINKS_LRU = 26, 20


_INS = ["x_prompt", "x_sample", "state_hgrn", "state_lru", "state_conv", "norm_mix_pre", "norm_mix_post",
        "norm_ffn_pre", "norm_ffn_post", "w_in", "hg_lb_logits", "hg_out_norm", "lru_conv_w", "lru_conv_b",
        "lru_w_a", "lru_b_a", "lru_w_x", "lru_b_x", "lru_log_lambda", "w_branch_a", "w_branch_b", "w_out",
        "w_ffn_in", "w_ffn_out"]
_OUTS = [(1, TP, D), (NB, 1, D), (1, 1, NH, P, P), (1, 1, D), (1, 1, CW - 1, D),
         (1, NB, NH, P, P), (1, NB, D), (1, NB, CW - 1, D)]


def _level_masks(np):
    s = np.arange(P)[:, None]
    out = [np.eye(P, dtype=np.float32)]
    for i in range(1, NLEV):
        hs = 1 << (i - 1)
        tc = np.arange(P // 2)[None, :]
        t = tc // hs * 2 * hs + hs + tc % hs
        m = (s // (2 * hs) == t // (2 * hs)) & (s % (2 * hs) < hs)
        out.append(m.astype(np.float32))
    return np.ascontiguousarray(np.concatenate(out, axis=1))


def kernel(**inputs):
    import numpy as np
    import concourse.bacc as bacc
    from concourse import mybir as mb
    from concourse.bass_utils import run_bass_kernel_spmd as run

    nc = bacc.Bacc("TRN2", target_bir_lowering=False, num_devices=1)
    arrays, args = {}, []
    for name in _INS:
        a = np.ascontiguousarray(inputs[name])
        arrays[f"in_{name}"] = a
        args.append(nc.dram_tensor(f"in_{name}", a.shape, mb.dt.from_np(a.dtype), kind="ExternalInput").ap())
    for name, a in (("ident", np.eye(P, dtype=np.float32)), ("masks", _level_masks(np))):
        arrays[f"in_{name}"] = a
        args.append(nc.dram_tensor(f"in_{name}", a.shape, mb.dt.from_np(a.dtype), kind="ExternalInput").ap())
    for i, shape in enumerate(_OUTS):
        args.append(nc.dram_tensor(f"out_{i}", shape, mb.dt.float32, kind="ExternalOutput").ap())
    hybrid_decoder(nc, *args)
    r = run(nc, [arrays], core_ids=[0])
    return tuple(r.results[0][f"out_{i}"] for i in range(len(_OUTS)))
```

```python
from contextlib import ExitStack

import concourse.bass as bass
from concourse import mybir

F32 = mybir.dt.float32
F32R = mybir.dt.float32r
U8 = mybir.dt.uint8
ALU = mybir.AluOpType
AF = mybir.ActivationFunctionType
MUL, ADD, SUB = ALU.mult, ALU.add, ALU.subtract

P = 128
D = 1024
KT = D // P
TP = 512
NB = 8
T = TP + NB
TH = T // 2
NH = 8
NCH = TP // P
NLEV = 8
DFF = 2816
FT = DFF // P
KSPLIT = (6, 6, 5, 5)
KOFF = (0, 6, 12, 17)
CW = 4
EPS = 1e-6

R_MPRE, R_MPOST, R_FPRE, R_FPOST = 0, 8, 16, 24
R_LB, R_CW, R_CB, R_BA, R_BX, R_LL, R_ON = 32, 48, 80, 88, 96, 104, 112
NROW = 113
MW = P + (NLEV - 1) * P // 2

Q_HG, Q_LRU, Q_MIX, Q_OUT, Q_FFI, Q_FFO = NH, NH // 2, KT, 2, FT // 2, KT
G_HG = 0
G_LRU = G_HG + Q_HG
G_MIX = G_LRU + Q_LRU
G_OUT = G_MIX + Q_MIX
G_FFI = G_OUT + Q_OUT
G_FFO = G_FFI + Q_FFI


class Chain:

    def __init__(self, eng, sem):
        self.eng, self.sem, self.base, self.k, self.i, self.per = eng, sem, 0, 0, None, 0

    def begin(self, i, per):
        self.base += self.k
        self.i, self.per, self.k = i, per, 0

    def end(self, n):
        assert self.k == self.per, (self.k, self.per)
        self.base += self.per * n
        self.i, self.k = None, 0

    def link(self, ins):
        ins.then_inc(self.sem, 1)
        self.k += 1

    def wait(self):
        v = self.base + self.k
        self.eng.wait_ge(self.sem, v if self.i is None else self.i * self.per + v)

    def then_wait(self, ins):
        self.link(ins)
        self.wait()


def hybrid_decoder(nc, x_prompt, x_sample, state_hgrn, state_lru, state_conv, norm_mix_pre, norm_mix_post,
                   norm_ffn_pre, norm_ffn_post, w_in, hg_lb_logits, hg_out_norm, lru_conv_w, lru_conv_b,
                   lru_w_a, lru_b_a, lru_w_x, lru_b_x, lru_log_lambda, w_branch_a, w_branch_b, w_out,
                   w_ffn_in, w_ffn_out, ident_in, masks_in, y_p, y_s, hg_p, lru_p, cv_p, hg_s, lru_s, cv_s):
    with ExitStack() as ctx:
        def sb(name, shape, dt=F32):
            return ctx.enter_context(nc.sbuf_tensor(name, shape, dt))

        sems = {}

        def E(name):
            if name not in sems:
                sems[name] = ctx.enter_context(nc.semaphore(name))
            return sems[name]

        raw = sb("raw", [P, 4, KT, P])
        wh = sb("wh", [P, 2, KT, P], F32R)
        wl = sb("wl", [P, 2, KT, P], F32R)
        acts = sb("acts", [P, 64, T], F32R)
        tmp = sb("tmp", [P, 16 * T])
        extra = sb("extra", [P, 3 * T])
        ident = sb("ident", [P, P])
        ones = sb("ones", [P, P])
        masks = sb("masks", [P, TP + (NLEV - 1) * TP // 2], U8)
        prm = sb("prm", [P, NROW])
        lb = sb("lb", [P, 2 * NH])
        c4 = sb("c4", [P, 2 * NH])
        sp = sb("sp", [P, 5 * NH])
        eps = sb("eps", [P, 1])
        rt = sb("rt", [P, 2 * NB])
        stk = sb("stk", [P, 2, 3 * NB], F32R)
        sel = sb("sel", [3 * NB, NB])
        cst = sb("cst", [P, NH, 3 * NB])
        hst = sb("hst", [P, NH, NB])
        hout = sb("hout", [P, 1 + NB, NH])
        cout = sb("cout", [P, 3 * (1 + NB), NH])

        pp = [ctx.enter_context(nc.psum_tensor(f"proj{i}", [P, 2, 512], F32)) for i in range(2)]
        pr = ctx.enter_context(nc.psum_tensor("pr", [P, 2, 512], F32))
        pi = ctx.enter_context(nc.psum_tensor("pi", [P, 2, 512], F32))
        SA, SB, PO, PM = pr[:, 0, :], pr[:, 1, :], pi[:, 0, :], pi[:, 1, :]
        xt_dram = nc.dram_tensor("xt_scratch", (P, KT * T), F32, kind="Internal").ap()

        XN, OA, GB, MG, HN, HD = (0, 8), (16, 24), (32, 40), (48, 56), (0, 8), (16, 16 + FT)

        def U(i, n=T, at=0):
            return tmp[:, i * T + at:i * T + at + n]

        def X(i, n=T, at=0):
            return extra[:, i * T + at:i * T + at + n]

        def halves(ap):
            return ap.rearrange("p (a t) -> p a t", a=2)

        def proj(par):
            return pp[par][:, :, 0:TH]

        def PRM(r):
            return prm[:, r:r + 1] if isinstance(r, int) else prm[:, bass.ds(r, 1)]

        def hi_of(reg, j):
            return acts[:, reg[0] + j, :] if isinstance(j, int) else acts[:, bass.ds(j + reg[0], 1), :].rearrange("p a t -> p (a t)")

        def lo_of(reg, j):
            return acts[:, reg[1] + j, :] if isinstance(j, int) else acts[:, bass.ds(j + reg[1], 1), :].rearrange("p a t -> p (a t)")

        SUMS, ROOTS = rt[:, 0:NB], rt[:, NB:2 * NB]
        PROWS, HROWS, CROWS = extra[:, D:D + P], extra[0:NB * NH, D + P:D + 2 * P], \
            [extra[0:96, D + (2 + k) * P:D + (3 + k) * P] for k in range(2)]
        DIAG, DIAGS = raw[:, 2, 0:NCH, :], raw[0:NB, 2, NCH, 0:NB]
        ALLX = tmp[:, 8 * T:16 * T].rearrange("p (j t) -> p j t", t=T)

        FF, QP, KS, VT, SIG, SOG, AT = U(0), U(1), U(2), U(3), U(5), U(6), U(7, TP)
        TT = U(11, TP)
        VTOK, KTOK, SQ, O1 = U(8, TP), U(9, TP), U(10), U(12)
        SCH = U(13, TP)
        SS = tmp[:, 14 * T:14 * T + NB * P].rearrange("p (b v) -> p b v", b=NB)
        NS = 3 * NB
        spare = acts[:, 60:64].rearrange("p a t -> p (a t)")
        VBD, STOK = spare[0:NS, 0:NB * P], spare[0:NS, NB * P:(NB + 2) * P]
        QS = extra[:, 1280:1280 + NB]
        TOFF = {}
        at = 0
        for b in (2, 4, 8, 16, 32, 64, 128):
            TOFF[b] = at
            at += TP // b

        def tot(b):
            return FF[:, 0:TP] if b == 1 else TT[:, TOFF[b]:TOFF[b] + TP // b]

        def mask(i):
            return masks[:, 0:TP] if i == 0 else masks[:, TP + (i - 1) * TP // 2:TP + i * TP // 2]

        NX = CW - 1 + T + CW * NB
        XP = tmp[:, 6 * T - NX:6 * T]
        XS = XP[:, CW - 1 + T:NX].rearrange("p (b j) -> p b j", j=CW)
        XF = tmp[:, 3 * T:3 * T + NX - (CW - 1)]
        SR, SI, AA, XC, TA, SQT = U(0), U(1), U(2), U(3), U(6), U(7)
        GSQ, GG, HH, A2 = U(8), U(9), U(10), U(12)

        def wblock(i):
            return tmp[:, 4 * T + (i * P + P // 2):4 * T + (i * P + 3 * P // 2)] if i < 3 else extra[:, 1288:1288 + P]

        X1TOK = tmp[:, 8 * T:16 * T].rearrange("p (j t) -> p j t", t=T)
        X1S, YS = cst[:, :, 0:NB], cst[:, :, NB:2 * NB]
        FOUT = tmp[:, 0:8 * T].rearrange("p (j t) -> p j t", t=T)
        YC = (pr, pi, pp[0], pp[1])

        wi, wfi = w_in[0], w_ffn_in[0]
        wpa, wpb, wo, wfo = w_branch_a[0], w_branch_b[0], w_out[0], w_ffn_out[0]

        def at_col(i, off):
            return i * P + off if off else (i * 2) * (P // 2)

        def load_hg(i, s):
            return wi, at_col(i, (2 * D, 0, D, 3 * D)[s])

        def load_lru(i, s):
            return wi, i * 2 * P + (4 * D, 5 * D)[s % 2] + (s // 2) * P

        def load_mix(i, s):
            return (wi, wpa, wi, wpb)[s], at_col(i, (6 * D, 0, 7 * D, 0)[s])

        def load_out(i, s):
            return (wo, i * 4 * P + s * P) if s else (wo, (i * 4) * P)

        def load_ffi(i, s):
            off = (s // 2) * P + (s % 2) * DFF
            return (wfi, i * 2 * P + off) if off else (wfi, (i * 2) * P)

        def load_ffo(i, s):
            return wfo[KOFF[s] * P:(KOFF[s] + KSPLIT[s]) * P, :], i * P

        def load_block(eng, s, w, at):
            nk = w.shape[0] // P
            eng.dma_start(raw[:, s, 0:nk], w[:, bass.ds(at, P)].rearrange("(k p) n -> p k n", p=P))\
               .then_inc(E(f"raw_in{s}"), 16)

        block = ctx.enter_context(nc.Block())

        @block.sync
        def _(eng):
            x_t = x_prompt[0].rearrange("(c p) d -> p c d", p=P)
            for ch in range(NCH):
                eng.dma_start(tmp[:, ch * D:(ch + 1) * D], x_t[:, ch, :]).then_inc(E(f"x_in{ch}"), 16)
            eng.dma_start(extra[0:NB, 0:D], x_sample[:, 0, :]).then_inc(E("xs_in"), 16)
            eng.dma_start(ident[:], ident_in).then_inc(E("id_in"), 16)
            load_block(eng, 0, *load_hg(0, 0))
            load_block(eng, 1, *load_hg(0, 1))
            pv = PROWS
            rows = ((norm_mix_pre, R_MPRE, 8), (norm_mix_post, R_MPOST, 8), (norm_ffn_pre, R_FPRE, 8),
                    (norm_ffn_post, R_FPOST, 8), (lru_conv_b, R_CB, 8), (lru_log_lambda, R_LL, 8))
            for src, r, n in rows:
                eng.dma_start(pv[r:r + n, :], src[0].rearrange("(n p) -> n p", p=P)).then_inc(E("p_in"), 16)
            eng.dma_start(pv[R_LB:R_LB + 16, :], hg_lb_logits.rearrange("a (n p) -> (a n) p", p=P)).then_inc(E("p_in"), 16)
            eng.dma_start(pv[R_CW:R_CW + 32, :], lru_conv_w[0].rearrange("a (n p) -> (a n) p", p=P)).then_inc(E("p_in"), 16)
            eng.dma_start(pv[R_BA:R_BA + 8, :], lru_b_a[0]).then_inc(E("p_in"), 16)
            eng.dma_start(pv[R_BX:R_BX + 8, :], lru_b_x[0]).then_inc(E("p_in"), 16)
            eng.dma_start(pv[R_ON:R_ON + 1, :], hg_out_norm).then_inc(E("p_in"), 16)
            eng.dma_start(HROWS, state_lru[0].rearrange("b (n p) -> (b n) p", p=P)).then_inc(E("p_in"), 16)
            for k in range(2):
                eng.dma_start(CROWS[k], state_conv[0, 4 * k:4 * k + 4].rearrange("b j (n p) -> (b j n) p", p=P))\
                   .then_inc(E("p_in"), 16)
            eng.dma_start(raw[:, 3].rearrange("p k n -> p (k n)")[:, 0:MW], masks_in).then_inc(E("m_in"), 16)
            eng.wait_ge(E("r_spread"), 1)
            load_block(eng, 2, *load_hg(0, 2))
            eng.wait_ge(E("m_made"), NLEV)
            load_block(eng, 3, *load_hg(0, 3))
            eng.wait_ge(E("xt_ready"), KT)
            eng.wait_ge(E("xs_ready"), 1)
            eng.dma_start(xt_dram, tmp[:, 8 * T:16 * T]).then_inc(E("xt_out"), 16)

            def load_quad(src, i, g):
                for s in range(4):
                    w, at = src(i, s)
                    eng.wait_ge(E("lo_ready"), 4 * (g - 1) + s + 1)
                    load_block(eng, s, w, at)

            with eng.Fori(1, Q_HG) as i:
                load_quad(load_hg, i, i + G_HG)

            def load_gates(i):
                if isinstance(i, int):
                    eng.wait_ge(E("xt_out"), 16)
                for bb in range(2):
                    n = 2 * i + bb
                    if not isinstance(i, int):
                        eng.wait_ge(E("p_gates"), 2 * i + (bb - 1))
                    for a, w in enumerate((lru_w_a, lru_w_x)):
                        src = w[0, bass.ds(n, 1)].rearrange("n c d -> c (n d)")
                        eng.dma_start(wblock(2 * bb + a), src).then_inc(E(f"gates_in{bb}"), 16)

            load_quad(load_lru, 0, G_LRU)
            load_gates(0)
            with eng.Fori(1, Q_LRU) as i:
                load_quad(load_lru, i, i + G_LRU)
                load_gates(i)
            with eng.Fori(0, Q_MIX) as i:
                load_quad(load_mix, i, i + G_MIX)
            with eng.Fori(0, Q_OUT) as i:
                load_quad(load_out, i, i + G_OUT)
            eng.wait_ge(E("xt_out"), 16)
            eng.wait_ge(E("row_out"), 16 * 5)
            eng.dma_start(tmp[:, 8 * T:16 * T], xt_dram).then_inc(E("xt_back"), 16)
            with eng.Fori(0, Q_FFI) as i:
                load_quad(load_ffi, i, i + G_FFI)
            with eng.Fori(0, Q_FFO) as i:
                load_quad(load_ffo, i, i + G_FFO)
            for c in range(NCH):
                eng.wait_ge(E("d_y"), c + 1)
                eng.dma_start(y_p[0, c * P:(c + 1) * P, :], raw[:, c].rearrange("p k n -> p (k n)"))\
                   .then_inc(E("y_out"), 16)
            eng.wait_ge(E("ys_ready"), 1)
            eng.dma_start(y_s[:, 0, :], extra[0:NB, 0:D]).then_inc(E("y_out"), 16)
            eng.wait_ge(E("y_out"), 16 * (NCH + 1))
            eng.wait_ge(E("xt_back"), 16)

        @block.gpsimd
        def _(eng):
            eng.wait_ge(E("rows_ready"), 1)
            rows = tmp[:, 13 * T:13 * T + 4 * P]
            hrow = rows[0:72, 0:P]
            eng.dma_start(lru_p[0, 0].rearrange("(n p) -> n p", p=P), hrow[0:8, :]).then_inc(E("row_out"), 16)
            eng.dma_start(lru_s[0].rearrange("b (n p) -> (b n) p", p=P), hrow[8:72, :]).then_inc(E("row_out"), 16)
            eng.dma_start(cv_p[0, 0].rearrange("j (n p) -> (j n) p", p=P), rows[0:24, P:2 * P]).then_inc(E("row_out"), 16)
            for k in range(2):
                eng.dma_start(cv_s[0, 4 * k:4 * k + 4].rearrange("b j (n p) -> (b j n) p", p=P),
                              rows[0:96, (2 + k) * P:(3 + k) * P]).then_inc(E("row_out"), 16)
            eng.wait_ge(E("row_out"), 16 * 5)

        @block.scalar
        def _(eng):
            ch = Chain(eng, E("act_order"))
            act = eng.activation

            def prep(u, s, nk=KT):
                g = (u - s) // 4 if isinstance(u, int) else None
                eng.wait_ge(E(f"raw_in{s}"), 16 * (g + 1) if g is not None else u * 4 + (16 - 4 * s))
                if not isinstance(u, int) or u >= 2:
                    eng.wait_ge(E("unit_done"), u - 1)
                act(wh[:, s % 2, 0:nk], raw[:, s, 0:nk], AF.Copy).then_inc(E("hi_ready"), 1)

            def posted(s):
                return E(f"proj_free{s % 2}")

            def inverse_rms(k, x):
                eng.wait_ge(E("n_mm"), k + 1)
                ch.then_wait(act(halves(X(x)), pr[:, :, 0:TH], AF.Ln, bias=eps[:, 0:1], scale=1.0 / D))
                act(X(x), X(x), AF.Exp, scale=-0.5).then_inc(E("n_rs"), 1)

            for c in range(NCH):
                eng.wait_ge(E(f"x_in{c}"), 16)
                ch.link(act(acts[:, 48 + 2 * c:50 + 2 * c].rearrange("p a t -> p (a t)")[:, 0:D], tmp[:, c * D:(c + 1) * D],
                            AF.Square, accum_out=SUMS[:, c:c + 1]))
            eng.wait_ge(E("xs_in"), 16)
            ch.then_wait(act(acts[0:NB, 56:58].rearrange("p a t -> p (a t)")[:, 0:D], extra[0:NB, 0:D], AF.Square,
                             accum_out=SUMS[0:NB, NCH:NCH + 1]))
            eng.wait_ge(E("eps_ready"), 2)
            act(ROOTS[:, 0:NCH], SUMS[:, 0:NCH], AF.Sqrt, bias=eps[:, 0:1], scale=1.0 / D).then_inc(E("a_root"), 1)
            act(ROOTS[0:NB, NCH:NCH + 1], SUMS[0:NB, NCH:NCH + 1], AF.Sqrt, bias=eps[0:NB, 0:1], scale=1.0 / D)\
                .then_inc(E("a_root"), 1)
            prep(0, 0)
            eng.wait_ge(E("xs_turned"), 1)
            act(ALLX[:, :, TP:T], PO[:, 0:KT * NB].rearrange("p (j b) -> p j b", j=KT), AF.Copy).then_inc(E("xs_ready"), 1)
            eng.wait_ge(E("turned"), 1)
            act(prm[:], PM[:, 0:NROW], AF.Copy).then_inc(E("prm_ready"), 1)
            act(hst[:].rearrange("p n b -> p b n"), PM[:, P:P + NB * NH].rearrange("p (b n) -> p b n", b=NB), AF.Copy)
            for k in range(2):
                n = 4 * (CW - 1)
                act(cst[:, :, k * n:(k + 1) * n].rearrange("p n r -> p r n"),
                    PM[:, 2 * P + k * 96:2 * P + (k + 1) * 96].rearrange("p (r n) -> p r n", n=NH), AF.Copy)\
                    .then_inc(E("cst_ready"), 1)
            prep(1, 1)

            def high(j):
                eng.wait_ge(E("d_norm"), j + 1)
                act(hi_of(XN, j), X(j % 2), AF.Copy).then_inc(E("a_nhi"), 1)

            for j in range(KT):
                eng.wait_ge(E("x_turned"), j + 1)
                act(U(8 + j, TP), (SA, SB)[j % 2], AF.Copy).then_inc(E("xt_ready"), 1)
                if j == 1:
                    eng.wait_ge(E("r_spread"), 1)
                    act(X(2, TP), PO, AF.Copy)
                    act(X(2, NB, TP), PM[:, 0:NB], AF.Copy).then_inc(E("r_ready"), 1)
                if j >= 1:
                    high(j - 1)
            high(KT - 1)
            def exponentials():
                eng.wait_ge(E("lb_in"), 1)
                act(sp[:, 0:16], sp[:, 0:16], AF.Exp).then_inc(E("lb_exp"), 1)
                eng.wait_ge(E("lb_in"), 2)
                act(sp[:, 16:24], sp[:, 16:24], AF.Exp).then_inc(E("lb_exp"), 1)

            def hg_steps(h, prev):
                if prev:
                    prep(4 * h + 1, 1)
                    eng.wait_ge(E("unit_done"), 4 * h)
                    eng.wait_ge(E("d_f"), h)
                    act(halves(SIG), proj(1), AF.Sigmoid).then_inc(E("a_sg"), 1)
                if not prev:
                    exponentials()
                prep(4 * h + 2, 2)
                eng.wait_ge(E("unit_done"), 4 * h + 1)
                if prev:
                    sample_rows(h - 1)
                act(halves(VT), proj(0), AF.Copy).then_inc(posted(0), 1)
                if prev:
                    turned_keys(h - 1)
                prep(4 * h + 3, 3)
                eng.wait_ge(E("unit_done"), 4 * h + 2)
                if prev:
                    eng.wait_ge(posted(1), 2 * h)
                act(halves(SIG), proj(1), AF.Sigmoid).then_inc(E("a_sq"), 1)
                if prev:
                    squares(h - 1)
                    state_out(h - 1)
                prep(4 * h + 4, 0)
                eng.wait_ge(E("unit_done"), 4 * h + 3)
                eng.wait_ge(posted(1), 2 * h + 1)
                act(halves(SIG), proj(0), AF.Sigmoid).then_inc(posted(2), 1)
                if prev:
                    roots(h - 1)
                eng.wait_ge(E("p_vt"), h + 1)
                if not prev:
                    eng.wait_ge(E("xt_out"), 16)
                act(VTOK, SA, AF.Copy).then_inc(E("a_vt"), 1)
                if prev:
                    out_high(h - 1)
                    state_in(h)

            def state_in(h):
                eng.wait_ge(E("st_out"), 32 * h)
                eng.dma_start(SS, state_hgrn[0, :, bass.ds(h, 1)].rearrange("b h k v -> k (b h) v"))\
                   .then_inc(E("st_in"), 16)

            def state_out(h):
                eng.wait_ge(E("d_kv"), h + 1)
                eng.dma_start(hg_p[0, 0, bass.ds(h, 1)].rearrange("h k v -> k (h v)"), SCH[:, 3 * P:4 * P])\
                   .then_inc(E("st_out"), 16)
                eng.wait_ge(E("d_half"), 2 * h + 2)
                eng.dma_start(hg_s[0, :, bass.ds(h, 1)].rearrange("b h k v -> k (b h) v"), SS)\
                   .then_inc(E("st_out"), 16)

            def sample_rows(h):
                eng.wait_ge(E("p_st"), h + 1)
                act(STOK, PM[0:NS, 0:2 * P], AF.Copy).then_inc(E("a_st"), 1)

            def turned_keys(h):
                eng.wait_ge(E("p_kst"), h + 1)
                act(KTOK, SB, AF.Copy).then_inc(E("a_kst"), 1)

            def squares(h):
                eng.wait_ge(E("p_os"), h + 1)
                eng.wait_ge(E("p_so"), h + 1)
                ch.link(act(SQ[:, 0:TP], PO, AF.Square))
                act(SQ[:, TP:T], PM[:, 0:NB], AF.Square).then_inc(E("a_square"), 1)

            def roots(h):
                eng.wait_ge(E("p_ones"), h + 1)
                ch.link(act(SQ[:, 0:TP], SB, AF.Ln, bias=eps[:, 0:1], scale=1.0 / P))
                act(SQ[:, TP:T], PM[:, NB:2 * NB], AF.Ln, bias=eps[:, 0:1], scale=1.0 / P).then_inc(E("a_ln"), 1)
                ch.wait()
                eng.wait_ge(E("a_ln"), h + 1)
                act(SQ, SQ, AF.Exp, scale=-0.5).then_inc(E("a_rs"), 1)

            def out_high(h):
                eng.wait_ge(E("d_o"), h + 1)
                act(hi_of(OA, h), O1, AF.Copy).then_inc(E("a_ohi"), 1)

            hg_steps(0, False)
            eng.dma_start(SS, state_hgrn[0, :, 0].rearrange("b k v -> k b v")).then_inc(E("st_in"), 16)
            with eng.Fori(1, NH) as h:
                ch.begin(h - 1, 2)
                hg_steps(h, True)
                ch.end(NH - 1)

            def squares_of_ly(n):
                eng.wait_ge(E("unit_done"), n * 2 + 4 * G_LRU + 2)
                eng.wait_ge(posted(1), n + 2 * G_LRU)
                act(halves(GSQ), proj(1), AF.Square, scale=0.044715 ** 0.5).then_inc(E("a_gsq"), 1)

            def branch_high(n):
                eng.wait_ge(E("d_gh"), n + 1)
                act(hi_of(GB, n), GG, AF.Copy).then_inc(E("a_ghi"), 1)

            def cn(a, n):
                return c4[:, a + n:a + n + 1] if isinstance(n, int) else c4[:, bass.ds(n + a, 1)]

            def gelu_tanh(n):
                eng.wait_ge(E("d_u"), n + 1)
                act(GSQ, GSQ, AF.Tanh, scale=0.7978845608028654).then_inc(E("a_th"), 1)

            def gates(n):
                eng.wait_ge(E("p_gates"), n + 1)
                ch.link(act(halves(SR), pr[:, :, 0:TH], AF.Tanh, bias=PRM(n + R_BA), scale=0.5))
                act(halves(SI), pi[:, :, 0:TH], AF.Tanh, bias=PRM(n + R_BX), scale=0.5).then_inc(E("a_si"), 1)
                ch.wait()
                act(AA, SR, AF.Exp, bias=cn(NH, n), scale=cn(NH, n)).then_inc(E("a_a"), 1)
                act(TA, SR, AF.Tanh, bias=cn(0, n), scale=cn(0, n)).then_inc(E("a_t"), 1)

            def multiplier(n):
                eng.wait_ge(E("d_v"), n + 1)
                act(SQT, TA, AF.Sqrt, scale=0.25).then_inc(E("a_sqt"), 1)

            def pre_conv(n, u):
                eng.wait_ge(E("unit_done"), u + 1)
                eng.wait_ge(E("d_xc"), n)
                cs = cst[:, n, :] if isinstance(n, int) else cst[:, bass.ds(n, 1), :].rearrange("p a r -> p (a r)")
                act(XS[:, :, 0:CW - 1], cs.rearrange("p (b j) -> p b j", j=CW - 1), AF.Copy)
                act(halves(XP[:, CW - 1:CW - 1 + T]), proj(0), AF.Copy)
                act(XS[:, :, CW - 1], pp[0][:, 1, TH - NB:TH], AF.Copy).then_inc(posted(0), 1)

            def first_tap(n):
                eng.wait_ge(E("d_m1"), n)
                eng.wait_ge(posted(0), n + 2 * G_LRU + 1)
                act(XF, XP[:, 0:NX - (CW - 1)], AF.Identity, bias=PRM(n + R_CB), scale=PRM(n + R_CW))\
                    .then_inc(E("a_tap"), 1)

            h, u0 = NH - 1, 4 * G_LRU
            prep(u0 + 1, 1)
            eng.wait_ge(E("unit_done"), 4 * NH)
            eng.wait_ge(E("d_f"), NH)
            act(halves(SIG), proj(1), AF.Sigmoid).then_inc(E("a_sg"), 1)
            eng.wait_ge(posted(1), 2 * G_LRU)
            pre_conv(0, u0)
            prep(u0 + 2, 2)
            sample_rows(h)
            turned_keys(h)
            first_tap(0)
            eng.wait_ge(E("p_os"), NH)
            squares_of_ly(0)
            prep(u0 + 3, 3)
            squares(h)
            state_out(h)
            gelu_tanh(0)
            roots(h)
            out_high(h)
            pre_conv(1, u0 + 2)
            prep(u0 + 4, 0)
            gates(0)
            first_tap(1)
            multiplier(0)
            with eng.Fori(1, Q_LRU) as i:
                ch.begin(i - 1, 2)
                u0 = i * 4 + 4 * G_LRU
                for bb in range(2):
                    n = i * 2 + bb
                    squares_of_ly(n - 1)
                    prep(u0 + 2 * bb + 1, 2 * bb + 1)
                    gelu_tanh(n - 1)
                    branch_high(n - 2)
                    gates(n - 1)
                    prep(u0 + 2 * bb + 2, (2 * bb + 2) % 4)
                    pre_conv(n, u0 + 2 * bb)
                    first_tap(n)
                    multiplier(n - 1)
                ch.end(Q_LRU - 1)
            squares_of_ly(NH - 1)
            prep(4 * G_MIX + 1, 1)
            gelu_tanh(NH - 1)
            branch_high(NH - 2)
            gates(NH - 1)
            prep(4 * G_MIX + 2, 2)
            multiplier(NH - 1)
            def branch_gate(j, part):
                eng.wait_ge(E("unit_done"), j * 4 + 4 * G_MIX + 2 * part + 1)
                eng.wait_ge(posted(1), j * 2 + 2 * G_MIX - 1 + part)
                act(halves(U(2 * part)), proj(0), AF.Sigmoid).then_inc(posted(0), 1)

            def mix(j):
                u0 = j * 4 + 4 * G_MIX
                if not isinstance(j, int):
                    prep(u0 + 2, 2)
                    branch_gate(j, 0)
                prep(u0 + 3, 3)
                prep(u0 + 4, 0)
                branch_gate(j, 1)
                prep(u0 + 5, 1)
                eng.wait_ge(E("d_mb"), j + 1)
                act(hi_of(MG, j), U(3), AF.Copy).then_inc(E("a_mhi"), 1)

            eng.wait_ge(E("a_t"), NH)
            eng.wait_ge(E("a_a"), NH)
            branch_gate(0, 0)
            branch_high(NH - 1)
            eng.wait_ge(E("d_hl"), NH)
            mix(0)
            with eng.Fori(1, Q_MIX) as j:
                mix(j)

            eng.wait_ge(E("d_mlo"), KT)
            for i in range(Q_OUT):
                for s in range(4):
                    u = i * 4 + 4 * G_OUT + s
                    eng.wait_ge(E("unit_done"), u + 1)
                    eng.wait_ge(E("d_acc"), i * 4 + s - 1 if s else i * 4)
                    act(halves(X(s % 2)), proj(s % 2), AF.Square).then_inc(E("a_osq"), 1)
                    act(halves(U(4 * i + s)), proj(s % 2), AF.Copy,
                        scale=PRM(i * 4 + (R_MPOST + s))).then_inc(posted(s), 1)
                    prep(u + 2, (s + 2) % 4)
            inverse_rms(0, 0)
            def turned_x1(j):
                eng.wait_ge(E("p_x1t"), j + 1)
                act(U(8 + j, TP), (PO, PM)[j % 2], AF.Copy).then_inc(E("a_x1t"), 1)

            for j in range(KT):
                eng.wait_ge(E("d_x1"), j + 1)
                act(hi_of(HN, j), U(j), AF.Copy, scale=PRM(R_FPRE + j)).then_inc(E("a_nhi"), 1)
                if j:
                    eng.wait_ge(E("d_facc"), j)
                act(X(1), U(j), AF.Square).then_inc(E("n_sq"), 1)
                if j:
                    turned_x1(j - 1)
            prep(4 * G_FFI + 2, 2)
            inverse_rms(1, 0)
            turned_x1(KT - 1)
            prep(4 * G_FFI + 3, 3)
            eng.wait_ge(E("d_gate0"), 1)
            act(U(1), U(0), AF.Sigmoid).then_inc(E("a_sgate"), 1)
            eng.wait_ge(E("d_hid0"), 1)
            act(hi_of(HD, 0), U(3), AF.Copy).then_inc(E("a_hhi"), 1)

            def ffi(i):
                u0 = i * 4 + 4 * G_FFI
                for jj in (1,) if isinstance(i, int) else range(2):
                    j = i * 2 + jj
                    prep(u0 + 2 * jj + 2, (2 * jj + 2) % 4)
                    eng.wait_ge(E("d_slr"), j)
                    eng.wait_ge(posted(0), j + 2 * G_FFI + 1)
                    act(U(1), U(0), AF.Sigmoid).then_inc(E("a_sgate"), 1)
                    prep(u0 + 2 * jj + 3, (2 * jj + 3) % 4)
                    eng.wait_ge(posted(1), j + 2 * G_FFI + 1)
                    act(hi_of(HD, j), U(3), AF.Copy).then_inc(E("a_hhi"), 1)

            ffi(0)
            with eng.Fori(1, Q_FFI) as i:
                ffi(i)

            def ffo(i, last):
                for jj in range(2):
                    j = i * 2 + jj
                    for s in range(4):
                        u = i * 8 + 4 * G_FFO + 4 * jj + s
                        if not (last and jj == 1 and s >= 2):
                            eng.wait_ge(E("unit_done"), u + 1)
                            prep(u + 2, (s + 2) % 4, KSPLIT[(s + 2) % 4])
                    eng.wait_ge(E("unit_done"), u + 1)
                    if isinstance(i, int) and j == 0:
                        eng.wait_ge(E("d_hlo"), FT)
                    eng.wait_ge(E("d_acc"), j + (KT - 1))
                    act(halves(X(1 + jj)), proj(jj), AF.Square).then_inc(E("a_osq"), 1)
                    act(halves(U(j) if isinstance(i, int) else tmp[:, bass.ds(j * T, T)]), proj(jj), AF.Copy,
                        scale=PRM(j + R_FPOST)).then_inc(posted(jj), 1)

            ffo(0, False)
            with eng.Fori(1, KT // 2 - 1) as i:
                ffo(i, False)
            ffo(KT // 2 - 1, True)
            eng.wait_ge(E("n_mm"), 3)
            act(rt[:, 0:NCH + NB], pp[1][:, 0, 0:NCH + NB], AF.Sqrt, bias=eps[:, 0:1], scale=1.0 / D).then_inc(E("a_last"), 1)
            eng.wait_ge(E("ys_turned"), 1)
            act(extra[0:NB, 0:D].rearrange("p (a k) -> p a k", a=2), pr[0:NB, :, :], AF.Copy).then_inc(E("ys_ready"), 1)

        @block.vector
        def _(eng):
            ch = Chain(eng, E("dve_order"))
            tt, ts, stt, cp = eng.tensor_tensor, eng.tensor_scalar, eng.scalar_tensor_tensor, eng.tensor_copy

            def posted(s):
                return E(f"proj_free{s % 2}")

            def prep(u, s, nk=KT):
                eng.wait_ge(E("hi_ready"), u + 1)
                tt(wl[:, s % 2, 0:nk], raw[:, s, 0:nk], wh[:, s % 2, 0:nk].bitcast(F32), SUB).then_inc(E("lo_ready"), 1)

            def add_square(n, x, acc, j):
                eng.wait_ge(E("a_osq"), n + 1)
                if isinstance(j, int) and j == 0:
                    cp(X(acc), X(x)).then_inc(E("d_acc"), 1)
                else:
                    eng.wait_ge(E("d_acc"), n)
                    tt(X(acc), X(acc), X(x), ADD).then_inc(E("d_acc"), 1)

            eng.memset(ones[:], 1.0).then_inc(E("eps_ready"), 1)
            eng.memset(eps[:], EPS).then_inc(E("eps_ready"), 1)
            eng.wait_ge(E("a_root"), 2)
            eng.wait_ge(E("id_in"), 16)
            ch.link(eng.reciprocal(ROOTS[:, 0:NCH], ROOTS[:, 0:NCH]))
            ch.link(eng.reciprocal(ROOTS[0:NB, NCH:NCH + 1], ROOTS[0:NB, NCH:NCH + 1]))
            ch.wait()
            tt(DIAG, ident[:].unsqueeze(1).to_broadcast([P, NCH, P]), ROOTS[:, 0:NCH].unsqueeze(2).to_broadcast([P, NCH, P]), MUL)
            ts(DIAGS, ident[0:NB, 0:NB], ROOTS[0:NB, NCH:NCH + 1], None, MUL).then_inc(E("d_diag"), 1)
            prep(0, 0)
            prep(1, 1)
            eng.wait_ge(E("prm_ready"), 1)
            L0, L1 = prm[:, R_LB:R_LB + 8], prm[:, R_LB + 8:R_LB + 16]
            ll = prm[:, R_LL:R_LL + 8]
            mx = sp[:, 24:32]
            ch.then_wait(tt(mx, L0, L1, ALU.max))
            ch.link(tt(sp[:, 0:8], L0, mx, SUB))
            tt(sp[:, 8:16], L1, mx, SUB).then_inc(E("lb_in"), 1)
            ch.wait()
            ch.then_wait(ts(sp[:, 16:24], ll, -1.0, None, MUL))
            tt(sp[:, 16:24], sp[:, 16:24], ll, ALU.min).then_inc(E("lb_in"), 1)
            eng.wait_ge(E("r_ready"), 1)
            eng.wait_ge(E("xs_ready"), 1)

            def low(j):
                eng.wait_ge(E("a_nhi"), j + 1)
                tt(lo_of(XN, j), X(j % 2), hi_of(XN, j).bitcast(F32), SUB).then_inc(E("d_nlo"), 1)

            for j in range(KT):
                eng.wait_ge(E("xt_ready"), j + 1)
                if j >= 2:
                    eng.wait_ge(E("d_nlo"), j - 1)
                stt(X(j % 2), U(8 + j), PRM(R_MPRE + j), X(2), MUL, MUL).then_inc(E("d_norm"), 1)
                if j >= 1:
                    low(j - 1)
            low(KT - 1)
            eng.wait_ge(E("m_in"), 16)
            for i in range(NLEV):
                n = P if i == 0 else P // 2
                at = 0 if i == 0 else P + (i - 1) * n
                src = raw[:, 3].rearrange("p k n -> p (k n)")[:, at:at + n].unsqueeze(1).to_broadcast([P, NCH, n])
                cp(mask(i).rearrange("p (c n) -> p c n", c=NCH), src).then_inc(E("m_made"), 1)
            ch.then_wait(tt(sel[:], ident[0:NS, 0:NB], ident[0:NS, NB:2 * NB], ADD))
            ch.link(tt(sel[:], sel[:], ident[0:NS, 2 * NB:3 * NB], ADD))
            eng.wait_ge(E("x_turned"), KT)
            ch.link(eng.memset(AT, 0.0))
            ch.link(eng.memset(XP[:, 0:3], 0.0))
            ch.wait()
            eng.wait_ge(E("m_made"), NLEV)

            def cols_of(ap, b):
                return ap.rearrange("p (n two b) -> p n two b", two=2, b=b)

            def level(h, i):
                eng.wait_ge(E("p_L"), h * 8 + i)
                if i == 1:
                    tt(QP[:, 0:TP], QP[:, 0:TP], FF[:, 0:TP], MUL).then_inc(E("d_L"), 1)
                else:
                    b = 1 << (i - 2)
                    n = TP // (2 * b)
                    tb = tot(b).rearrange("p (n two) -> p n two", two=2)
                    q2, k1 = cols_of(QP[:, 0:TP], b)[:, :, 1, :], cols_of(KS[:, 0:TP], b)[:, :, 0, :]
                    if i > 2:
                        ch.wait()
                    eng.wait_ge(E("d_L"), h * 8 + i - 1)
                    eng.wait_ge(E("d_take"), h * 8 + i - 1)
                    ch.link(tt(q2, q2, tb[:, :, 0:1].to_broadcast([P, n, b]), MUL))
                    ch.link(tt(tot(2 * b), tb[:, :, 0], tb[:, :, 1], MUL))
                    tt(k1, k1, tb[:, :, 1:2].to_broadcast([P, n, b]), MUL).then_inc(E("d_L"), 1)
                take(i - 1)

            def take(i):
                bank = SB if i % 2 == 0 else SA
                if i == 0:
                    eng.copy_predicated(AT, mask(0), bank).then_inc(E("d_take"), 1)
                else:
                    hs = 1 << (i - 1)
                    v = "p (n b) -> p n b"
                    eng.copy_predicated(cols_of(AT, hs)[:, :, 1, :], mask(i).rearrange(v, b=hs),
                                        bank[:, 0:TP // 2].rearrange(v, b=hs)).then_inc(E("d_take"), 1)

            def chunk_states(h):
                eng.wait_ge(E("p_kv"), h + 1)
                eng.wait_ge(E("st_out"), h * 32)
                t128 = tot(P)
                ch.wait()
                ch.then_wait(cp(SCH[:, 0:P], SA[:, 0:P]))
                for k in range(1, NCH):
                    o = stt(SCH[:, k * P:(k + 1) * P], SCH[:, (k - 1) * P:k * P], t128[:, k:k + 1],
                            SA[:, k * P:(k + 1) * P], MUL, ADD)
                    if k < NCH - 1:
                        ch.then_wait(o)
                o.then_inc(E("d_kv"), 1)

            def stack_samples(h):
                kv, v = KS[:, TP:T], VT[:, TP:T]
                eng.wait_ge(E("p_st"), h)
                kk, vv = stk[:, 0].rearrange("p (c b) -> p c b", b=NB), stk[:, 1].rearrange("p (c b) -> p c b", b=NB)
                ch.link(cp(kk[:, 0:2], kv.unsqueeze(1).to_broadcast([P, 2, NB])))
                ch.link(cp(vv[:, 0:3:2], v.unsqueeze(1).to_broadcast([P, 2, NB])))
                ch.wait()
                tt(kk[:, 2], kv, kk[:, 0].bitcast(F32), SUB)
                tt(vv[:, 1], v, vv[:, 0].bitcast(F32), SUB).then_inc(E("d_stk"), 1)

            def sample_values(h):
                eng.wait_ge(E("a_st"), h + 1)
                vs = STOK[:, P:2 * P].bitcast(F32).unsqueeze(1).to_broadcast([NS, NB, P])
                dd = sel[:].unsqueeze(2).to_broadcast([NS, NB, P])
                tt(VBD.rearrange("p (b v) -> p b v", b=NB), vs, dd, MUL).then_inc(E("d_vbd"), 1)

            def sample_states(h):
                eng.wait_ge(E("st_in"), h * 16 + 16)
                for k, bank in enumerate((PM, SB)):
                    eng.wait_ge(E("p_outer"), h * 2 + k + 1)
                    for b in range(4):
                        o = stt(SS[:, 4 * k + b, :], SS[:, 4 * k + b, :], FF[:, TP + 4 * k + b:TP + 4 * k + b + 1],
                                bank[:, b * P:(b + 1) * P], MUL, ADD)
                        if b < 3:
                            ch.link(o)
                    o.then_inc(E("d_half"), 1)

            def gate_head(h):
                eng.wait_ge(E("a_ln"), h + 1)
                eng.wait_ge(E("a_ohi"), h)
                eng.wait_ge(E("d_olo"), h)
                ch.link(stt(O1[:, 0:TP], PO, PRM(R_ON), SOG[:, 0:TP], MUL, MUL))
                stt(O1[:, TP:T], PM[:, 0:NB], PRM(R_ON), SOG[:, TP:T], MUL, MUL).then_inc(E("d_o1"), 1)

            def norm_head(h):
                ch.wait()
                eng.wait_ge(E("d_o1"), h + 1)
                eng.wait_ge(E("a_rs"), h + 1)
                tt(O1, O1, SQ, MUL).then_inc(E("d_o"), 1)

            def head_low(h):
                eng.wait_ge(E("a_ohi"), h + 1)
                tt(lo_of(OA, h), O1, hi_of(OA, h).bitcast(F32), SUB).then_inc(E("d_olo"), 1)

            def out_gate(h):
                eng.wait_ge(E("a_sg"), h + 1)
                tt(halves(SOG), proj(1), halves(SIG), MUL).then_inc(posted(1), 1)

            def lower_bound():
                eng.wait_ge(E("lb_exp"), 1)
                ch.then_wait(tt(mx, sp[:, 0:8], sp[:, 8:16], ADD))
                ch.then_wait(eng.reciprocal(mx, mx))
                ch.link(tt(lb[:, 0:8], sp[:, 0:8], mx, MUL))
                ch.wait()
                ch.then_wait(ts(lb[:, 8:16], lb[:, 0:8], -1.0, 1.0, MUL, ADD))

            def softplus():
                eng.wait_ge(E("lb_exp"), 2)
                ee, z, z2, acc = sp[:, 16:24], sp[:, 0:8], sp[:, 8:16], sp[:, 24:32]
                ch.then_wait(ts(z, ee, 2.0, None, ADD))
                ch.then_wait(eng.reciprocal(z, z))
                ch.then_wait(tt(z, z, ee, MUL))
                ch.then_wait(tt(z2, z, z, MUL))
                ch.then_wait(ts(acc, z2, 1.0 / 19, None, MUL))
                for k in (17, 15, 13, 11, 9, 7, 5, 3):
                    ch.then_wait(stt(acc, acc, 1.0 / k, z2, ADD, MUL))
                ch.then_wait(stt(acc, acc, 1.0, z, ADD, MUL))
                ch.then_wait(ts(z, ll, -4.0, 0.0, MUL, ALU.max))
                ch.then_wait(stt(c4[:, 0:NH], acc, 8.0, z, MUL, ADD))
                ch.link(ts(c4[:, NH:2 * NH], c4[:, 0:NH], -1.0, None, MUL))
                ch.link(ts(prm[:, R_BA:R_BX + 8], prm[:, R_BA:R_BX + 8], 0.5, None, MUL))

            def hg_steps(h, prev):
                if prev:
                    prep(4 * h + 1, 1)
                    level(h - 1, 4)
                    stack_samples(h - 1)
                    out_gate(h - 1)
                    level(h - 1, 5)
                    level(h - 1, 6)
                    level(h - 1, 7)
                prep(4 * h + 2, 2)
                if not prev:
                    lower_bound()
                if prev:
                    level(h - 1, 8)
                    sample_values(h - 1)
                    chunk_states(h - 1)
                prep(4 * h + 3, 3)
                if prev:
                    sample_states(h - 1)
                    eng.wait_ge(E("p_os"), h)
                eng.wait_ge(E("a_sq"), h + 1)
                tt(halves(QP), proj(1), halves(SIG), MUL).then_inc(posted(1), 1)
                if not prev:
                    softplus()
                prep(4 * h + 4, 0)
                eng.wait_ge(posted(0), 2 * h + 2)
                eng.wait_ge(posted(1), 2 * h + 1)
                if prev:
                    eng.wait_ge(E("p_so"), h)
                ch.link(cp(QS, QP[:, TP:T]))
                lbs = lambda a: lb[:, a:a + 1] if isinstance(a, int) else lb[:, bass.ds(a, 1)]
                ch.then_wait(ts(FF, SIG, lbs(h + NH), lbs(h), MUL, ADD))
                ts(KS, FF, -1.0, 1.0, MUL, ADD).then_inc(E("d_f"), 1)
                eng.wait_ge(E("d_f"), h + 1)
                if prev:
                    gate_head(h - 1)
                level(h, 1)
                if prev:
                    norm_head(h - 1)
                level(h, 2)
                if prev:
                    head_low(h - 1)
                level(h, 3)

            hg_steps(0, False)
            with eng.Fori(1, NH) as h:
                ch.begin(h - 1, LINKS_HG)
                hg_steps(h, True)
                ch.end(NH - 1)
            def conv(n):
                eng.wait_ge(E("a_tap"), n + 1)
                w = lambda j: PRM(n + (R_CW + 8 * j))
                co = cout[:, 3:27, bass.ds(n, 1)].rearrange("p (b j) n -> p b (j n)", j=CW - 1)
                keep = ((cout[:, 0:3, bass.ds(n, 1)], XP[:, TP:TP + 3].unsqueeze(2)), (co, XS[:, :, 1:CW]))
                for j in range(1, CW):
                    ch.link(stt(XF, XP[:, j:j + NX - (CW - 1)], w(j), XF, MUL, ADD))
                    if j < CW - 1:
                        cp(*keep[j - 1])
                    ch.wait()
                cp(XC[:, TP:T], XF[:, T:T + CW * NB].rearrange("p (b j) -> p b j", j=CW)[:, :, CW - 1])\
                    .then_inc(E("d_xc"), 1)

            def gelu_inner(n):
                eng.wait_ge(E("a_gsq"), n + 1)
                tt_in = halves(GSQ)
                stt(tt_in, tt_in, 1.0, proj(1), ADD, MUL).then_inc(E("d_u"), 1)

            def branch_low(n):
                eng.wait_ge(E("a_ghi"), n + 1)
                tt(lo_of(GB, n), GG, hi_of(GB, n).bitcast(F32), SUB).then_inc(E("d_hl"), 1)

            def gelu(n):
                eng.wait_ge(E("a_th"), n + 1)
                eng.wait_ge(E("d_hl"), n)
                stt(halves(GG), halves(GSQ), 1.0, proj(1), ADD, MUL).then_inc(posted(1), 1)

            def gated(n):
                eng.wait_ge(E("a_si"), n + 1)
                eng.wait_ge(E("d_xc"), n + 1)
                stt(SI, SI, 1.0, XC, ADD, MUL).then_inc(E("d_m1"), 1)
                eng.wait_ge(E("a_a"), n + 1)
                ch.then_wait(tt(A2, AA, AA, MUL))
                eng.wait_ge(E("a_t"), n + 1)
                stt(TA, A2, 1.0, TA, ADD, MUL).then_inc(E("d_v"), 1)

            def recurrence(n):
                eng.wait_ge(E("a_sqt"), n + 1)
                eng.wait_ge(E("d_m1"), n + 1)
                ch.link(tt(SQT[:, 1:T], SQT[:, 1:T], SI[:, 1:T], MUL))
                ch.link(ts(SQT[:, 0:1], SI[:, 0:1], 0.5, None, MUL))
                hs = hst[:, n, :] if isinstance(n, int) else hst[:, bass.ds(n, 1), :].rearrange("p a r -> p (a r)")
                ch.link(tt(HH[:, TP:T], AA[:, TP:T], hs, MUL))
                ch.wait()
                ch.link(eng.tensor_tensor_scan(HH[:, 0:TP], AA[:, 0:TP], SQT[:, 0:TP], 0.0, MUL, ADD))
                ch.then_wait(tt(HH[:, TP:T], HH[:, TP:T], SQT[:, TP:T], ADD))
                stt(GG, GG, 0.5, HH, MUL, MUL).then_inc(E("d_gh"), 1)
                ch.link(cp(hout[:, :, bass.ds(n, 1)], HH[:, TP - 1:T].unsqueeze(2)))

            h, u0 = NH - 1, 4 * G_LRU
            prep(u0 + 1, 1)
            level(h, 4)
            stack_samples(h)
            out_gate(h)
            for i in (5, 6, 7):
                level(h, i)
            prep(u0 + 2, 2)
            level(h, 8)
            sample_values(h)
            chunk_states(h)
            conv(0)
            prep(u0 + 3, 3)
            sample_states(h)
            gelu_inner(0)
            gelu(0)
            gate_head(h)
            norm_head(h)
            head_low(h)
            prep(u0 + 4, 0)
            eng.wait_ge(E("d_olo"), NH)
            gated(0)
            conv(1)
            with eng.Fori(1, Q_LRU) as i:
                ch.begin(i - 1, LINKS_LRU)
                u0 = i * 4 + 4 * G_LRU
                for bb in range(2):
                    n = i * 2 + bb
                    gelu_inner(n - 1)
                    recurrence(n - 2)
                    prep(u0 + 2 * bb + 1, 2 * bb + 1)
                    branch_low(n - 2)
                    gelu(n - 1)
                    gated(n - 1)
                    prep(u0 + 2 * bb + 2, (2 * bb + 2) % 4)
                    conv(n)
                ch.end(Q_LRU - 1)
            gelu_inner(NH - 1)
            prep(4 * G_MIX + 1, 1)
            recurrence(NH - 2)
            branch_low(NH - 2)
            gelu(NH - 1)
            gated(NH - 1)
            prep(4 * G_MIX + 2, 2)
            recurrence(NH - 1)
            branch_low(NH - 1)
            eng.wait_ge(E("st_out"), 32 * NH)

            eng.wait_ge(E("a_ghi"), NH)
            eng.wait_ge(E("d_hl"), NH)
            def mix(j):
                u0 = j * 4 + 4 * G_MIX
                if not isinstance(j, int):
                    prep(u0 + 2, 2)
                eng.wait_ge(posted(0), j * 2 + 2 * G_MIX + 1)
                eng.wait_ge(E("unit_done"), u0 + 2)
                tt(halves(U(1)), proj(1), halves(U(0)), MUL).then_inc(posted(1), 1)
                prep(u0 + 3, 3)
                prep(u0 + 4, 0)
                eng.wait_ge(posted(0), j * 2 + 2 * G_MIX + 2)
                eng.wait_ge(E("unit_done"), u0 + 4)
                eng.wait_ge(E("d_mlo"), j)
                eng.wait_ge(E("a_mhi"), j)
                tt(halves(U(3)), proj(1), halves(U(2)), MUL).then_inc(posted(1), 1)
                prep(u0 + 5, 1)
                eng.wait_ge(posted(1), j * 2 + 2 * G_MIX + 2)
                tt(U(3), U(3), U(1), ADD).then_inc(E("d_mb"), 1)
                eng.wait_ge(E("a_mhi"), j + 1)
                tt(lo_of(MG, j), U(3), hi_of(MG, j).bitcast(F32), SUB).then_inc(E("d_mlo"), 1)

            mix(0)
            with eng.Fori(1, Q_MIX) as j:
                mix(j)
            rows = tmp[:, 13 * T:13 * T + 4 * P]
            eng.wait_ge(E("p_rows"), 1)
            ch.link(cp(rows[0:72, 0:P], SA[0:72, 0:P]))
            ch.link(cp(rows[0:24, P:2 * P], SA[0:24, P:2 * P]))
            cp(rows[0:96, 2 * P:4 * P], SA[0:96, 2 * P:4 * P]).then_inc(E("rows_ready"), 1)

            for i in range(Q_OUT):
                for s in range(4):
                    add_square(4 * i + s, s % 2, 2, 4 * i + s)
                    prep(i * 4 + 4 * G_OUT + s + 2, (s + 2) % 4)
            eng.wait_ge(E("n_rs"), 1)
            eng.wait_ge(E("xt_back"), 16)
            eng.wait_ge(posted(0), 2 * G_FFI)
            eng.wait_ge(posted(1), 2 * G_FFI)
            def ffn_low(j):
                eng.wait_ge(E("a_nhi"), KT + j + 1)
                stt(lo_of(HN, j), U(j), PRM(R_FPRE + j), hi_of(HN, j).bitcast(F32), MUL, SUB).then_inc(E("d_nlo"), 1)

            def ffn_square(j):
                eng.wait_ge(E("n_sq"), j + 1)
                if j == 0:
                    cp(X(2), X(1)).then_inc(E("d_facc"), 1)
                else:
                    eng.wait_ge(E("d_facc"), j)
                    tt(X(2), X(2), X(1), ADD).then_inc(E("d_facc"), 1)

            for j in range(KT):
                ch.then_wait(tt(U(j), U(j), X(0), MUL))
                tt(U(j), U(j), U(8 + j), ADD).then_inc(E("d_x1"), 1)
                if j:
                    ffn_low(j - 1)
                    ffn_square(j - 1)
            ffn_low(KT - 1)
            ffn_square(KT - 1)
            eng.wait_ge(E("d_x1"), KT)
            cp(X1S, FOUT[:, :, TP:T]).then_inc(E("d_x1s"), 1)
            eng.wait_ge(E("a_x1t"), 4)
            eng.wait_ge(E("d_x1s"), 1)

            prep(4 * G_FFI + 2, 2)
            eng.wait_ge(E("unit_done"), 4 * G_FFI + 2)
            cp(halves(U(0)), proj(0)).then_inc(posted(0), 1)
            cp(halves(U(3)), proj(1)).then_inc(posted(1), 1)
            prep(4 * G_FFI + 3, 3)
            eng.wait_ge(E("n_rs"), 2)
            eng.wait_ge(posted(0), 2 * G_FFI + 1)
            eng.wait_ge(posted(1), 2 * G_FFI + 1)
            tt(U(0), U(0), X(0), MUL).then_inc(E("d_gate0"), 1)
            eng.wait_ge(E("d_gate0"), 1)
            eng.wait_ge(E("a_sgate"), 1)
            ch.then_wait(tt(U(2), U(0), U(1), MUL))
            tt(U(2), U(2), X(0), MUL).then_inc(E("d_slr"), 1)
            eng.wait_ge(E("d_slr"), 1)
            tt(U(3), U(3), U(2), MUL).then_inc(E("d_hid0"), 1)
            eng.wait_ge(E("d_hid0"), 1)
            eng.wait_ge(E("a_hhi"), 1)
            tt(lo_of(HD, 0), U(3), hi_of(HD, 0).bitcast(F32), SUB).then_inc(E("d_hlo"), 1)

            def ffi(i):
                u0 = i * 4 + 4 * G_FFI
                for jj in (1,) if isinstance(i, int) else range(2):
                    j = i * 2 + jj
                    prep(u0 + 2 * jj + 2, (2 * jj + 2) % 4)
                    eng.wait_ge(E("unit_done"), u0 + 2 * jj + 1)
                    tt(halves(U(0)), proj(0), halves(X(0)), MUL).then_inc(posted(0), 1)
                    eng.wait_ge(E("a_sgate"), j + 1)
                    ch.then_wait(tt(U(2), U(0), U(1), MUL))
                    tt(U(2), U(2), X(0), MUL).then_inc(E("d_slr"), 1)
                    prep(u0 + 2 * jj + 3, (2 * jj + 3) % 4)
                    eng.wait_ge(E("unit_done"), u0 + 2 * jj + 2)
                    eng.wait_ge(E("a_hhi"), j)
                    eng.wait_ge(E("d_hlo"), j)
                    eng.wait_ge(E("d_slr"), j + 1)
                    tt(halves(U(3)), proj(1), halves(U(2)), MUL).then_inc(posted(1), 1)
                    eng.wait_ge(posted(1), j + 2 * G_FFI + 1)
                    eng.wait_ge(E("a_hhi"), j + 1)
                    tt(lo_of(HD, j), U(3), hi_of(HD, j).bitcast(F32), SUB).then_inc(E("d_hlo"), 1)

            ffi(0)
            with eng.Fori(1, Q_FFI) as i:
                ch.begin(i - 1, 2)
                ffi(i)
                ch.end(Q_FFI - 1)

            def ffo(i, last, first=False):
                for jj in range(2):
                    if jj == 0 and not first:
                        add_square(i * 2 + (KT - 1), 2, 0, i * 2 - 1)
                    if jj == 1:
                        add_square(i * 2 + KT, 1, 0, i * 2)
                    for s in range(4):
                        if not (last and jj == 1 and s >= 2):
                            prep(i * 8 + 4 * G_FFO + 4 * jj + s + 2, (s + 2) % 4, KSPLIT[(s + 2) % 4])

            ffo(0, False, first=True)
            with eng.Fori(1, KT // 2 - 1) as i:
                ffo(i, False)
            ffo(KT // 2 - 1, True)
            add_square(2 * KT - 1, 2, 0, KT - 1)
            eng.wait_ge(E("a_last"), 1)
            ch.then_wait(eng.reciprocal(rt[:, 0:NCH + NB], rt[:, 0:NCH + NB]))

            def last_sum(c):
                eng.wait_ge(E("y_turned"), c + 1)
                stt(raw[:, c], YC[c][:].rearrange("p a (k n) -> p (a k) n", n=P), rt[:, c:c + 1],
                    X1TOK[:, :, c * P:(c + 1) * P], MUL, ADD).then_inc(E("d_y"), 1)

            last_sum(0)
            rs = rt[:, NCH:NCH + NB].unsqueeze(1).to_broadcast([P, KT, NB])
            ch.then_wait(tt(YS, FOUT[:, :, TP:T], rs, MUL))
            tt(YS, YS, X1S, ADD).then_inc(E("d_ys"), 1)
            for c in range(1, NCH):
                last_sum(c)

        @block.tensor
        def _(eng):
            mm = eng.matmul

            def ktile(s, par, reg, k, start, stop, koff=0):
                xh, xl = acts[:, reg[0] + koff + k], acts[:, reg[1] + koff + k]
                a, b = wh[:, s % 2, k, :], wl[:, s % 2, k, :]
                for n, (w, x) in enumerate(((a, xh), (a, xl), (b, xh))):
                    for hf in range(2):
                        o = mm(pp[par][:, hf, 0:TH], w, x[:, hf * TH:(hf + 1) * TH],
                               start=start and n == 0, stop=stop and n == 2)
                return o

            def unit(u, s, reg, fill=None, koff=0, nk=KT, par=None, free=None, first=True, last=True, ready=None):
                par = s % 2 if par is None else par
                eng.wait_ge(E("lo_ready"), u + 1)
                if free is not None:
                    eng.wait_ge(E(f"proj_free{par}"), free)
                for k in range(nk):
                    if ready:
                        ready(k)
                    o = ktile(s, par, reg, k, first and k == 0, last and k == nk - 1, koff)
                    if k == nk - 1:
                        o.then_inc(E("unit_done"), 1)
                    if fill and k % 2 == 1 and k // 2 in fill:
                        for f in fill[k // 2]:
                            f()

            def sum_up(src, start=True, stop=True):
                for hf in range(2):
                    o = mm(pr[:, hf, 0:TH], ones[:], src[:, hf * TH:(hf + 1) * TH], start=start, stop=stop)
                return o

            def first_pair(reg, u, ready, after):
                for k in range(KT):
                    ready(k)
                    for s in range(2):
                        if k == 0:
                            eng.wait_ge(E("lo_ready"), u + s + 1)
                            eng.wait_ge(E(f"proj_free{s}"), u // 2)
                        o = ktile(s, s, reg, k, k == 0, k == KT - 1)
                        if k == KT - 1:
                            o.then_inc(E("unit_done"), 1)
                    if after:
                        after(k)

            def turn_input(j):
                if j >= 2:
                    eng.wait_ge(E("xt_ready"), j - 1)
                for c in range(NCH):
                    o = eng.transpose((SA, SB)[j % 2][:, c * P:(c + 1) * P], tmp[:, c * D + j * P:c * D + (j + 1) * P], ident[:])
                o.then_inc(E("x_turned"), 1)

            eng.wait_ge(E("id_in"), 16)
            eng.wait_ge(E("xs_in"), 16)
            for j in range(KT):
                o = eng.transpose(PO[:, j * NB:(j + 1) * NB], extra[0:NB, j * P:(j + 1) * P], ident[0:NB, 0:NB])
            o.then_inc(E("xs_turned"), 1)
            for c in range(NCH):
                eng.wait_ge(E(f"x_in{c}"), 16)
            turn_input(0)
            turn_input(1)
            eng.wait_ge(E("p_in"), 16 * 14)
            eng.transpose(PM[:, 0:NROW], PROWS[0:NROW, :], ident[0:NROW, 0:NROW])
            eng.transpose(PM[:, P:P + NB * NH], HROWS, ident[0:NB * NH, 0:NB * NH])
            for k in range(2):
                o = eng.transpose(PM[:, 2 * P + k * 96:2 * P + (k + 1) * 96], CROWS[k], ident[0:96, 0:96])
            o.then_inc(E("turned"), 1)
            eng.wait_ge(E("d_diag"), 1)
            eng.wait_ge(E("eps_ready"), 2)
            eng.wait_ge(E("xs_ready"), 1)
            mm(PO, ones[:], DIAG.rearrange("p c t -> p (c t)"), start=True, stop=True)
            eng.wait_ge(E("cst_ready"), 2)
            mm(PM[:, 0:NB], ones[0:NB, :], DIAGS, start=True, stop=True).then_inc(E("r_spread"), 1)

            def turn_values(h, prev):
                if prev:
                    eng.wait_ge(E("d_kv"), h)
                eng.wait_ge(E("proj_free0"), 2 * h + 1)
                for k in range(NCH):
                    o = eng.transpose(SA[:, k * P:(k + 1) * P], VT[:, k * P:(k + 1) * P], ident[:])
                o.then_inc(E("p_vt"), 1)

            def score(h, i, prev=True):
                if i == 0:
                    eng.wait_ge(E("d_f"), h + 1)
                    if prev:
                        eng.wait_ge(E("a_ln"), h)
                else:
                    eng.wait_ge(E("d_L"), h * 8 + i)
                    if i == 1:
                        eng.wait_ge(E("a_vt"), h + 1)
                    else:
                        eng.wait_ge(E("d_take"), h * 8 + i - 1)
                bank = SB if i % 2 == 0 else SA
                n = P if i == 0 else P // 2
                for k in range(NCH):
                    rhs = QP[:, k * P:(k + 1) * P]
                    if i:
                        rhs = rhs.rearrange("p (n two b) -> p n two b", two=2, b=1 << (i - 1))[:, :, 1, :]
                    o = mm(bank[:, k * n:(k + 1) * n], KS[:, k * P:(k + 1) * P], rhs, start=True, stop=True)
                o.then_inc(E("p_L"), 1)

            def turn_sample(h):
                if not isinstance(h, int) or h > 0:
                    eng.wait_ge(E("d_o1"), h)
                    eng.wait_ge(E("a_ln"), h)
                eng.wait_ge(E("d_stk"), h + 1)
                for a in range(2):
                    o = eng.transpose(PM[0:NS, a * P:(a + 1) * P], stk[:, a].bitcast(F32), ident[:])
                o.then_inc(E("p_st"), 1)

            def turn_keys(h):
                eng.wait_ge(E("d_L"), h * 8 + 8)
                eng.wait_ge(E("d_take"), h * 8 + 7)
                for k in range(NCH):
                    o = eng.transpose(SB[:, k * P:(k + 1) * P], KS[:, k * P:(k + 1) * P], ident[:])
                o.then_inc(E("p_kst"), 1)

            def key_values(h):
                eng.wait_ge(E("a_kst"), h + 1)
                eng.wait_ge(E("d_take"), h * 8 + 8)
                for k in range(NCH):
                    o = mm(SA[:, k * P:(k + 1) * P], KTOK[:, k * P:(k + 1) * P], VTOK[:, k * P:(k + 1) * P],
                           start=True, stop=True)
                o.then_inc(E("p_kv"), 1)

            def out_scores(h):
                if not isinstance(h, int) or h > 0:
                    eng.wait_ge(E("d_o1"), h)
                for k in range(NCH):
                    mm(PO[:, k * P:(k + 1) * P], VTOK[:, k * P:(k + 1) * P], AT[:, k * P:(k + 1) * P],
                       start=k == 0, stop=False, skip_group_check=True)

            def out_states(h):
                eng.wait_ge(E("d_kv"), h + 1)
                for k in range(1, NCH):
                    o = mm(PO[:, k * P:(k + 1) * P], SCH[:, (k - 1) * P:k * P], QP[:, k * P:(k + 1) * P],
                           start=False, stop=k == NCH - 1, skip_group_check=True)
                o.then_inc(E("p_os"), 1)

            def outer(h, k):
                eng.wait_ge(E("d_vbd"), h + 1)
                mm((PM, SB)[k], STOK[:, 0:P], VBD[:, k * 512:(k + 1) * 512], start=True, stop=True)\
                    .then_inc(E("p_outer"), 1)

            def sample_out(h):
                eng.wait_ge(E("d_half"), h * 2 + 2)
                for b in range(NB):
                    o = mm(PM[:, b:b + 1], SS[:, b, :], QS[:, b:b + 1], start=True, stop=True)
                o.then_inc(E("p_so"), 1)

            def head_sums(h):
                eng.wait_ge(E("a_square"), h + 1)
                mm(SB, ones[:], SQ[:, 0:TP], start=True, stop=True)
                mm(PM[:, NB:2 * NB], ones[:], SQ[:, TP:T], start=True, stop=True).then_inc(E("p_ones"), 1)

            def hg_steps(h, prev):
                p = h - 1
                def first_ready(k):
                    if k + 2 < KT:
                        turn_input(k + 2)
                    eng.wait_ge(E("d_nlo"), k + 1)

                if not prev:
                    first_pair(XN, 0, first_ready, None)
                else:
                    unit(4 * h, 0, XN, {k: [lambda k=k: score(p, k + 3)] for k in range(4)}, free=2 * h)
                    unit(4 * h + 1, 1, XN, {0: [lambda: score(p, 7), lambda: turn_sample(p)], 1: [lambda: turn_keys(p)],
                                            2: [lambda: key_values(p)], 3: [lambda: out_scores(p)]}, free=2 * h)
                unit(4 * h + 2, 2, XN, {0: [lambda: out_states(p), lambda: outer(p, 0)], 1: [lambda: outer(p, 1)],
                                        2: [lambda: sample_out(p)], 3: [lambda: head_sums(p)]} if prev else None, free=2 * h + 1)
                unit(4 * h + 3, 3, XN, {0: [lambda: turn_values(h, prev)], 1: [lambda: score(h, 0, prev)],
                                        2: [lambda: score(h, 1)], 3: [lambda: score(h, 2)]}, free=2 * h + 1)

            hg_steps(0, False)
            with eng.Fori(1, NH) as h:
                hg_steps(h, True)
            def gate_sums(n):
                i, bb = n if isinstance(n, tuple) else divmod(n, 2)
                n = i * 2 + bb
                eng.wait_ge(E("d_xc"), n + 1)
                if isinstance(n, int) and n == 0:
                    eng.wait_ge(E("a_ln"), NH)
                    eng.wait_ge(E("d_o1"), NH)
                else:
                    eng.wait_ge(E("a_si"), n)
                eng.wait_ge(E(f"gates_in{bb}"), i * 32 + 32)
                for a, bank in enumerate((pr, pi)):
                    for hf in range(2):
                        o = mm(bank[:, hf, 0:TH], wblock(2 * bb + a), XC[:, hf * TH:(hf + 1) * TH], start=True, stop=True)
                o.then_inc(E("p_gates"), 1)

            h, u0, v = NH - 1, 4 * G_LRU, 2 * G_LRU
            unit(u0, 0, XN, {k: [lambda k=k: score(h, k + 3)] for k in range(4)}, free=v)
            unit(u0 + 1, 1, XN, {0: [lambda: score(h, 7), lambda: turn_sample(h)], 1: [lambda: turn_keys(h)],
                                 2: [lambda: key_values(h)], 3: [lambda: out_scores(h)]}, free=v)
            unit(u0 + 2, 2, XN, {0: [lambda: out_states(h), lambda: outer(h, 0)], 1: [lambda: outer(h, 1)],
                                 2: [lambda: sample_out(h)], 3: [lambda: head_sums(h)]}, free=v + 1)
            unit(u0 + 3, 3, XN, {2: [lambda: gate_sums(0)]}, free=v + 1)
            with eng.Fori(1, Q_LRU) as i:
                u0, v = i * 4 + 4 * G_LRU, i * 2 + 2 * G_LRU
                unit(u0, 0, XN, {1: [lambda: gate_sums((i - 1, 1))]}, free=v)
                unit(u0 + 1, 1, XN, free=v)
                unit(u0 + 2, 2, XN, {1: [lambda: gate_sums((i, 0))]}, free=v + 1)
                unit(u0 + 3, 3, XN, free=v + 1)
            gate_sums(NH - 1)

            with eng.Fori(0, Q_MIX) as j:
                for s, reg in enumerate((XN, OA, XN, GB)):
                    if s % 2:
                        eng.wait_ge(E("d_hl" if s == 3 else "d_olo"), NH)
                    unit(j * 4 + 4 * G_MIX + s, s, reg, free=j * 2 + 2 * G_MIX + s // 2)
            eng.wait_ge(E("d_hl"), NH)
            hv, cv = hout[:].rearrange("p a n -> p (a n)"), cout[:].rearrange("p a n -> p (a n)")
            eng.transpose(SA[0:72, 0:P], hv, ident[:])
            eng.transpose(SA[0:24, P:2 * P], cv[:, 0:24], ident[:])
            for k in range(2):
                o = eng.transpose(SA[0:96, (2 + k) * P:(3 + k) * P], cv[:, 24 + 96 * k:120 + 96 * k], ident[:])
            o.then_inc(E("p_rows"), 1)
            for i in range(Q_OUT):
                for s in range(4):
                    unit(i * 4 + 4 * G_OUT + s, s, MG, free=i * 2 + 2 * G_OUT + s // 2,
                         ready=(lambda k: eng.wait_ge(E("d_mlo"), k + 1)) if i == s == 0 else None)
            eng.wait_ge(E("d_acc"), KT)
            sum_up(X(2)).then_inc(E("n_mm"), 1)

            def ffn_ready(k):
                eng.wait_ge(E("d_nlo"), KT + k + 1)

            def turn_x1(j):
                if j >= 2:
                    eng.wait_ge(E("a_x1t"), j - 1)
                for c in range(NCH):
                    o = eng.transpose((PO, PM)[j % 2][:, c * P:(c + 1) * P], U(j, P, c * P), ident[:])
                o.then_inc(E("p_x1t"), 1)

            first_pair(HN, 4 * G_FFI, ffn_ready, lambda k: turn_x1(k) if k < KT - 1 else None)
            eng.wait_ge(E("n_rs"), 1)
            eng.wait_ge(E("d_facc"), KT)
            sum_up(X(2)).then_inc(E("n_mm"), 1)
            turn_x1(KT - 1)
            for s in range(2, 4):
                unit(4 * G_FFI + s, s, HN, free=2 * G_FFI + s // 2)
            with eng.Fori(1, Q_FFI) as i:
                for s in range(4):
                    unit(i * 4 + 4 * G_FFI + s, s, HN, free=i * 2 + 2 * G_FFI + s // 2)

            def ffo(i):
                for jj in range(2):
                    for s in range(4):
                        if isinstance(i, int) and jj == 0:
                            eng.wait_ge(E("d_hlo"), KOFF[s] + KSPLIT[s])
                        unit(i * 8 + 4 * G_FFO + 4 * jj + s, s, HD, koff=KOFF[s], nk=KSPLIT[s], par=jj,
                             free=i + 2 * G_FFO if s == 0 else None, first=s == 0, last=s == 3)

            ffo(0)
            with eng.Fori(1, KT // 2) as i:
                ffo(i)

            def turn_result(c, j):
                o = eng.transpose(YC[c][:, j // 4, (j % 4) * P:(j % 4 + 1) * P], U(j, P, c * P), ident[:])
                if j == KT - 1:
                    o.then_inc(E("y_turned"), 1)

            eng.wait_ge(E("n_rs"), 2)
            eng.wait_ge(E("a_x1t"), KT)
            eng.wait_ge(E("proj_free0"), 2 * G_FFO + KT // 2)
            eng.wait_ge(E("proj_free1"), 2 * G_FFO + KT // 2 - 1)
            for j in range(KT - 1):
                turn_result(0, j)
            eng.wait_ge(E("proj_free1"), 2 * G_FFO + KT // 2)
            eng.wait_ge(E("d_acc"), 2 * KT)
            for c in range(NCH):
                mm(pp[1][:, 0, c:c + 1], X(0, P, c * P), ones[:, 0:1], start=True, stop=True)
            mm(pp[1][:, 0, NCH:NCH + NB], ones[:], X(0, NB, TP), start=True, stop=True).then_inc(E("n_mm"), 1)
            turn_result(0, KT - 1)
            for c in range(1, NCH):
                if c == NCH - 1:
                    eng.wait_ge(E("a_last"), 1)
                for j in range(KT):
                    turn_result(c, j)
            eng.wait_ge(E("d_ys"), 1)
            eng.wait_ge(E("d_y"), 1)
            for j in range(KT):
                o = eng.transpose(pr[0:NB, j // 4, (j % 4) * P:(j % 4 + 1) * P], YS[:, j, :], ident[:])
            o.then_inc(E("ys_turned"), 1)


LINKS_HG, LINKS_LRU = 28, 20


_INS = ["x_prompt", "x_sample", "state_hgrn", "state_lru", "state_conv", "norm_mix_pre", "norm_mix_post",
        "norm_ffn_pre", "norm_ffn_post", "w_in", "hg_lb_logits", "hg_out_norm", "lru_conv_w", "lru_conv_b",
        "lru_w_a", "lru_b_a", "lru_w_x", "lru_b_x", "lru_log_lambda", "w_branch_a", "w_branch_b", "w_out",
        "w_ffn_in", "w_ffn_out"]
_OUTS = [(1, TP, D), (NB, 1, D), (1, 1, NH, P, P), (1, 1, D), (1, 1, CW - 1, D),
         (1, NB, NH, P, P), (1, NB, D), (1, NB, CW - 1, D)]


def _level_masks(np):
    s = np.arange(P)[:, None]
    out = [np.eye(P, dtype=np.float32)]
    for i in range(1, NLEV):
        hs = 1 << (i - 1)
        tc = np.arange(P // 2)[None, :]
        t = tc // hs * 2 * hs + hs + tc % hs
        m = (s // (2 * hs) == t // (2 * hs)) & (s % (2 * hs) < hs)
        out.append(m.astype(np.float32))
    return np.ascontiguousarray(np.concatenate(out, axis=1))


def kernel(**inputs):
    import numpy as np
    import concourse.bacc as bacc
    from concourse import mybir as mb
    from concourse.bass_utils import run_bass_kernel_spmd as run

    nc = bacc.Bacc("TRN2", target_bir_lowering=False, num_devices=1)
    arrays, args = {}, []
    for name in _INS:
        a = np.ascontiguousarray(inputs[name])
        arrays[f"in_{name}"] = a
        args.append(nc.dram_tensor(f"in_{name}", a.shape, mb.dt.from_np(a.dtype), kind="ExternalInput").ap())
    for name, a in (("ident", np.eye(P, dtype=np.float32)), ("masks", _level_masks(np))):
        arrays[f"in_{name}"] = a
        args.append(nc.dram_tensor(f"in_{name}", a.shape, mb.dt.from_np(a.dtype), kind="ExternalInput").ap())
    for i, shape in enumerate(_OUTS):
        args.append(nc.dram_tensor(f"out_{i}", shape, mb.dt.float32, kind="ExternalOutput").ap())
    hybrid_decoder(nc, *args)
    r = run(nc, [arrays], core_ids=[0])
    return tuple(r.results[0][f"out_{i}"] for i in range(len(_OUTS)))
```
